# Optimizing a Trainium2 kernel written in Bass

```python
import math
import jax, jax.numpy as jnp
from jax import lax
import numpy as np

D_MODEL = 1024
BATCH = 1
SEQ = 256
DEPTH = 2

GRID_W = 64
CTX_LEN = 256
D_FF = 2816
FFN_RES = 0.5
N_MOD = 9
RMS_EPS = 1e-6

NA_HEADS = 8
NA_HEAD_DIM = 64
NA_WIDTH = NA_HEADS * NA_HEAD_DIM
NA_KH = 8
NA_KW = 16
SC_WIDTH = D_MODEL // 2
AB_IN = 3 * NA_WIDTH + 3 * SC_WIDTH
AB_OUT = NA_WIDTH + SC_WIDTH

HY_WIDTH = D_MODEL
HY_EMB = 33
HY_BANDS = (HY_EMB - 1) // 2
HY_FFN = 64
HY_TARGET = 1e-2
HY_FAST_PCT = 0.3
HY_SLOW_PCT = 1.5

N_EVEN = (DEPTH + 1) // 2
N_ODD = DEPTH // 2

kernel_name = 'hybrid_na_shortconv_hyena_dit'

def rms_norm(x, g):
    xf = x.astype(jnp.float32)
    y = xf * lax.rsqrt(jnp.mean(xf * xf, axis=-1, keepdims=True) + RMS_EPS)
    return (y * g.astype(jnp.float32)).astype(x.dtype)

def modulated_norm(x, g, shift, scale):
    return rms_norm(x, g) * (1 + scale) + shift

def half_step_ffn(x, g_pre, g_post, shift, scale, gate, w_gate, w_up, w_down):
    h = modulated_norm(x, g_pre, shift, scale)
    y = (jax.nn.silu(h @ w_gate) * (h @ w_up)) @ w_down
    return x + FFN_RES * gate * rms_norm(y, g_post)

def short_conv(u, w):
    up = jnp.pad(u, ((0, 0), (1, 1), (0, 0)))
    return up[:, :-2] * w[0] + up[:, 1:-1] * w[1] + up[:, 2:] * w[2]

def window_index(n, k):
    start = jnp.clip(jnp.arange(n) - k // 2, 0, n - k)
    return start[:, None] + jnp.arange(k)[None, :]

def split_heads(t):
    return t.reshape(t.shape[:-1] + (NA_HEADS, NA_HEAD_DIM))

def neighbourhood_attention(q, k, v, k_ctx, v_ctx, rpb):
    b, s, h, dh = q.shape
    rows = s // GRID_W
    kh = min(NA_KH, rows)
    kw = NA_KW
    to_grid = lambda t: t.reshape(b, rows, GRID_W, h, dh)
    qg = to_grid(q) * (dh ** -0.5)
    kg, vg = to_grid(k), to_grid(v)
    row_idx = window_index(rows, kh)
    col_idx = window_index(GRID_W, kw)
    k_band = kg[:, row_idx]
    v_band = vg[:, row_idx]
    sel = (col_idx[:, :, None] == jnp.arange(GRID_W)[None, None, :]).astype(q.dtype)
    s_band = jnp.einsum('brchd,brykhd->bhrcyk', qg, k_band)
    s_win = jnp.einsum('bhrcyk,cwk->bhrcyw', s_band, sel)
    dy = row_idx - jnp.arange(rows)[:, None] + (NA_KH - 1)
    dx = col_idx - jnp.arange(GRID_W)[:, None] + (NA_KW - 1)
    bias = rpb[:, dy[:, None, :, None], dx[None, :, None, :]]
    s_win = s_win + bias[None].astype(s_win.dtype)
    s_ctx = jnp.einsum('brchd,bjhd->bhrcj', qg, k_ctx)
    logits = jnp.concatenate([s_win.reshape(b, h, rows, GRID_W, kh * kw), s_ctx], axis=-1)
    p = jax.nn.softmax(logits.astype(jnp.float32), axis=-1).astype(v.dtype)
    p_win = p[..., :kh * kw].reshape(b, h, rows, GRID_W, kh, kw)
    p_band = jnp.einsum('bhrcyw,cwk->bhrcyk', p_win, sel)
    out = (jnp.einsum('bhrcyk,brykhd->brchd', p_band, v_band)
           + jnp.einsum('bhrcj,bjhd->brchd', p[..., kh * kw:], v_ctx))
    return out.reshape(b, s, h * dh)

def context_attention(q, k, v):
    b, n, h, dh = q.shape
    logits = jnp.einsum('bihd,bjhd->bhij', q * (dh ** -0.5), k)
    p = jax.nn.softmax(logits.astype(jnp.float32), axis=-1).astype(v.dtype)
    return jnp.einsum('bhij,bjhd->bihd', p, v).reshape(b, n, h * dh)

def mixer_ab(h_lat, h_ctx, w_in, rpb, conv_w, w_out, ctx_out):
    cuts = [NA_WIDTH, 2 * NA_WIDTH, 3 * NA_WIDTH, 3 * NA_WIDTH + SC_WIDTH, 3 * NA_WIDTH + 2 * SC_WIDTH]
    q, k, v, gb, gc, xb = jnp.split(h_lat @ w_in, cuts, axis=-1)
    if ctx_out:
        q_c, k_c, v_c, gb_c, gc_c, xb_c = jnp.split(h_ctx @ w_in, cuts, axis=-1)
    else:
        k_c, v_c = jnp.split(h_ctx @ w_in[:, NA_WIDTH:3 * NA_WIDTH], 2, axis=-1)
    k_c, v_c = split_heads(k_c), split_heads(v_c)
    a_lat = neighbourhood_attention(split_heads(q), split_heads(k), split_heads(v), k_c, v_c, rpb)
    b_lat = gb * short_conv(gc * xb, conv_w)
    y_lat = jnp.concatenate([a_lat, b_lat], axis=-1) @ w_out
    if not ctx_out:
        return y_lat, None
    a_ctx = context_attention(split_heads(q_c), k_c, v_c)
    b_ctx = gb_c * short_conv(gc_c * xb_c, conv_w)
    y_ctx = jnp.concatenate([a_ctx, b_ctx], axis=-1) @ w_out
    return y_lat, y_ctx

def hyena_filters(n, w1, b1, w2, b2, w3, b3, w4, freq):
    f32 = jnp.float32
    t = jnp.linspace(0.0, 1.0, n, dtype=f32)[:, None]
    w = 2.0 * math.pi * jnp.arange(n, dtype=f32)[:, None] / n
    bands = jnp.linspace(1e-4, HY_BANDS - 1, HY_BANDS, dtype=f32)[None, :]
    z = jnp.concatenate([t, jnp.cos(bands * w), -jnp.sin(bands * w)], axis=-1)
    fr = freq.astype(f32)
    hdn = jnp.sin(fr * (z @ w1.astype(f32) + b1.astype(f32)))
    hdn = jnp.sin(fr * (hdn @ w2.astype(f32) + b2.astype(f32)))
    hdn = jnp.sin(fr * (hdn @ w3.astype(f32) + b3.astype(f32)))
    filt = (hdn @ w4.astype(f32)).reshape(n, 2, HY_WIDTH)
    max_decay = math.log(HY_TARGET) / HY_FAST_PCT
    min_decay = math.log(HY_TARGET) / HY_SLOW_PCT
    deltas = jnp.linspace(min_decay, max_decay, HY_WIDTH, dtype=f32)
    window = jnp.exp(-t * jnp.abs(deltas)[None, :])
    filt = filt * window[:, None, :]
    return filt[:, 0], filt[:, 1]

def bidirectional_long_conv(u, h_fwd, h_bwd):
    n = u.shape[1]
    k = jnp.concatenate([h_fwd, jnp.zeros((1, HY_WIDTH), jnp.float32), h_bwd[1:][::-1]], axis=0)
    u_f = jnp.fft.rfft(u.astype(jnp.float32), n=2 * n, axis=1)
    k_f = jnp.fft.rfft(k, n=2 * n, axis=0)
    y = jnp.fft.irfft(u_f * k_f[None], n=2 * n, axis=1)[:, :n]
    return y.astype(u.dtype)

def hyena_mixer(h, w_in, short_w, w1, b1, w2, b2, w3, b3, w4, freq, bias, w_out):
    n = h.shape[1]
    x0, x1, v = jnp.split(short_conv(h @ w_in, short_w), 3, axis=-1)
    h_fwd, h_bwd = hyena_filters(n, w1, b1, w2, b2, w3, b3, w4, freq)
    u = v * x1
    return (x0 * (bidirectional_long_conv(u, h_fwd, h_bwd) + u * bias)) @ w_out

def setup_inputs(seed: int = 0) -> dict:
    key = jax.random.key(seed)
    ks = jax.random.split(key, 26)
    f32 = jnp.float32
    nrm = lambda k, shape: jax.random.normal(k, shape, f32)
    lin = lambda k, shape, fan_in: nrm(k, shape) * fan_in ** -0.5
    return {
        'x': nrm(ks[0], (BATCH, SEQ, D_MODEL)),
        'c': nrm(ks[1], (BATCH, D_MODEL)),
        'ctx': nrm(ks[2], (BATCH, CTX_LEN, D_MODEL)),
        'c_ctx': nrm(ks[3], (D_MODEL,)),
        'w_mod': 0.5 * lin(ks[4], (DEPTH, D_MODEL, N_MOD * D_MODEL), D_MODEL),
        'b_mod': 0.02 * nrm(ks[5], (DEPTH, N_MOD * D_MODEL)),
        'norm_g': 1.0 + 0.05 * nrm(ks[6], (DEPTH, 6, D_MODEL)),
        'ffn_w_gate': lin(ks[7], (DEPTH, 2, D_MODEL, D_FF), D_MODEL),
        'ffn_w_up': lin(ks[8], (DEPTH, 2, D_MODEL, D_FF), D_MODEL),
        'ffn_w_down': lin(ks[9], (DEPTH, 2, D_FF, D_MODEL), D_FF),
        'ab_w_in': lin(ks[10], (N_EVEN, D_MODEL, AB_IN), D_MODEL),
        'na_rpb': 0.1 * nrm(ks[11], (N_EVEN, NA_HEADS, 2 * NA_KH - 1, 2 * NA_KW - 1)),
        'sc_conv_w': lin(ks[12], (N_EVEN, 3, SC_WIDTH), 3),
        'ab_w_out': lin(ks[13], (N_EVEN, AB_OUT, D_MODEL), AB_OUT),
        'hy_w_in': lin(ks[14], (N_ODD, D_MODEL, 3 * HY_WIDTH), D_MODEL),
        'hy_short_w': lin(ks[15], (N_ODD, 3, 3 * HY_WIDTH), 3),
        'hy_f_w1': lin(ks[16], (N_ODD, HY_EMB, HY_FFN), HY_EMB),
        'hy_f_b1': 0.02 * nrm(ks[17], (N_ODD, HY_FFN)),
        'hy_f_w2': lin(ks[18], (N_ODD, HY_FFN, HY_FFN), HY_FFN),
        'hy_f_b2': 0.02 * nrm(ks[19], (N_ODD, HY_FFN)),
        'hy_f_w3': lin(ks[20], (N_ODD, HY_FFN, HY_FFN), HY_FFN),
        'hy_f_b3': 0.02 * nrm(ks[21], (N_ODD, HY_FFN)),
        'hy_f_w4': lin(ks[22], (N_ODD, HY_FFN, 2 * HY_WIDTH), HY_FFN),
        'hy_sin_freq': 1.0 + 0.1 * nrm(ks[23], (N_ODD, HY_FFN)),
        'hy_bias': 0.5 * nrm(ks[24], (N_ODD, HY_WIDTH)),
        'hy_w_out': lin(ks[25], (N_ODD, HY_WIDTH, D_MODEL), HY_WIDTH),
    }

def reference(x, c, ctx, c_ctx, w_mod, b_mod, norm_g, ffn_w_gate, ffn_w_up, ffn_w_down,
              ab_w_in, na_rpb, sc_conv_w, ab_w_out,
              hy_w_in, hy_short_w, hy_f_w1, hy_f_b1, hy_f_w2, hy_f_b2, hy_f_w3, hy_f_b3,
              hy_f_w4, hy_sin_freq, hy_bias, hy_w_out):
    b = x.shape[0]
    last_attn = (DEPTH - 1) - (DEPTH - 1) % 2
    for i in range(DEPTH):
        j = i // 2
        g = norm_g[i]
        m_lat = (jax.nn.silu(c) @ w_mod[i] + b_mod[i]).reshape(b, N_MOD, 1, D_MODEL)
        m_ctx = (jax.nn.silu(c_ctx) @ w_mod[i] + b_mod[i]).reshape(N_MOD, D_MODEL)
        keep_ctx = i <= last_attn
        upd_ctx = i < last_attn
        x = half_step_ffn(x, g[0], g[1], m_lat[:, 0], m_lat[:, 1], m_lat[:, 2],
                          ffn_w_gate[i, 0], ffn_w_up[i, 0], ffn_w_down[i, 0])
        h_lat = modulated_norm(x, g[2], m_lat[:, 3], m_lat[:, 4])
        h_ctx = None
        if keep_ctx:
            ctx = half_step_ffn(ctx, g[0], g[1], m_ctx[0], m_ctx[1], m_ctx[2],
                                ffn_w_gate[i, 0], ffn_w_up[i, 0], ffn_w_down[i, 0])
            h_ctx = modulated_norm(ctx, g[2], m_ctx[3], m_ctx[4])
        if i % 2 == 0:
            y_lat, y_ctx = mixer_ab(h_lat, h_ctx, ab_w_in[j], na_rpb[j], sc_conv_w[j], ab_w_out[j], upd_ctx)
        else:
            hy = lambda h: hyena_mixer(h, hy_w_in[j], hy_short_w[j], hy_f_w1[j], hy_f_b1[j], hy_f_w2[j],
                                       hy_f_b2[j], hy_f_w3[j], hy_f_b3[j], hy_f_w4[j], hy_sin_freq[j],
                                       hy_bias[j], hy_w_out[j])
            y_lat = hy(h_lat)
            y_ctx = hy(h_ctx) if upd_ctx else None
        x = x + m_lat[:, 5] * rms_norm(y_lat, g[3])
        x = half_step_ffn(x, g[4], g[5], m_lat[:, 6], m_lat[:, 7], m_lat[:, 8],
                          ffn_w_gate[i, 1], ffn_w_up[i, 1], ffn_w_down[i, 1])
        if upd_ctx:
            ctx = ctx + m_ctx[5] * rms_norm(y_ctx, g[3])
            ctx = half_step_ffn(ctx, g[4], g[5], m_ctx[6], m_ctx[7], m_ctx[8],
                                ffn_w_gate[i, 1], ffn_w_up[i, 1], ffn_w_down[i, 1])
    return x


_drawn_inputs = setup_inputs


def setup_inputs(seed=0):
    import zlib

    import numpy as np

    out = dict(_drawn_inputs(seed))
    spreads = {}
    factors = {'na_rpb': 31.813,
     'hy_f_b1': 5.879,
     'hy_f_b2': 5.167,
     'hy_f_b3': 6.319,
     'ctx': 8.0,
     'c_ctx': 5.461}
    for name, (base, spread) in spreads.items():
        noise = np.random.default_rng([zlib.crc32(name.encode()), seed]).standard_normal(out[name].shape)
        drawn = base * np.exp(spread * noise) if base else spread * noise
        out[name] = __import__('jax').numpy.asarray(drawn.astype(out[name].dtype))
    for name, factor in factors.items():
        out[name] = (out[name] * factor).astype(out[name].dtype)
    return out
```

```python
import math
from contextlib import ExitStack

import numpy as np

import concourse.bass as bass
from concourse import mybir

F32 = mybir.dt.float32
F32R = mybir.dt.float32r
ACT = mybir.ActivationFunctionType
ALU = mybir.AluOpType
AX = mybir.AxisListType

P = 128
D = 1024
T = 256
KT = D // P
DFF = 2816
FT = DFF // P
FH = FT // 2
HEADS = 8
DH = 64
GRID_W = 64
ROWS = T // GRID_W
KH, KW = 8, 16
EPS = 1e-6
HY_EMB = 33
HY_FFN = 64
NEG = -1e30

RING = 6
RAW = 3
UNIT = 1024

PER_FFN = 3 * FT
U_FFN = [0, PER_FFN, 2 * PER_FFN + 32, 3 * PER_FFN + 32, 4 * PER_FFN + 64]
U_AB = 2 * PER_FFN
U_ABO = U_AB + 24
U_HY = 4 * PER_FFN + 32
U_HYO = U_HY + 24
UNITS = 5 * PER_FFN + 64
FFN_OF = [(0, 0), (0, 0), (0, 1), (1, 0), (1, 1)]

LAT, CTX = 0, 1
BLOCKS = [(0, 0, LAT), (0, 1, LAT), (0, 2, LAT), (0, 0, CTX), (0, 1, CTX), (0, 3, LAT), (0, 4, LAT),
          (0, 2, CTX), (0, 3, CTX), (0, 4, CTX), (0, 5, LAT), (0, 6, LAT), (0, 7, LAT), (0, 8, LAT)] \
    + [(1, b, LAT) for b in range(9)]
JOBS = 2 * len(BLOCKS)
JOBS_AHEAD = 4
FFN_JOBS = [11, 11, 11, 9, 0]
FFN_JOB0 = [4, 15, 26, 37, 46]
LOOP_END = [10, 10, 10, 8, 10]

POST, PRE = "post", "pre"
NORMS = [(PRE, 0, LAT, 0, 0, 1), (PRE, 0, CTX, 0, 0, 1),
         (POST, 0, LAT, 1, 2, 0.5), (PRE, 0, LAT, 2, 3, 4),
         (POST, 0, CTX, 1, 2, 0.5), (PRE, 0, CTX, 2, 3, 4),
         (POST, 0, LAT, 3, 5, 1.0), (PRE, 0, LAT, 4, 6, 7),
         (POST, 0, LAT, 5, 8, 0.5), (PRE, 1, LAT, 0, 0, 1),
         (POST, 1, LAT, 1, 2, 0.5), (PRE, 1, LAT, 2, 3, 4),
         (POST, 1, LAT, 3, 5, 1.0), (PRE, 1, LAT, 4, 6, 7),
         (POST, 1, LAT, 5, 8, 0.5)]
NTH = [sum(n[0] == NORMS[q][0] for n in NORMS[:q]) for q in range(len(NORMS))]
NORM_UNIT = {2: PER_FFN, 4: 2 * PER_FFN, 6: U_ABO + 8, 8: U_FFN[2] + PER_FFN, 10: U_FFN[3] + PER_FFN,
             12: U_HYO + 8, 14: UNITS}

S_NORM = 0
S_CONV = S_NORM + 96
S_SHORT = S_CONV + 12
S_BIAS = S_SHORT + 72
S_COLS = S_BIAS + 8


def mod_column(layer, block, stream):
    return 8 * BLOCKS.index((layer, block, stream))


def program(nc, wstream, wmod, cjob, bmod, small, x_in, ctx_in, rpb, mask_in, ident_in, turn_in, zfeat, fw1, fw2,
            fw3, fw4, fcols, window_in, dft_in, out):
    with ExitStack() as ctx:
        def sb(name, shape, dt=F32):
            return ctx.enter_context(nc.sbuf_tensor(name, shape, dt))

        def ps(name, shape):
            return ctx.enter_context(nc.psum_tensor(name, shape, F32))

        def sem(name):
            return ctx.enter_context(nc.semaphore(name))

        raw = sb("raw", [P, RAW, UNIT])
        whi = sb("whi", [P, RING, UNIT], F32R)
        wlo = sb("wlo", [P, RING, UNIT], F32R)
        wm = sb("wm", [P, 8, 512])
        part = sb("part", [P, 512])
        total = sb("total", [P, 512])
        cs = sb("cs", [P, JOBS * 8])
        bm = sb("bm", [P, JOBS * 4])
        mod = sb("mod", [P, JOBS * 4])
        sm = sb("sm", [P, S_COLS])
        coef = sb("coef", [P, len(NORMS), KT])
        x_lat = sb("x_lat", [P, KT, T])
        h_hi = [sb("h_lat_hi", [P, KT, T], F32R), sb("h_ctx_hi", [P, KT, T], F32R)]
        h_lo = [sb("h_lat_lo", [P, KT, T], F32R), sb("h_ctx_lo", [P, KT, T], F32R)]
        m_hi, m_lo = h_hi[CTX], h_lo[CTX]
        sq = sb("sq", [P, KT, T])
        z = sb("z", [P, KT, T])
        root = sb("root", [P, T])
        rstd = sb("rstd", [P, T])
        gated = sb("gated", [P, 2, T])
        act = sb("act", [P, 2, T])
        act_hi = sb("act_hi", [P, 2, T], F32R)
        act_lo = sb("act_lo", [P, 2, T], F32R)
        mean_mat = sb("mean_mat", [P, P])
        ones = sb("ones", [P, 1])
        eps = sb("eps", [P, 1])
        ident = sb("ident", [P, P])
        turn = sb("turn", [P, P])
        mask = sb("mask", [P, GRID_W])
        area = sb("area", [P, 13312])
        at = [0]

        def take(*shape):
            n = int(np.prod(shape))
            v = area[:, at[0]:at[0] + n]
            at[0] += n
            assert at[0] <= 13312
            letters = "abc"[:len(shape)]
            if len(shape) == 1:
                return v
            return v.rearrange(f"p ({' '.join(letters)}) -> p {' '.join(letters)}",
                               **{c: s for c, s in zip(letters, shape)})

        x_ctx = take(KT, T)
        bias = take(4, 2, T)
        q_t = take(4, T)
        k_t = take(4, 2 * T)
        v_n = take(4, 512)
        conv_b = take(4, T)
        prob = take(4, 2 * T)
        gates = take(3, T)
        prod = take(1, T)
        at[0] -= 4 * T
        prob_t = take(4, T)
        at[0] = 0
        k_re = take(2, D)
        k_s = take(2, D)
        y_f = take(4, D)
        dft = take(8, T)
        x0 = take(KT, T)
        conv = take(4, T)
        k_nyq = [part, total]
        sin_a = x0[:, 0, :]
        sin_k = x0[:, 1, :]
        sin_r = x0[:, 2, :]
        hid = x0[:, 3, :]
        zf = x0[:, 4, :]
        fw = x0[:, 5, :]
        fc = x0[:, 6, 0:4]
        p_f = y_f[:, 0:2, :]
        m_f = y_f[:, 2:4, :]
        w4 = k_re[:, :, :].rearrange("p a b -> p (a b)")
        window = k_s
        u_t = z
        u_n = sq[:, :, :].rearrange("p a b -> p (a b)").rearrange("p (a b) -> p a b", a=2)

        stats = sb("stats", [P, 4, 4])

        acc = ps("acc", [P, 4, 512])
        gu = ps("gu", [P, 2, 512])
        job_p = ps("job_p", [P, 512])
        mean_p = ps("mean_p", [P, 512])

        def region(i):
            return gu[:, i % 2, 0:T]

        def acc_tile(m):
            return acc[:, m // 2, (m % 2) * T:(m % 2) * T + T]

        def spectrum_bank(i):
            return [gu[:, 0, :], gu[:, 1, :], job_p[:, :]][i % 3]

        def scores(i):
            return [gu[:, 0, :], gu[:, 1, :], job_p[:, :], mean_p[:, :]][i % 4]

        landed = [sem(f"unit_landed{i}") for i in range(RAW)]
        hi_done, lo_done, pe_done = sem("hi_done"), sem("lo_done"), sem("pe_done")
        wm_landed = [sem("wm_landed0"), sem("wm_landed1")]
        gemv, colsum, mod_ready = sem("gemv_step"), sem("colsum_done"), sem("mod_ready")
        const_in, x_landed, ctx_landed, bias_in = sem("const_in"), sem("x_landed"), sem("ctx_landed"), [sem(f"bias_in{i}") for i in range(4)]
        filt_in, dft_landed = sem("filt_in"), sem("dft_landed")
        made = sem("constants_made")
        cs_ready = sem("cs_ready")
        sq_done, sum_done, root_done = sem("sq_done"), sem("sum_done"), sem("root_done")
        coef_done, rstd_done, z_done, x_upd = sem("coef_done"), sem("rstd_done"), sem("z_done"), sem("x_updated")
        hf_done, hh_done, h_ready = sem("hf_done"), sem("hh_done"), sem("h_ready")
        silu_done, act_mul, act_hi_done, act_lo_done = sem("silu_done"), sem("act_mul"), sem("act_hi_done"), sem("act_lo_done")
        proj_out, conv_step = sem("proj_out"), sem("conv_step")
        s_done, s_max, p_exp, p_norm = sem("s_done"), sem("s_max"), sem("p_exp"), sem("p_norm")
        soft_step = sem("soft_step")
        pt_done, pt_out, pv_done = sem("pt_done"), sem("pt_out"), sem("pv_done")
        masked = sem("masked")
        m_half, m_ready = sem("m_hi_done"), sem("m_ready")
        hy_act, hy_step, u_ready = sem("hy_act"), sem("hy_step"), sem("u_ready")
        fp, fa, fd = sem("filter_pe"), sem("filter_act"), sem("filter_dve")
        tr_done, un_out, uf_done, yf_step = sem("tr_done"), sem("un_out"), sem("uf_done"), sem("yf_step")
        inv_done, inv_step = sem("inv_done"), sem("inv_step")
        stored = sem("stored")

        X = [x_lat, x_ctx]

        block = ctx.enter_context(nc.Block())

        @block.sync
        def _(sp):
            def load(u, phase):
                sp.dma_start(raw[:, phase % RAW, :],
                             wstream[u] if isinstance(u, int) else
                             wstream[bass.ds(u, 1)].rearrange("a p n -> p (a n)")).then_inc(landed[phase % RAW], 16)

            sp.dma_start(sm[:, :], small).then_inc(const_in, 16)
            sp.dma_start(cs[:, :], cjob).then_inc(const_in, 16)
            sp.dma_start(bm[:, :], bmod).then_inc(const_in, 16)
            sp.dma_start(x_lat[:, :, :], x_in).then_inc(x_landed, 16)
            sp.dma_start(ident[:, :], ident_in).then_inc(const_in, 16)
            sp.dma_start(turn[:, :], turn_in).then_inc(const_in, 16)
            sp.dma_start(mask[:, :], mask_in).then_inc(const_in, 16)
            sp.dma_start(x_ctx, ctx_in).then_inc(ctx_landed, 16)
            for u in range(RAW):
                load(u, u)
            for u in range(RAW, RING):
                sp.wait_ge(lo_done, u - RAW + 1)
                load(u, u)
            turns = UNITS // RING
            with sp.Fori(1, turns) as i:
                for k in range(RING):
                    sp.wait_ge(lo_done, i * RING + (k - RAW + 1))
                    load(i * RING + k, k)
            for u in range(turns * RING, UNITS):
                sp.wait_ge(lo_done, u - RAW + 1)
                load(u, u)
            sp.wait_ge(x_upd, 4 * 7)
            sp.dma_start(out, x_lat[:, :, :]).then_inc(stored, 16)
            sp.wait_ge(stored, 16)

        @block.gpsimd
        def _(pool):
            def load_job(j):
                for half in range(2):
                    if not (isinstance(j, int) and j == 0):
                        pool.wait_ge(gemv, j * 8 + (4 * half + 4 - 8))
                    src = wmod[j] if isinstance(j, int) else wmod[bass.ds(j, 1)].rearrange("a p k n -> p (a k) n")
                    pool.dma_start(wm[:, 4 * half:4 * half + 4, :],
                                   src[:, 4 * half:4 * half + 4, :]).then_inc(wm_landed[half], 16)

            def load_bias(h):
                if h >= 4:
                    pool.wait_ge(p_exp, 2 * (h - 4) + 2)
                for r in range(ROWS):
                    src = bass.AP(rpb.tensor, rpb.offset + (h * 15 + 7 - r) * 127,
                                  [[1, GRID_W], [127, ROWS], [1, GRID_W]])
                    q0 = (r % 2) * GRID_W
                    dst = bias[q0:q0 + GRID_W, h % 4, r // 2, :].rearrange("p (y k) -> p y k", y=ROWS)
                    pool.dma_start(dst, src).then_inc(bias_in[h % 4], 16)

            def mask_bias(h):
                pool.wait_ge(bias_in[h % 4], 64 * (h // 4 + 1))
                v = bias[:, h % 4, :, :].rearrange("p t (y k) -> p (t y) k", y=ROWS)
                nc.gpsimd.tensor_tensor(v, v, mask[:, :].unsqueeze(1).to_broadcast([P, 2 * ROWS, GRID_W]),
                                        ALU.add).then_inc(masked, 1)

            load_job(0)
            with pool.Fori(1, FFN_JOB0[2]) as j:
                load_job(j)
            pool.wait_ge(const_in, 96)
            for h in range(4):
                load_bias(h)
            for h in range(4):
                mask_bias(h)
            for h in range(4, HEADS):
                load_bias(h)
                mask_bias(h)
            load_job(FFN_JOB0[2])
            load_job(FFN_JOB0[2] + 1)
            pool.wait_ge(x_upd, 4 * 3)
            pool.dma_start(zf[0:HY_EMB, :], zfeat).then_inc(filt_in, 16)
            pool.dma_start(fw[0:HY_EMB, 0:64], fw1).then_inc(filt_in, 16)
            pool.dma_start(fw[0:HY_FFN, 64:128], fw2).then_inc(filt_in, 16)
            pool.dma_start(fw[0:HY_FFN, 128:192], fw3).then_inc(filt_in, 16)
            pool.dma_start(fc[0:HY_FFN, :], fcols).then_inc(filt_in, 16)
            pool.dma_start(dft, dft_in).then_inc(dft_landed, 16)
            pool.dma_start(w4[0:HY_FFN, :], fw4).then_inc(filt_in, 16)
            pool.dma_start(window, window_in).then_inc(filt_in, 16)
            with pool.Fori(FFN_JOB0[2] + 2, JOBS) as j:
                load_job(j)

        @block.scalar
        def _(a):
            def split_hi(u, phase, first=False):
                turn = u * 16 if isinstance(u, int) else None
                if isinstance(u, int):
                    a.wait_ge(landed[u % RAW], 16 * (u // RAW + 1))
                else:
                    base, i = u.base, u.i
                    a.wait_ge(landed[base % RAW], i * 32 + 16 * (base // RAW + 1))
                if not first:
                    a.wait_ge(pe_done, at_unit(u, -RING + 1))
                nc.scalar.activation(whi[:, phase % RING, :], raw[:, phase % RAW, :], ACT.Copy).then_inc(hi_done, 1)

            def split(u):
                if u.base < UNITS or u.i is not None:
                    if u.i is None and u.base >= UNITS:
                        return
                    split_hi(u if u.i is not None else u.base, u.base)

            def squares(q):
                kind, _, stream, *_ = NORMS[q]
                if q:
                    a.wait_ge(sum_done, q)
                if kind == POST:
                    a.wait_ge(pe_done, NORM_UNIT[q])
                elif q == 0:
                    a.wait_ge(x_landed, 16)
                elif q == 1:
                    a.wait_ge(ctx_landed, 16)
                for c in range(4):
                    if kind == PRE and q > 1:
                        a.wait_ge(x_upd, 4 * NTH[q - 1] + c + 1)
                    src = acc[:, c, :] if kind == POST else X[stream][:, 2 * c:2 * c + 2, :]
                    dst = sq[:, 2 * c:2 * c + 2, :]
                    if kind == POST:
                        dst = dst.rearrange("p a b -> p (a b)")
                    nc.scalar.activation(dst, src, ACT.Square).then_inc(sq_done, 1)

            def roots(q):
                a.wait_ge(sum_done, q + 1)
                if q:
                    a.wait_ge(rstd_done, q)
                nc.scalar.activation(root[:, :], mean_p[:, 0:T], ACT.Sqrt, bias=eps[:, 0:1]).then_inc(root_done, 1)

            def h_his(q, chunks=range(4)):
                p = NTH[q]
                stream = NORMS[q][2]
                for c in chunks:
                    a.wait_ge(hf_done, 8 * p + 2 * c + 2)
                    nc.scalar.activation(h_hi[stream][:, 2 * c:2 * c + 2, :], z[:, 2 * c:2 * c + 2, :],
                                         ACT.Copy).then_inc(hh_done, 1)

            def ffn_turn(u, n, between={}):
                for k in range(6):
                    s = (k // 2) % 2
                    if k in (1, 3):
                        a.wait_ge(pe_done, at_unit(u, k + 1))
                        nc.scalar.activation(gated[:, s, :], gu[:, s, 0:T], ACT.Silu).then_inc(silu_done, 1)
                        a.wait_ge(act_mul, n + (s + 1))
                        nc.scalar.activation(act_hi[:, s, :], act[:, s, :], ACT.Copy).then_inc(act_hi_done, 1)
                    split(u.plus(k + RING))
                    if k in between:
                        between[k]()

            def ffn(f, first={}, peeled={}):
                ffn_turn(Unit(U_FFN[f]), FT * f, first)
                with a.Fori(1, LOOP_END[f]) as i:
                    ffn_turn(Unit(U_FFN[f], i), i * 2 + FT * f)
                for i in range(LOOP_END[f], FH):
                    ffn_turn(Unit(U_FFN[f] + 6 * i), FT * f + 2 * i, peeled.get(i, {}))

            a.wait_ge(const_in, 96)
            nc.scalar.activation(cs[:, :], cs[:, :], ACT.Silu).then_inc(cs_ready, 1)
            a.wait_ge(made, 3)
            squares(0)
            for u in range(RING):
                split_hi(u, u, first=True)
            roots(0)
            h_his(0)
            ffn(0, peeled={FH - 1: {0: lambda: squares(1), 1: lambda: (roots(1)), 2: lambda: h_his(1)}})
            squares(2)
            ffn(1, first={0: lambda: roots(2), 2: lambda: squares(3), 3: lambda: (roots(3), h_his(3))})
            squares(4)

            def take_out(idx):
                a.wait_ge(pe_done, U_AB + idx + 1)
                if idx < 4:
                    ins = nc.scalar.activation(q_t[:, idx, :], region(idx), ACT.Copy, scale=DH ** -0.5)
                elif idx < 16:
                    if idx >= 7:
                        a.wait_ge(conv_step, 5 * ((idx - 4) // 3))
                    ins = nc.scalar.activation(gates[:, (idx - 4) % 3, :], region(idx), ACT.Copy)
                else:
                    ins = nc.scalar.activation(k_t[:, idx - 16, :], gu[:, idx % 2, :], ACT.Copy)
                ins.then_inc(proj_out, 1)

            for idx in range(20):
                take_out(idx)
                split(Unit(U_AB + idx + RING))
                if idx == 0:
                    roots(4)
                if idx == 3:
                    squares(5)
                if idx == 4:
                    roots(5)
                    h_his(5)
            for idx in range(20, 24):
                split(Unit(U_AB + idx + RING))
            a.wait_ge(pe_done, U_AB + 24)
            for t in range(4):
                nc.scalar.activation(v_n[:, t, :], acc[:, t, :], ACT.Copy).then_inc(proj_out, 1)

            for c in range(4):
                a.wait_ge(conv_step, 5 * (c + 1))
                nc.scalar.activation(m_hi[:, 4 + c, :], conv_b[:, c, :], ACT.Copy).then_inc(m_half, 1)

            def exps(h):
                for t in range(2):
                    i = 2 * h + t
                    a.wait_ge(s_max, i + 1)
                    if h >= 2:
                        a.wait_ge(pt_done, i - 3)
                    nc.scalar.activation(prob[:, i % 4, :], scores(i), ACT.Exp, bias=stats[:, i % 4, 1:2],
                                         accum_out=stats[:, i % 4, 2:3]).then_inc(p_exp, 1)

            exps(0)
            for h in range(HEADS):
                if h + 1 < HEADS:
                    exps(h + 1)
                for t in range(2):
                    i = 2 * h + t
                    a.wait_ge(pt_done, i + 1)
                    if h:
                        a.wait_ge(pv_done, h)
                    nc.scalar.activation(prob_t[:, :, t * P:(t + 1) * P],
                                         acc[:, t, :].rearrange("p (k q) -> p k q", k=4),
                                         ACT.Copy).then_inc(pt_out, 1)
            for c in range(8):
                a.wait_ge(pe_done, U_ABO + c + 1)
                split(Unit(U_ABO + c + RING))
            squares(6)
            roots(6)
            squares(7)
            roots(7)
            h_his(7)
            ffn(2)
            squares(8)
            roots(8)
            squares(9)
            roots(9)
            h_his(9)
            def sine(l):
                a.wait_ge(fd, FD_SIN[l])
                nc.scalar.activation(hid[0:HY_FFN, :], sin_r[0:HY_FFN, :], ACT.Sin).then_inc(fa, 1)

            def spectrum_out(i):
                half, what, w = SPECTRUM[i]
                cols = slice(half * 512, half * 512 + 512)
                a.wait_ge(fp, FP_DFT + i + 1)
                if what == "nyquist":
                    ins = nc.scalar.activation(k_nyq[half][0:1, :], spectrum_bank(i)[0:1, :], ACT.Copy)
                else:
                    ins = nc.scalar.activation((k_re if what == "re" else k_s)[:, w, cols], spectrum_bank(i), ACT.Copy)
                ins.then_inc(fa, 1)

            ffn(3, peeled=at_steps(FILTER_AT, [lambda l=l: sine(l) for l in range(3)]))
            squares(10)
            roots(10)
            for i in range(5):
                spectrum_out(i)
            squares(11)
            roots(11)
            spectrum_out(5)
            spectrum_out(6)
            h_his(11, (0, 1))
            spectrum_out(7)
            h_his(11, (2, 3))
            spectrum_out(8)
            spectrum_out(9)


            for idx in range(24):
                j = hy_tile(idx)
                a.wait_ge(pe_done, U_HY + idx + 1)
                if idx >= 4:
                    a.wait_ge(hy_step, HY_STEPS(idx - 3 if idx < 20 and idx % 2 == 0 else idx - 4))
                nc.scalar.activation(conv[:, idx % 4, :], region(idx), ACT.Copy,
                                     scale=sm[:, S_SHORT + 24 + j:S_SHORT + 25 + j]).then_inc(hy_act, 1)
                split(Unit(U_HY + idx + RING))
                if idx in (TR_AT[0] + 1, TR_AT[1] + 1):
                    g = (TR_AT[0] + 1, TR_AT[1] + 1).index(idx)
                    a.wait_ge(tr_done, g + 1)
                    nc.scalar.activation(u_n[:, 0, g * 512:g * 512 + 512], job_p[:, :], ACT.Copy).then_inc(un_out, 1)
                    nc.scalar.activation(u_n[:, 1, g * 512:g * 512 + 512], mean_p[:, :], ACT.Copy).then_inc(un_out, 1)
            for c in range(KT):
                a.wait_ge(inv_step, 2 * c + 2)
                nc.scalar.activation(m_hi[:, c, :], conv[:, c % 4, :], ACT.Copy).then_inc(m_half, 1)
            for c in range(8):
                a.wait_ge(pe_done, U_HYO + c + 1)
                split(Unit(U_HYO + c + RING))
            squares(12)
            roots(12)
            squares(13)
            roots(13)
            h_his(13)
            ffn(4)
            squares(14)
            roots(14)

        @block.vector
        def _(v):
            def split(u):
                if u.i is None and u.base >= UNITS:
                    return
                v.wait_ge(hi_done, at_unit(u, 1))
                nc.vector.tensor_tensor(wlo[:, u.base % RING, :], raw[:, u.base % RAW, :],
                                        whi[:, u.base % RING, :].bitcast(F32), ALU.subtract).then_inc(lo_done, 1)

            def job_ops(j, kts):
                for kt in kts:
                    if kt in (0, 4):
                        v.wait_ge(wm_landed[kt // 4], j * 16 + 16)
                    c = cs[:, j * 8 + kt:j * 8 + kt + 1] if isinstance(j, int) else cs[:, bass.ds(j * 8 + kt, 1)]
                    if not (isinstance(j, int) and j == 0 and kt == 0):
                        v.wait_ge(gemv, j * 8 + kt)
                    dst = total if kt == 7 else part
                    if kt == 0:
                        ins = nc.vector.tensor_scalar(dst[:, :], wm[:, kt, :], c, None, ALU.mult)
                    else:
                        ins = nc.vector.scalar_tensor_tensor(out=dst[:, :], in0=wm[:, kt, :], scalar=c,
                                                             in1=part[:, :], op0=ALU.mult, op1=ALU.add)
                    ins.then_inc(gemv, 1)

            def job_out(j):
                v.wait_ge(colsum, j + 1)
                b = bm[:, 4 * j:4 * j + 4] if isinstance(j, int) else bm[:, bass.ds(j * 4, 4)]
                m = mod[:, 4 * j:4 * j + 4] if isinstance(j, int) else mod[:, bass.ds(j * 4, 4)]
                nc.vector.tensor_tensor(m, job_p[:, 0:4], b, ALU.add).then_inc(mod_ready, 1)

            def norm_coef(q):
                kind, layer, stream, g, b0, b1 = NORMS[q]
                gain = sm[:, S_NORM + (layer * 6 + g) * 8:S_NORM + (layer * 6 + g) * 8 + 8]
                block_ = b0 if kind == POST else b1
                col = mod_column(layer, block_, stream)
                v.wait_ge(mod_ready, col // 4 + 2)
                scalar, op = (b1, ALU.mult) if kind == POST else (1.0, ALU.add)
                nc.vector.scalar_tensor_tensor(out=coef[:, q, :], in0=mod[:, col:col + 8], scalar=scalar, in1=gain,
                                               op0=op, op1=ALU.mult).then_inc(coef_done, 1)

            def norm_scale(q):
                kind, layer, stream, *_ = NORMS[q]
                norm_coef(q)
                v.wait_ge(root_done, q + 1)
                nc.vector.reciprocal(rstd[:, :], root[:, :]).then_inc(rstd_done, 1)
                v.wait_ge(rstd_done, q + 1)
                for c in range(4):
                    src = acc[:, c, :].rearrange("p (a b) -> p a b", a=2) if kind == POST else X[stream][:, 2 * c:2 * c + 2, :]
                    nc.vector.tensor_tensor(z[:, 2 * c:2 * c + 2, :], src,
                                            rstd[:, :].unsqueeze(1).to_broadcast([P, 2, T]), ALU.mult).then_inc(z_done, 1)

            def post(q):
                stream, p = NORMS[q][2], NTH[q]
                norm_scale(q)
                v.wait_ge(coef_done, q + 1)
                for c in range(4):
                    v.wait_ge(z_done, 4 * q + c + 1)
                    for m in (2 * c, 2 * c + 1):
                        ins = nc.vector.scalar_tensor_tensor(out=X[stream][:, m, :], in0=z[:, m, :],
                                                             scalar=coef[:, q, m:m + 1], in1=X[stream][:, m, :],
                                                             op0=ALU.mult, op1=ALU.add)
                    ins.then_inc(x_upd, 1)

            def pre(q):
                _, layer, stream, _, shift, _ = NORMS[q]
                p = NTH[q]
                if q > 1:
                    v.wait_ge(x_upd, 4 * NTH[q - 1] + 4)
                norm_scale(q)
                v.wait_ge(coef_done, q + 1)
                col = mod_column(layer, shift, stream)
                v.wait_ge(mod_ready, col // 4 + 2)

                def affine(c):
                    v.wait_ge(z_done, 4 * q + c + 1)
                    for m in (2 * c, 2 * c + 1):
                        nc.vector.tensor_scalar(z[:, m, :], z[:, m, :], coef[:, q, m:m + 1], mod[:, col + m:col + m + 1],
                                                ALU.mult, ALU.add).then_inc(hf_done, 1)

                def rest(c):
                    v.wait_ge(hf_done, 8 * p + 2 * c + 2)
                    v.wait_ge(hh_done, 4 * p + c + 1)
                    nc.vector.tensor_tensor(h_lo[stream][:, 2 * c:2 * c + 2, :], z[:, 2 * c:2 * c + 2, :],
                                            h_hi[stream][:, 2 * c:2 * c + 2, :].bitcast(F32), ALU.subtract).then_inc(h_ready, 1)

                affine(0)
                affine(1)
                rest(0)
                affine(2)
                rest(1)
                affine(3)
                rest(2)
                rest(3)

            def ffn_turn(u, n, j, out_j, between={}):
                def ops(*kts):
                    if j is not None:
                        job_ops(j, kts)

                for k in range(6):
                    s = (k // 2) % 2
                    if k == 0 and out_j is not None:
                        job_out(out_j)
                    if k in (0, 2):
                        ops(2 * k, 2 * k + 1)
                    if k in (1, 3):
                        v.wait_ge(silu_done, n + (s + 1))
                        nc.vector.tensor_tensor(act[:, s, :], gated[:, s, :], gu[:, s, T:2 * T], ALU.mult).then_inc(act_mul, 1)
                        ops(2 * k)
                        v.wait_ge(act_hi_done, n + (s + 1))
                        v.wait_ge(act_mul, n + (s + 1))
                        nc.vector.tensor_tensor(act_lo[:, s, :], act[:, s, :], act_hi[:, s, :].bitcast(F32),
                                                ALU.subtract).then_inc(act_lo_done, 1)
                        ops(2 * k + 1)
                    split(u.plus(k + RING))
                    if k in between:
                        between[k]()

            def ffn(f, first={}, peeled={}):
                j0, jobs, u0 = FFN_JOB0[f], FFN_JOBS[f], U_FFN[f]
                ffn_turn(Unit(u0), FT * f, j0 if jobs else None, None, first)
                end = LOOP_END[f]
                with v.Fori(1, end) as i:
                    ffn_turn(Unit(u0, i), i * 2 + FT * f, (i + j0) if jobs else None, (i + (j0 - 1)) if jobs else None)
                for i in range(end, FH):
                    ffn_turn(Unit(u0 + 6 * i), FT * f + 2 * i, j0 + i if i < jobs else None,
                             j0 + i - 1 if i - 1 < jobs and jobs else None, peeled.get(i, {}))
                if jobs == FH:
                    job_out(j0 + jobs - 1)

            nc.vector.memset(mean_mat[:, :], 1.0 / D).then_inc(made, 1)
            nc.vector.memset(ones[:, :], 1.0).then_inc(made, 1)
            nc.vector.memset(eps[:, :], EPS).then_inc(made, 1)
            v.wait_ge(cs_ready, 1)
            for j in range(JOBS_AHEAD):
                if j == 1:
                    for u in range(RING):
                        split(Unit(u))
                job_ops(j, range(8))
                job_out(j)
            v.wait_ge(x_landed, 16)
            pre(0)
            ffn(0, peeled={FH - 1: {2: lambda: pre(1)}})
            ffn(1, first={0: lambda: post(2), 3: lambda: pre(3)})

            def short_conv(c):
                n = 5 * c
                v.wait_ge(proj_out, 4 + 3 * c + 3)
                nc.vector.tensor_tensor(prod[:, 0, :], gates[:, 0, :], gates[:, 1, :], ALU.mult).then_inc(conv_step, 1)
                v.wait_ge(conv_step, n + 1)
                w = [sm[:, S_CONV + 4 * i + c:S_CONV + 4 * i + c + 1] for i in range(3)]
                nc.vector.tensor_scalar(conv_b[:, c, :], prod[:, 0, :], w[1], None, ALU.mult).then_inc(conv_step, 1)
                v.wait_ge(conv_step, n + 2)
                nc.vector.scalar_tensor_tensor(out=conv_b[:, c, 1:T], in0=prod[:, 0, 0:T - 1], scalar=w[0],
                                               in1=conv_b[:, c, 1:T], op0=ALU.mult, op1=ALU.add).then_inc(conv_step, 1)
                v.wait_ge(conv_step, n + 3)
                nc.vector.scalar_tensor_tensor(out=conv_b[:, c, 0:T - 1], in0=prod[:, 0, 1:T], scalar=w[2],
                                               in1=conv_b[:, c, 0:T - 1], op0=ALU.mult, op1=ALU.add).then_inc(conv_step, 1)
                v.wait_ge(conv_step, n + 4)
                nc.vector.tensor_tensor(conv_b[:, c, :], conv_b[:, c, :], gates[:, 2, :], ALU.mult).then_inc(conv_step, 1)

            for idx in range(24):
                split(Unit(U_AB + idx + RING))
                if idx == 0:
                    post(4)
                if idx == 4:
                    pre(5)
                if idx >= 6 and idx % 3 == 0 and idx <= 15:
                    short_conv(idx // 3 - 2)
            for c in range(4):
                v.wait_ge(m_half, c + 1)
                nc.vector.tensor_tensor(m_lo[:, 4 + c, :], conv_b[:, c, :], m_hi[:, 4 + c, :].bitcast(F32),
                                        ALU.subtract).then_inc(m_ready, 1)

            def maxima(h):
                for t in range(2):
                    i, n = 2 * h + t, soft_of(2 * h + t)
                    v.wait_ge(s_done, i + 1)
                    if i >= 4:
                        v.wait_ge(p_norm, i - 3)
                    nc.vector.tensor_reduce(stats[:, i % 4, 0:1], scores(i), AX.X, ALU.max).then_inc(soft_step, 1)
                    v.wait_ge(soft_step, n + 1)
                    nc.vector.tensor_scalar(stats[:, i % 4, 1:2], stats[:, i % 4, 0:1], -1.0, None, ALU.mult).then_inc(s_max, 1)

            def soft_of(i):
                return soft_base[i]

            soft_base, recip_base, n = {}, {}, 0
            for i in (0, 1):
                soft_base[i] = n
                n += 1
            for h in range(HEADS):
                if h + 1 < HEADS:
                    for t in range(2):
                        soft_base[2 * h + 2 + t] = n
                        n += 1
                for t in range(2):
                    recip_base[2 * h + t] = n
                    n += 1
            def pair_out(pair):
                v.wait_ge(pv_done, 2 * pair + 2)
                o = acc[:, 2 + pair % 2, 0:T]
                nc.vector.tensor_copy(m_hi[:, pair, :], o).then_inc(m_half, 1)
                v.wait_ge(m_half, 4 + pair + 1)
                nc.vector.tensor_tensor(m_lo[:, pair, :], o, m_hi[:, pair, :].bitcast(F32),
                                        ALU.subtract).then_inc(m_ready, 1)

            maxima(0)
            for h in range(HEADS):
                if h + 1 < HEADS:
                    maxima(h + 1)
                for t in range(2):
                    i = 2 * h + t
                    v.wait_ge(p_exp, i + 1)
                    nc.vector.reciprocal(stats[:, i % 4, 3:4], stats[:, i % 4, 2:3]).then_inc(soft_step, 1)
                    v.wait_ge(soft_step, recip_base[i] + 1)
                    nc.vector.tensor_scalar(prob[:, i % 4, :], prob[:, i % 4, :], stats[:, i % 4, 3:4], None,
                                            ALU.mult).then_inc(p_norm, 1)
                if h % 2 == 0 and h:
                    pair_out(h // 2 - 1)
            pair_out(HEADS // 2 - 1)
            for c in range(8):
                split(Unit(U_ABO + c + RING))
            post(6)
            pre(7)
            ffn(2)
            post(8)
            pre(9)
            count = [0]

            def step(ins):
                ins.then_inc(fd, 1)
                count[0] += 1

            def settle():
                v.wait_ge(fd, count[0])

            TWO_PI = 2 * math.pi
            c1 = 6.28125
            c2 = float(np.float32(math.floor((TWO_PI - c1) * 2 ** 21) / 2 ** 21))
            c3 = TWO_PI - c1 - c2
            big = 1.5 * 2 ** 23
            H = slice(0, HY_FFN)

            def sine_argument(l):
                if l == 0:
                    v.wait_ge(filt_in, 16 * 7)
                v.wait_ge(fp, l + 1)
                step(nc.vector.tensor_scalar(sin_a[H, :], mean_p[H, 0:T], fc[H, l:l + 1], fc[H, 3:4], ALU.add, ALU.mult))
                settle()
                step(nc.vector.tensor_scalar(sin_k[H, :], sin_a[H, :], 1 / TWO_PI, big, ALU.mult, ALU.add))
                settle()
                step(nc.vector.tensor_scalar(sin_k[H, :], sin_k[H, :], -big, None, ALU.add))
                settle()
                for c in (c1, c2, c3):
                    step(nc.vector.scalar_tensor_tensor(out=sin_a[H, :], in0=sin_k[H, :], scalar=-c, in1=sin_a[H, :],
                                                        op0=ALU.mult, op1=ALU.add))
                    settle()
                step(nc.vector.tensor_scalar(sin_r[H, :], sin_a[H, :], PI_F, -PI_F, ALU.min, ALU.max))
                assert count[0] == FD_SIN[l]

            def filter_sums(i):
                th, half = i % 2, i // 2
                cols = slice(half * 512, half * 512 + 512)
                v.wait_ge(fp, 3 + i + 1)
                step(nc.vector.tensor_tensor(p_f[:, th, cols], job_p[:, :], window[:, th, cols], ALU.mult))
                step(nc.vector.tensor_tensor(m_f[:, th, cols], mean_p[:, :], window[:, th, cols], ALU.mult))
                settle()
                if th == 0:
                    step(nc.vector.memset(m_f[0:1, th, cols], 0.0))
                    settle()
                step(nc.vector.tensor_tensor(p_f[:, th, cols], p_f[:, th, cols], m_f[:, th, cols], ALU.add))
                settle()
                step(nc.vector.scalar_tensor_tensor(out=m_f[:, th, cols], in0=m_f[:, th, cols], scalar=-2.0,
                                                    in1=p_f[:, th, cols], op0=ALU.mult, op1=ALU.add))
                assert count[0] == FD_SUM[i]

            ffn(3, peeled=at_steps(FILTER_AT, [lambda l=l: sine_argument(l) for l in range(3)]
                                   + [lambda i=i: filter_sums(i) for i in range(4)]))
            post(10)
            pre(11)
            v.wait_ge(fa, 3 + 10)
            step(nc.vector.memset(k_s[0:1, 0, :], 0.0))

            def taps(idx):
                j, n = hy_tile(idx), HY_STEPS(idx - 1) if idx else 0
                w0 = sm[:, S_SHORT + j:S_SHORT + j + 1]
                w2 = sm[:, S_SHORT + 48 + j:S_SHORT + 49 + j]
                c = conv[:, idx % 4, :]
                r = region(idx)
                v.wait_ge(hy_act, idx + 1)
                nc.vector.scalar_tensor_tensor(out=c[:, 1:T], in0=r[:, 0:T - 1], scalar=w0, in1=c[:, 1:T],
                                               op0=ALU.mult, op1=ALU.add).then_inc(hy_step, 1)
                v.wait_ge(hy_step, n + 1)
                nc.vector.scalar_tensor_tensor(out=c[:, 0:T - 1], in0=r[:, 1:T], scalar=w2, in1=c[:, 0:T - 1],
                                               op0=ALU.mult, op1=ALU.add).then_inc(hy_step, 1)
                v.wait_ge(hy_step, n + 2)
                if idx < 16 and idx % 2:
                    nc.vector.tensor_tensor(u_t[:, idx // 2, :], conv[:, (idx - 1) % 4, :], c, ALU.mult).then_inc(hy_step, 1)
                elif idx >= 16:
                    nc.vector.tensor_copy(x0[:, idx - 16, :], c).then_inc(hy_step, 1)

            def spectrum_product(g):
                cols = slice(g * 512, g * 512 + 512)
                n = 7 * g
                v.wait_ge(uf_done, g + 1)
                re, s_ = y_f[:, 0:2, cols], y_f[:, 2:4, cols]
                tmp = prod_tmp(0)
                tmp2 = prod_tmp(1)
                nc.vector.tensor_tensor(re, acc[:, 0:2, :], k_re[:, :, cols], ALU.mult).then_inc(yf_step, 1)
                nc.vector.tensor_tensor(tmp, acc[:, 2:4, :], k_s[:, :, cols], ALU.mult).then_inc(yf_step, 1)
                nc.vector.tensor_tensor(s_, acc[:, 0:2, :], k_s[:, :, cols], ALU.mult).then_inc(yf_step, 1)
                nc.vector.tensor_tensor(tmp2, acc[:, 2:4, :], k_re[:, :, cols], ALU.mult).then_inc(yf_step, 1)
                v.wait_ge(yf_step, n + 4)
                nc.vector.tensor_tensor(re, re, tmp, ALU.subtract).then_inc(yf_step, 1)
                nc.vector.tensor_tensor(s_, s_, tmp2, ALU.add).then_inc(yf_step, 1)
                v.wait_ge(yf_step, n + 6)
                nc.vector.tensor_tensor(y_f[0:1, 2, cols], acc[0:1, 2, :], k_nyq[g][0:1, :], ALU.mult).then_inc(yf_step, 1)

            def prod_tmp(i):
                return wm[:, 2 * i:2 * i + 2, :]

            for idx in range(24):
                taps(idx)
                split(Unit(U_HY + idx + RING))
                if idx == 0:
                    v.wait_ge(fd, count[0])
                if idx in (13, 21):
                    spectrum_product((13, 21).index(idx))
            for c in range(KT):
                v.wait_ge(inv_done, c + 1)
                b = sm[:, S_BIAS + c:S_BIAS + c + 1]
                if c >= 4:
                    v.wait_ge(m_ready, 8 + c - 3)
                nc.vector.scalar_tensor_tensor(out=conv[:, c % 4, :], in0=u_t[:, c, :], scalar=b, in1=region(c),
                                               op0=ALU.mult, op1=ALU.add).then_inc(inv_step, 1)
                v.wait_ge(inv_step, 2 * c + 1)
                nc.vector.tensor_tensor(conv[:, c % 4, :], conv[:, c % 4, :], x0[:, c, :], ALU.mult).then_inc(inv_step, 1)
                v.wait_ge(m_half, 8 + c + 1)
                nc.vector.tensor_tensor(m_lo[:, c, :], conv[:, c % 4, :], m_hi[:, c, :].bitcast(F32),
                                        ALU.subtract).then_inc(m_ready, 1)
            for c in range(8):
                split(Unit(U_HYO + c + RING))
            post(12)
            pre(13)
            ffn(4)
            post(14)

        @block.tensor
        def _(pe):
            def product(out_, w_hi, w_lo, x_hi, x_lo, start, stop):
                nc.tensor.matmul(out_, w_hi, x_hi, start=start, stop=False, skip_group_check=True)
                nc.tensor.matmul(out_, w_hi, x_lo, start=False, stop=False, skip_group_check=True)
                return nc.tensor.matmul(out_, w_lo, x_hi, start=False, stop=stop, skip_group_check=True)

            def wblock(u, kt):
                s = u.base % RING
                return whi[:, s, kt * P:(kt + 1) * P], wlo[:, s, kt * P:(kt + 1) * P]

            def column_unit(u, out_, xs, wait_h=None, last=True):
                pe.wait_ge(lo_done, at_unit(u, 1))
                for kt in range(KT):
                    if wait_h is not None and kt % 2 == 0:
                        pe.wait_ge(h_ready, wait_h + kt // 2 + 1)
                    ins = product(out_, *wblock(u, kt), xs[0][:, kt, :], xs[1][:, kt, :], kt == 0, kt == KT - 1)
                if last:
                    ins.then_inc(pe_done, 1)
                return ins

            def colsum_of(j):
                pe.wait_ge(gemv, j * 8 + 8)
                for i in range(4):
                    ins = nc.tensor.matmul(job_p[:, i:i + 1], total[:, i * P:(i + 1) * P], ones[:, 0:1], start=True, stop=True)
                ins.then_inc(colsum, 1)

            def mean_of(q):
                if q:
                    pe.wait_ge(root_done, q)
                for m in range(KT):
                    if m % 2 == 0:
                        pe.wait_ge(sq_done, 4 * q + m // 2 + 1)
                    ins = nc.tensor.matmul(mean_p[:, 0:T], mean_mat[:, :], sq[:, m, :], start=(m == 0), stop=(m == KT - 1))
                ins.then_inc(sum_done, 1)

            def ffn_turn(u, n, j, xs, first=False, acc_free=0, wait_h=None, bank_wait=True, stop=False, between={}):
                for k in range(6):
                    s = (k // 2) % 2
                    uk = u.plus(k)
                    if k < 4:
                        if k % 2 == 0 and bank_wait:
                            pe.wait_ge(act_mul, n + (s - 1))
                        column_unit(uk, gu[:, s, (k % 2) * T:(k % 2) * T + T], xs,
                                    wait_h if k == 0 else None)
                    else:
                        s = k - 4
                        if first and s == 0 and acc_free:
                            pe.wait_ge(z_done, acc_free)
                        pe.wait_ge(act_lo_done, n + (s + 1))
                        pe.wait_ge(lo_done, at_unit(uk, 1))
                        for m in range(KT):
                            ins = product(acc_tile(m), *wblock(uk, m), act_hi[:, s, :], act_lo[:, s, :],
                                          first and s == 0 and m % 2 == 0, stop and s == 1)
                        ins.then_inc(pe_done, 1)
                    if k == 5 and j is not None:
                        colsum_of(j)
                    if k in between:
                        between[k]()

            def ffn(f, p, stream, acc_free, first={}, peeled={}):
                xs = (h_hi[stream], h_lo[stream])
                j0, jobs, u0 = FFN_JOB0[f], FFN_JOBS[f], U_FFN[f]
                ffn_turn(Unit(u0), FT * f, j0 if jobs else None, xs, True, acc_free, 4 * p, f > 0, False, first)
                end = LOOP_END[f]
                with pe.Fori(1, end) as i:
                    ffn_turn(Unit(u0, i), i * 2 + FT * f, (i + j0) if jobs else None, xs)
                for i in range(end, FH):
                    ffn_turn(Unit(u0 + 6 * i), FT * f + 2 * i, j0 + i if i < jobs else None, xs,
                             stop=(i == FH - 1), between=peeled.get(i, {}))

            pe.wait_ge(made, 3)
            for j in range(JOBS_AHEAD):
                colsum_of(j)
                if j == 0:
                    mean_of(0)
            ffn(0, 0, LAT, 0, peeled={FH - 1: {1: lambda: mean_of(1)}})
            ffn(1, 1, CTX, 4 * 2 + 4, first={0: lambda: mean_of(2), 3: lambda: mean_of(3)})

            lat = (h_hi[LAT], h_lo[LAT])
            pe.wait_ge(h_ready, 4 * 3)
            pe.wait_ge(act_mul, 2 * FT)
            for idx in range(16):
                if idx >= 2:
                    pe.wait_ge(proj_out, idx - 1)
                column_unit(Unit(U_AB + idx), region(idx), lat)
                if idx == 0:
                    mean_of(4)
                if idx == 4:
                    mean_of(5)
            con = (h_hi[CTX], h_lo[CTX])
            pe.wait_ge(h_ready, 4 * 4)
            for idx in range(16, 20):
                pe.wait_ge(proj_out, idx - 1)
                column_unit(Unit(U_AB + idx), gu[:, idx % 2, 0:T], lat, last=False)
                column_unit(Unit(U_AB + idx), gu[:, idx % 2, T:2 * T], con)
            pe.wait_ge(z_done, 4 * 5)
            for c in range(4):
                u = Unit(U_AB + 20 + c)
                s = u.base % RING
                pe.wait_ge(lo_done, u.base + 1)
                for half in range(2):
                    kt = 2 * c + half
                    w_hi, w_lo = (w[:, s, half * 512:half * 512 + 512] for w in (whi, wlo))
                    for t in range(4):
                        st = t // 2
                        tok = slice((t % 2) * P, (t % 2) * P + P)
                        x_hi, x_lo = h_hi[st][:, kt, tok], h_lo[st][:, kt, tok]
                        nc.tensor.matmul(acc[:, t, :], x_hi, w_hi, start=(kt == 0), stop=False, skip_group_check=True)
                        nc.tensor.matmul(acc[:, t, :], x_lo, w_hi, start=False, stop=False, skip_group_check=True)
                        ins = nc.tensor.matmul(acc[:, t, :], x_hi, w_lo, start=False, stop=(kt == KT - 1),
                                               skip_group_check=True)
                ins.then_inc(pe_done, 1)

            def score(h):
                rows = slice(DH * (h % 2), DH * (h % 2) + DH)
                pe.wait_ge(masked, h + 1)
                for t in range(2):
                    i = 2 * h + t
                    if h >= 2:
                        pe.wait_ge(p_exp, i - 3)
                    nc.tensor.matmul(scores(i), q_t[rows, h // 2, t * P:(t + 1) * P], k_t[rows, h // 2, :],
                                     start=True, stop=False, skip_group_check=True)
                    nc.tensor.matmul(scores(i)[:, 0:T], turn[:, :], bias[:, h % 4, t, :], start=False, stop=True,
                                     skip_group_check=True).then_inc(s_done, 1)

            pe.wait_ge(proj_out, 24)
            pe.wait_ge(mod_ready, FFN_JOB0[2])
            score(0)
            score(1)
            for h in range(HEADS):
                for t in range(2):
                    i = 2 * h + t
                    pe.wait_ge(p_norm, i + 1)
                    if h:
                        pe.wait_ge(pt_out, i - 1)
                    for k in range(4):
                        ins = nc.tensor.transpose(acc[:, t, k * P:(k + 1) * P], prob[:, i % 4, k * P:(k + 1) * P], ident[:, :])
                    ins.then_inc(pt_done, 1)
                if h + 2 < HEADS:
                    score(h + 2)
                pe.wait_ge(pt_out, 2 * h + 2)
                pair = h // 2
                if h % 2 == 0 and pair >= 2:
                    pe.wait_ge(m_ready, 4 + pair - 1)
                rows = slice(DH * (h % 2), DH * (h % 2) + DH)
                for k in range(4):
                    ins = nc.tensor.matmul(acc[rows, 2 + pair % 2, 0:T], v_n[:, k, h * DH:(h + 1) * DH], prob_t[:, k, :],
                                           start=(k == 0), stop=(k == 3))
                ins.then_inc(pv_done, 1)

            def out_projection(u0, ready):
                pe.wait_ge(m_ready, ready)
                for m in range(KT):
                    u = Unit(u0 + m)
                    pe.wait_ge(lo_done, u.base + 1)
                    for kt in range(KT):
                        ins = product(acc_tile(m), *wblock(u, kt), m_hi[:, kt, :], m_lo[:, kt, :], kt == 0, kt == KT - 1)
                    ins.then_inc(pe_done, 1)

            out_projection(U_ABO, 8)
            mean_of(6)
            mean_of(7)
            ffn(2, 4, LAT, 4 * 7)
            mean_of(8)
            mean_of(9)

            E = slice(0, HY_EMB)
            H = slice(0, HY_FFN)

            def filter_layer(l):
                if l == 0:
                    pe.wait_ge(filt_in, 16 * 7)
                    w, x_ = fw[E, 0:64], zf[E, :]
                else:
                    pe.wait_ge(fa, l)
                    w, x_ = fw[H, 64 * l:64 * l + 64], hid[H, :]
                nc.tensor.matmul(mean_p[H, 0:T], w, x_, start=True, stop=True).then_inc(fp, 1)

            def filter_out(i):
                th, half = i % 2, i // 2
                if i == 0:
                    pe.wait_ge(fa, 3)
                    pe.wait_ge(mod_ready, JOBS)
                else:
                    pe.wait_ge(fd, FD_SUM[i - 1])
                for b, bank in enumerate((job_p, mean_p)):
                    ins = nc.tensor.matmul(bank[:, :], hid[H, th * P:(th + 1) * P],
                                           w4[H, b * D + half * 512:b * D + half * 512 + 512], start=True, stop=True)
                ins.then_inc(fp, 1)

            def spectrum(i):
                half, what, w = SPECTRUM[i]
                cols = slice(half * 512, half * 512 + 512)
                if i >= 3:
                    pe.wait_ge(fa, 3 + i - 2)
                for th in range(2):
                    if what == "nyquist":
                        out_, w_, x_ = spectrum_bank(i)[0:1, :], dft[:, 2 + th, 0:1], p_f
                    else:
                        base = 0 if what == "re" else 2
                        out_, w_, x_ = spectrum_bank(i), dft[:, base + th, w * P:(w + 1) * P], p_f if what == "re" else m_f
                    ins = nc.tensor.matmul(out_, w_, x_[:, th, cols], start=(th == 0), stop=(th == 1))
                ins.then_inc(fp, 1)

            ffn(3, 5, LAT, 4 * 9, peeled=at_steps(FILTER_AT, [lambda l=l: filter_layer(l) for l in range(3)]
                                                  + [lambda i=i: filter_out(i) for i in range(4)]))
            pe.wait_ge(dft_landed, 16)
            pe.wait_ge(act_mul, 4 * FT)
            pe.wait_ge(fd, FD_SUM[3])
            mean_of(10)
            for i in range(5):
                spectrum(i)
            mean_of(11)
            for i in range(5, 10):
                spectrum(i)

            pe.wait_ge(h_ready, 4 * 7)
            pe.wait_ge(fa, 3 + 10)

            def transposes(g):
                pe.wait_ge(hy_step, HY_STEPS(8 * g + 7))
                if g:
                    pe.wait_ge(un_out, 2)
                for th, bank in ((0, job_p), (1, mean_p)):
                    for c in range(4):
                        ins = nc.tensor.transpose(bank[:, c * P:(c + 1) * P], u_t[:, 4 * g + c, th * P:(th + 1) * P], ident[:, :])
                ins.then_inc(tr_done, 1)

            def u_spectrum(g):
                pe.wait_ge(un_out, 2 * g + 2)
                if g:
                    pe.wait_ge(yf_step, 7)
                for b in range(4):
                    base = 0 if b < 2 else 2
                    for th in range(2):
                        ins = nc.tensor.matmul(acc[:, b, :], dft[:, base + th, (b % 2) * P:(b % 2 + 1) * P],
                                               u_n[:, th, g * 512:g * 512 + 512], start=(th == 0), stop=(th == 1))
                ins.then_inc(uf_done, 1)

            for idx in range(24):
                if idx >= 2:
                    pe.wait_ge(hy_step, HY_STEPS(idx - 2))
                column_unit(Unit(U_HY + idx), region(idx), lat)
                if idx in TR_AT:
                    transposes(TR_AT.index(idx))
                if idx in (12, 20):
                    u_spectrum((12, 20).index(idx))
            pe.wait_ge(hy_step, HY_STEPS(23))
            pe.wait_ge(yf_step, 14)
            for c in range(KT):
                if c >= 2:
                    pe.wait_ge(inv_step, 2 * (c - 2) + 1)
                for k in range(4):
                    ins = nc.tensor.matmul(region(c), y_f[:, k, c * P:(c + 1) * P], dft[:, 4 + k, :], start=(k == 0), stop=(k == 3))
                ins.then_inc(inv_done, 1)
            out_projection(U_HYO, 16)
            mean_of(12)
            mean_of(13)
            ffn(4, 7, LAT, 4 * 13)
            mean_of(14)


class Unit:

    def __init__(self, base, i=None):
        self.base, self.i = base, i

    def plus(self, k):
        return Unit(self.base + k, self.i)


def at_unit(u, k):
    if isinstance(u, int):
        return u + k
    return u.base + k if u.i is None else u.i * 6 + (u.base + k)


PI_F = float(np.float32(3.1415925))
FD_SIN = [7, 14, 21]
FD_SUM = [21 + 5, 21 + 9, 21 + 14, 21 + 18]
FP_DFT = 7
SPECTRUM = [(half, what, w) for half in range(2) for what in ("re", "sine") for w in range(2)] \
    + [(half, "nyquist", 0) for half in range(2)]
FILTER_AT = [(8, 5), (9, 1), (9, 3), (9, 5), (10, 1), (10, 2), (10, 4)]


def at_steps(places, calls):
    table = {}
    for (turn_, k), call in zip(places, calls):
        table.setdefault(turn_, {})[k] = call
    return table


TR_AT = (9, 17)


def hy_tile(idx):
    if idx < 16:
        return 8 + idx // 2 if idx % 2 == 0 else 16 + idx // 2
    return idx - 16


def HY_STEPS(idx):
    return 2 * (idx + 1) + (min(idx + 1, 16) // 2) + max(idx + 1 - 16, 0)



def columns(w):
    k, n = w.shape
    return w.reshape(k // P, P, n // P, P).transpose(2, 1, 0, 3).reshape(n // P, P, k)


def rows(w):
    return w.reshape(w.shape[0] // P, P, D)


def pack_ffn(g, u, d):
    g, u, d = columns(g), columns(u), rows(d)
    return np.stack([g[0::2], u[0::2], g[1::2], u[1::2], d[0::2], d[1::2]], 1).reshape(-1, P, UNIT)


def pack(x, c, ctx, c_ctx, w_mod, b_mod, norm_g, ffn_w_gate, ffn_w_up, ffn_w_down, ab_w_in, na_rpb, sc_conv_w,
         ab_w_out, hy_w_in, hy_short_w, hy_f_w1, hy_f_b1, hy_f_w2, hy_f_b2, hy_f_w3, hy_f_b3, hy_f_w4,
         hy_sin_freq, hy_bias, hy_w_out):
    ffns = [pack_ffn(ffn_w_gate[l, j], ffn_w_up[l, j], ffn_w_down[l, j]) for l, j in FFN_OF]
    ab = columns(ab_w_in[0])
    ab_lat = ab[0:4], np.stack([ab[16:20], ab[20:24], ab[12:16]], 1).reshape(-1, P, UNIT)
    v = ab_w_in[0][:, 1024:1536].reshape(4, 2, P, 512).transpose(0, 2, 1, 3).reshape(4, P, UNIT)
    hy = columns(hy_w_in[0])
    order = [hy_tile(i) for i in range(24)]
    wstream = np.concatenate([ffns[0], ffns[1], *ab_lat, ab[4:8], v, columns(ab_w_out[0]), ffns[2], ffns[3],
                              hy[order], columns(hy_w_out[0]), ffns[4]])
    assert wstream.shape[0] == UNITS
    wmod = np.stack([w_mod[l][:, b * D + h * 512:b * D + h * 512 + 512].reshape(KT, P, 512).transpose(1, 0, 2)
                     for l, b, _ in BLOCKS for h in range(2)])
    cols = {LAT: c.reshape(KT, P).T, CTX: c_ctx.reshape(KT, P).T}
    cjob = np.concatenate([cols[s] for _, _, s in BLOCKS for h in range(2)], 1)
    bmod = np.concatenate([b_mod[l, b * D:b * D + D].reshape(KT, P).T for l, b, _ in BLOCKS], 1)
    small = np.concatenate([norm_g.reshape(12 * KT, P).T, sc_conv_w[0].reshape(12, P).T,
                            hy_short_w[0].reshape(72, P).T, hy_bias[0].reshape(8, P).T], 1)
    rpb = np.zeros((HEADS, 15, 127), np.float32)
    rpb[:, :, 48:79] = na_rpb[0]
    fcols = np.stack([hy_f_b1[0], hy_f_b2[0], hy_f_b3[0], hy_sin_freq[0]], 1)

    def stream(s):
        return s[0].T.reshape(KT, P, T).transpose(1, 0, 2)

    return {"wstream": wstream, "wmod": wmod, "cjob": cjob, "bmod": bmod, "small": small, "x_in": stream(x),
            "ctx_in": stream(ctx), "rpb": rpb, "fw1": hy_f_w1[0], "fw2": hy_f_w2[0], "fw3": hy_f_w3[0],
            "fw4": hy_f_w4[0], "fcols": fcols, **constants()}


def constants():
    f = np.float32
    c = np.arange(GRID_W)
    first = np.clip(c - KW // 2, 0, GRID_W - KW)
    inside = (c[None, :] >= first[:, None]) & (c[None, :] < first[:, None] + KW)
    mask = np.tile(np.where(inside, 0.0, NEG).astype(f)[::-1], (2, 1))
    t = np.linspace(0.0, 1.0, T, dtype=f)[:, None]
    w = (f(2.0 * math.pi) * np.arange(T, dtype=f)[:, None] / f(T)).astype(f)
    bands = np.linspace(1e-4, 15, 16, dtype=f)[None, :]
    bw = (bands * w).astype(f)
    z = np.concatenate([t, np.cos(bw), -np.sin(bw)], 1).astype(f)
    deltas = np.linspace(math.log(1e-2) / 1.5, math.log(1e-2) / 0.3, D, dtype=f)
    window = np.exp(-t * np.abs(deltas)[None, :]).astype(f).reshape(2, P, D).transpose(1, 0, 2)
    n = np.arange(T)
    angle = 2 * np.pi * np.outer(n, n) / (2 * T)
    cos, sin = np.cos(angle), np.sin(angle)
    nyquist = np.where(n % 2, -1.0, 1.0)
    fwd_sin = sin.copy()
    fwd_sin[:, 0] = nyquist
    inv_cos, inv_sin = 2 * cos / (2 * T), 2 * sin / (2 * T)
    inv_cos[0] = 1 / (2 * T)
    inv_sin[0] = nyquist / (2 * T)
    dft = np.stack([cos, fwd_sin, inv_cos, inv_sin]).astype(f).reshape(8, P, T).transpose(1, 0, 2)
    turn = np.kron(np.eye(2, dtype=f), np.eye(GRID_W, dtype=f)[::-1])
    return {"mask_in": mask, "ident_in": np.eye(P, dtype=f), "turn_in": turn, "zfeat": z.T, "window_in": window, "dft_in": dft}


_ORDER = ["wstream", "wmod", "cjob", "bmod", "small", "x_in", "ctx_in", "rpb", "mask_in", "ident_in", "turn_in", "zfeat",
          "fw1", "fw2", "fw3", "fw4", "fcols", "window_in", "dft_in"]


def kernel(**inputs):
    import numpy as _np
    import concourse.bacc as _bacc
    from concourse import mybir as _mybir
    from concourse.bass_utils import run_bass_kernel_spmd as _run

    packed = pack(**{k: _np.asarray(a) for k, a in inputs.items()})
    nc = _bacc.Bacc("TRN2", target_bir_lowering=False, num_devices=1)
    arrays, args = {}, []
    for name in _ORDER:
        a = _np.ascontiguousarray(packed[name])
        arrays[f"in_{name}_dram"] = a
        args.append(nc.dram_tensor(f"in_{name}_dram", a.shape, _mybir.dt.from_np(a.dtype), kind="ExternalInput").ap())
    args.append(nc.dram_tensor("out_0_dram", (P, KT, T), _mybir.dt.float32, kind="ExternalOutput").ap())
    program(nc, *args)
    r = _run(nc, [arrays], core_ids=[0])
    got = r.results[0]["out_0_dram"]
    return got.transpose(1, 0, 2).reshape(D, T).T.reshape(1, T, D)
```

```python
import math
from contextlib import ExitStack

import numpy as np

import concourse.bass as bass
from concourse import mybir

F32 = mybir.dt.float32
F32R = mybir.dt.float32r
ACT = mybir.ActivationFunctionType
ALU = mybir.AluOpType
AX = mybir.AxisListType

P = 128
D = 1024
T = 256
KT = D // P
DFF = 2816
FT = DFF // P
FH = FT // 2
HEADS = 8
DH = 64
GRID_W = 64
ROWS = T // GRID_W
KH, KW = 8, 16
EPS = 1e-6
HY_EMB = 33
HY_FFN = 64
NEG = -1e30

RING = 6
RAW = 3
UNIT = 1024

PER_FFN = 3 * FT
U_CD = PER_FFN
U_AB = U_CD + FT
U_ABO = U_AB + 24
U_F2 = U_ABO + 8
U_HY = U_F2 + 2 * PER_FFN
U_HYO = U_HY + 24
U_F4 = U_HYO + 8
UNITS = U_F4 + PER_FFN
FFN_OF = [(0, 0), (0, 1), (1, 0), (1, 1)]
U_FFN = [0, U_F2, U_F2 + PER_FFN, U_F4]
PAIR0 = [0, 2 * FT, 3 * FT, 4 * FT]
ACT0 = [0, 2 * FT, 3 * FT, 4 * FT]
LOOPS = [{1: 6, 6: 10}, {1: 10}, {1: 5, 6: 8}, {1: 10}]

LAT, CTX = 0, 1
DUAL = 5
PASSES = [(0, b, h, s) for b in range(DUAL) for h in range(2) for s in (LAT, CTX)] \
    + [(l, b, h, LAT) for l, b0 in ((0, DUAL), (1, 0)) for b in range(b0, 9) for h in range(2)]
LOADS = [(l, b, h) for l in range(2) for b in range(9) for h in range(2)]
AHEAD = 4
T_AHEAD = 2 * AHEAD
DUAL_TURNS = 2 * DUAL - AHEAD
WIDE = 2 * FH
JOB_T = [T_AHEAD, T_AHEAD + WIDE, T_AHEAD + WIDE + FH, len(PASSES)]
JOB_L = [AHEAD, JOB_T[1] - 2 * DUAL, JOB_T[2] - 2 * DUAL, len(LOADS)]
JOB_TURNS = [FH, FH, JOB_T[3] - JOB_T[2], 0]

POST, PRE = "post", "pre"
NORMS = [(PRE, 0, LAT, 0, 0, 1), (PRE, 0, CTX, 0, 0, 1),
         (POST, 0, LAT, 1, 2, 0.5), (PRE, 0, LAT, 2, 3, 4),
         (POST, 0, CTX, 1, 2, 0.5), (PRE, 0, CTX, 2, 3, 4),
         (POST, 0, LAT, 3, 5, 1.0), (PRE, 0, LAT, 4, 6, 7),
         (POST, 0, LAT, 5, 8, 0.5), (PRE, 1, LAT, 0, 0, 1),
         (POST, 1, LAT, 1, 2, 0.5), (PRE, 1, LAT, 2, 3, 4),
         (POST, 1, LAT, 3, 5, 1.0), (PRE, 1, LAT, 4, 6, 7),
         (POST, 1, LAT, 5, 8, 0.5)]
BESIDE = {
    2: dict(root=1, recip=1, scale=(2, 2, 3, 3), add=(4, 5, 6, 7), squares=(5, 6, 7, 8)),
    3: dict(mean=9, root=10, recip=11, scale=(12, 12, 13, 14), hi=(12, 13, 14, 15), lo=(13, 14, 15, 16)),
    4: dict(weigh=(0, 0, 1, 1), root=1, recip=2, scale=(2, 3, 3, 4), add=(4, 5, 5, 6), squares=(5, 6, 6, 7)),
    5: dict(mean=8, root=9, recip=9, scale=(10, 10, 11, 12), hi=(10, 11, 12, 13), lo=(11, 12, 13, 14)),
}
LATE = 3
NTH = [sum(n[0] == NORMS[q][0] for n in NORMS[:q]) for q in range(len(NORMS))]
NORM_UNIT = {2: PER_FFN, 4: U_AB, 6: U_F2, 8: U_FFN[2], 10: U_HY, 12: U_F4, 14: UNITS}

S_NORM = 0
S_CONV = S_NORM + 96
S_SHORT = S_CONV + 12
S_BIAS = S_SHORT + 72
S_COLS = S_BIAS + 8


def first_pass(layer, block, stream):
    return PASSES.index((layer, block, 0, stream))


def pass_step(layer, block):
    return 2 if layer == 0 and block < DUAL else 1


def turns_of(f):
    i = 0
    while i < FH:
        end = LOOPS[f].get(i)
        yield i, end
        i = end or i + 1


def mod_column(layer, block, stream, m):
    return 4 * PASSES.index((layer, block, m // 4, stream)) + m % 4


def mod_count(layer, block, stream):
    t = PASSES.index((layer, block, 1, stream))
    return t // 2 + 1 if t < T_AHEAD else AHEAD + sum(t >= t0 for t0 in JOB_T[:3])


def program(nc, wstream, wmod, cjob, cvec_in, bmod, small, x_in, ctx_in, rpb, mask_in, ident_in, turn_in, zfeat, fw1, fw2,
            fw3, fw4, fcols, window_in, dft_in, out):
    with ExitStack() as ctx:
        def sb(name, shape, dt=F32):
            return ctx.enter_context(nc.sbuf_tensor(name, shape, dt))

        def ps(name, shape):
            return ctx.enter_context(nc.psum_tensor(name, shape, F32))

        def sem(name):
            return ctx.enter_context(nc.semaphore(name))

        raw = sb("raw", [P, RAW, UNIT])
        whi = sb("whi", [P, RING, UNIT], F32R)
        wlo = sb("wlo", [P, RING, UNIT], F32R)
        wm = sb("wm", [P, 8, 512])
        part = sb("part", [P, 512])
        total = sb("total", [P, 512])
        cs = sb("cs", [P, len(PASSES) * 8])
        cvec = sb("cvec", [P, KT, 2])
        bm = sb("bm", [P, len(PASSES) * 4])
        mod = sb("mod", [P, len(PASSES) * 4])
        row_sb = sb("row_sb", [WIDE, 512])
        one_in = sb("one_in", [P, 2 * WIDE - 1])
        hot = sb("hot", [P, WIDE])
        sm = sb("sm", [P, S_COLS])
        coef = sb("coef", [P, len(NORMS), KT])
        x_lat = sb("x_lat", [P, KT, T])
        h_hi = [sb("h_lat_hi", [P, KT, T], F32R), sb("h_ctx_hi", [P, KT, T], F32R)]
        h_lo = [sb("h_lat_lo", [P, KT, T], F32R), sb("h_ctx_lo", [P, KT, T], F32R)]
        m_hi, m_lo = h_hi[CTX], h_lo[CTX]
        sq = sb("sq", [P, KT, T])
        z = sb("z", [P, KT, T])
        root = sb("root", [P, T])
        rstd = sb("rstd", [P, T])
        gated = sb("gated", [P, 2, T])
        act = sb("act", [P, 2, T])
        act_hi = sb("act_hi", [P, 2, T], F32R)
        act_lo = sb("act_lo", [P, 2, T], F32R)
        mean_mat = sb("mean_mat", [P, P])
        eps = sb("eps", [P, 1])
        ident = sb("ident", [P, P])
        turn = sb("turn", [P, P])
        mask = sb("mask", [P, GRID_W])
        area = sb("area", [P, 13312])
        at = [0]

        def take(*shape):
            n = int(np.prod(shape))
            v = area[:, at[0]:at[0] + n]
            at[0] += n
            assert at[0] <= 13312
            letters = "abc"[:len(shape)]
            if len(shape) == 1:
                return v
            return v.rearrange(f"p ({' '.join(letters)}) -> p {' '.join(letters)}",
                               **{c: s for c, s in zip(letters, shape)})

        x_ctx = take(KT, T)
        act_ctx = take(FT, T)
        wm_alt = act_ctx[:, 0:16, :].rearrange("p a b -> p (a b)").rearrange("p (k n) -> p k n", n=512)
        at[0] = KT * T
        bias = take(4, 2, T)
        q_t = take(4, T)
        k_t = take(4, 2 * T)
        v_n = take(4, 512)
        conv_b = take(4, T)
        prob = take(4, 2 * T)
        gates = take(3, T)
        prod = take(1, T)
        at[0] -= 4 * T
        prob_t = take(4, T)
        at[0] = 0
        k_re = take(2, D)
        k_s = take(2, D)
        y_f = take(4, D)
        dft = take(8, T)
        x0 = take(KT, T)
        conv = take(4, T)
        k_nyq = [part, total]
        sin_a = x0[:, 0, :]
        sin_k = x0[:, 1, :]
        sin_r = x0[:, 2, :]
        hid = x0[:, 3, :]
        zf = x0[:, 4, :]
        fw = x0[:, 5, :]
        fc = x0[:, 6, 0:4]
        p_f = y_f[:, 0:2, :]
        m_f = y_f[:, 2:4, :]
        w4 = k_re[:, :, :].rearrange("p a b -> p (a b)")
        window = k_s
        u_t = z
        u_n = sq[:, :, :].rearrange("p a b -> p (a b)").rearrange("p (a b) -> p a b", a=2)

        scrap = sb("scrap", [P, 12])
        stats = sb("stats", [P, 4, 4])

        acc = ps("acc", [P, 4, 512])
        gu = ps("gu", [P, 2, 512])
        job_p = ps("job_p", [P, 512])
        mean_p = ps("mean_p", [P, 512])

        def region(i):
            return gu[:, i % 2, 0:T]

        def acc_tile(m):
            return acc[:, m // 2, (m % 2) * T:(m % 2) * T + T]

        def scaled(q):
            return sq if q == 1 else z

        def spectrum_bank(i):
            return [gu[:, 0, :], gu[:, 1, :], job_p[:, :]][i % 3]

        def scores(i):
            return [gu[:, 0, :], gu[:, 1, :], job_p[:, :], mean_p[:, :]][i % 4]

        landed = [sem(f"unit_landed{i}") for i in range(RAW)]
        hi_done, lo_done, pe_done = sem("hi_done"), sem("lo_done"), sem("pe_done")
        wm_landed = [sem("wm_landed0"), sem("wm_landed1")]
        gemv, colsum, mod_ready = sem("gemv_step"), sem("colsum_done"), sem("mod_ready")
        const_in, x_landed, ctx_landed, bias_in = sem("const_in"), sem("x_landed"), sem("ctx_landed"), [sem(f"bias_in{i}") for i in range(4)]
        filt_in, dft_landed = sem("filt_in"), sem("dft_landed")
        made = sem("constants_made")
        c_landed = sem("c_landed")
        alt_landed = [sem("wm_alt_landed0"), sem("wm_alt_landed1")]
        wm_used, row_out, cols_done = sem("wm_used"), sem("row_out"), sem("cols_done")
        weighed = sem("weighed")
        lat_pair, y_copied = sem("latent_pair_done"), sem("y_copied")
        cs_ready = sem("cs_ready")
        sq_done, sum_done, root_done = sem("sq_done"), sem("sum_done"), sem("root_done")
        coef_done, rstd_done, z_done, x_upd = sem("coef_done"), sem("rstd_done"), sem("z_done"), sem("x_updated")
        hf_done, hh_done, h_ready = sem("hf_done"), sem("hh_done"), sem("h_ready")
        silu_done, act_mul, act_hi_done, act_lo_done = sem("silu_done"), sem("act_mul"), sem("act_hi_done"), sem("act_lo_done")
        proj_out, conv_step = sem("proj_out"), sem("conv_step")
        s_done, s_max, p_exp, p_norm = sem("s_done"), sem("s_max"), sem("p_exp"), sem("p_norm")
        soft_step = sem("soft_step")
        pt_done, pt_out, pv_done = sem("pt_done"), sem("pt_out"), sem("pv_done")
        masked = sem("masked")
        m_half, m_ready = sem("m_hi_done"), sem("m_ready")
        hy_act, hy_step, u_ready = sem("hy_act"), sem("hy_step"), sem("u_ready")
        fp, fa, fd = sem("filter_pe"), sem("filter_act"), sem("filter_dve")
        tr_done, un_out, uf_done, yf_step = sem("tr_done"), sem("un_out"), sem("uf_done"), sem("yf_step")
        inv_done, inv_step = sem("inv_done"), sem("inv_step")
        stored = sem("stored")

        X = [x_lat, x_ctx]

        block = ctx.enter_context(nc.Block())

        @block.sync
        def _(sp):
            def load(u, phase):
                sp.dma_start(raw[:, phase % RAW, :],
                             wstream[u] if isinstance(u, int) else
                             wstream[bass.ds(u, 1)].rearrange("a p n -> p (a n)")).then_inc(landed[phase % RAW], 16)

            sp.dma_start(cvec[:, :, :], cvec_in).then_inc(c_landed, 16)
            sp.dma_start(x_lat[:, :, :], x_in).then_inc(x_landed, 16)
            sp.dma_start(cs[:, :], cjob).then_inc(const_in, 16)
            sp.dma_start(sm[:, :], small).then_inc(const_in, 16)
            sp.dma_start(bm[:, :], bmod).then_inc(const_in, 16)
            sp.dma_start(ident[:, :], ident_in).then_inc(const_in, 16)
            sp.dma_start(turn[:, :], turn_in).then_inc(const_in, 16)
            sp.dma_start(mask[:, :], mask_in).then_inc(const_in, 16)
            sp.wait_ge(wm_landed[0], 32)
            sp.dma_start(x_ctx, ctx_in).then_inc(ctx_landed, 16)
            sp.wait_ge(wm_landed[0], 64)
            for u in range(RAW):
                load(u, u)
            for u in range(RAW, RING):
                sp.wait_ge(lo_done, u - RAW + 1)
                load(u, u)
            turns = UNITS // RING
            with sp.Fori(1, turns) as i:
                for k in range(RING):
                    sp.wait_ge(lo_done, i * RING + (k - RAW + 1))
                    load(i * RING + k, k)
            for u in range(turns * RING, UNITS):
                sp.wait_ge(lo_done, u - RAW + 1)
                load(u, u)
            sp.wait_ge(x_upd, 4 * 7)
            sp.dma_start(out, x_lat[:, :, :]).then_inc(stored, 16)
            sp.wait_ge(stored, 16)

        @block.gpsimd
        def _(pool):
            def load_job(l, used=None, count=None, dst=wm, sems=wm_landed):
                for part_ in range(4):
                    if used is not None:
                        pool.wait_ge(used, count(part_))
                    src = wmod[l] if isinstance(l, int) else wmod[bass.ds(l, 1)].rearrange("a p k n -> p (a k) n")
                    pool.dma_start(dst[:, 2 * part_:2 * part_ + 2, :],
                                   src[:, 2 * part_:2 * part_ + 2, :]).then_inc(sems[part_ // 2], 16)

            def steps_before(l):
                return lambda part_: l * 8 + (10 + 2 * part_)

            def load_bias(h):
                if h >= 4:
                    pool.wait_ge(p_exp, 2 * (h - 4) + 2)
                for r in range(ROWS):
                    src = bass.AP(rpb.tensor, rpb.offset + (h * 15 + 7 - r) * 127,
                                  [[1, GRID_W], [127, ROWS], [1, GRID_W]])
                    q0 = (r % 2) * GRID_W
                    dst = bias[q0:q0 + GRID_W, h % 4, r // 2, :].rearrange("p (y k) -> p y k", y=ROWS)
                    pool.dma_start(dst, src).then_inc(bias_in[h % 4], 16)

            def mask_bias(h):
                pool.wait_ge(bias_in[h % 4], 64 * (h // 4 + 1))
                v = bias[:, h % 4, :, :].rearrange("p t (y k) -> p (t y) k", y=ROWS)
                nc.gpsimd.tensor_tensor(v, v, mask[:, :].unsqueeze(1).to_broadcast([P, 2 * ROWS, GRID_W]),
                                        ALU.add).then_inc(masked, 1)

            load_job(0)
            load_job(1, dst=wm_alt, sems=alt_landed)
            load_job(2, wm_used, lambda part_: 1 + part_ // 2)
            load_job(3, wm_used, lambda part_: 3 + part_ // 2, wm_alt, alt_landed)
            load_job(AHEAD, wm_used, lambda part_: 5 + part_ // 2)
            with pool.Fori(1, DUAL_TURNS) as i:
                load_job(i + AHEAD, gemv, lambda part_: i * 16 + (2 * part_ - 6))
            with pool.Fori(AHEAD + DUAL_TURNS, JOB_L[1] + 1) as l:
                load_job(l, gemv, steps_before(l))
            pool.wait_ge(const_in, 16 * 6)
            pool.wait_ge(pe_done, U_AB)
            for h in range(4):
                load_bias(h)
            for h in range(4):
                mask_bias(h)
            for h in range(4, HEADS):
                load_bias(h)
                mask_bias(h)
            pool.wait_ge(x_upd, 4 * 3)
            pool.dma_start(zf[0:HY_EMB, :], zfeat).then_inc(filt_in, 16)
            pool.dma_start(fw[0:HY_EMB, 0:64], fw1).then_inc(filt_in, 16)
            pool.dma_start(fw[0:HY_FFN, 64:128], fw2).then_inc(filt_in, 16)
            pool.dma_start(fw[0:HY_FFN, 128:192], fw3).then_inc(filt_in, 16)
            pool.dma_start(fc[0:HY_FFN, :], fcols).then_inc(filt_in, 16)
            pool.dma_start(dft, dft_in).then_inc(dft_landed, 16)
            pool.dma_start(w4[0:HY_FFN, :], fw4).then_inc(filt_in, 16)
            pool.dma_start(window, window_in).then_inc(filt_in, 16)
            with pool.Fori(JOB_L[1] + 1, len(LOADS)) as l:
                load_job(l, gemv, steps_before(l))

        @block.scalar
        def _(a):
            def split_hi(u, phase, first=False):
                turn = u * 16 if isinstance(u, int) else None
                if isinstance(u, int):
                    a.wait_ge(landed[u % RAW], 16 * (u // RAW + 1))
                else:
                    base, i = u.base, u.i
                    a.wait_ge(landed[base % RAW], i * 32 + 16 * (base // RAW + 1))
                if not first:
                    a.wait_ge(pe_done, at_unit(u, -RING + 1))
                nc.scalar.activation(whi[:, phase % RING, :], raw[:, phase % RAW, :], ACT.Copy).then_inc(hi_done, 1)

            def split(u):
                if u.base < UNITS or u.i is not None:
                    if u.i is None and u.base >= UNITS:
                        return
                    split_hi(u if u.i is not None else u.base, u.base)

            def load_table(func):
                i = tables[0]
                tables[0] += 1
                nc.scalar.activation(scrap[:, i:i + 1], eps[:, 0:1], func)

            tables = [0]

            def squares(q, chunks=range(4)):
                kind, _, stream, *_ = NORMS[q]
                if 0 in chunks:
                    if q:
                        a.wait_ge(sum_done, q)
                    if kind == POST:
                        a.wait_ge(pe_done, NORM_UNIT[q])
                    elif q == 0:
                        a.wait_ge(x_landed, 16)
                    elif q == 1:
                        a.wait_ge(ctx_landed, 16)
                for c in chunks:
                    if kind == PRE and q > 1:
                        a.wait_ge(x_upd, 4 * NTH[q - 1] + c + 1)
                    src = acc[:, c, :] if kind == POST else X[stream][:, 2 * c:2 * c + 2, :]
                    dst = sq[:, 2 * c:2 * c + 2, :]
                    if kind == POST:
                        dst = dst.rearrange("p a b -> p (a b)")
                    nc.scalar.activation(dst, src, ACT.Square).then_inc(sq_done, 1)

            def roots(q):
                a.wait_ge(sum_done, q + 1)
                if q:
                    a.wait_ge(rstd_done, q)
                nc.scalar.activation(root[:, :], mean_p[:, 0:T], ACT.Sqrt, bias=eps[:, 0:1]).then_inc(root_done, 1)

            def weigh(q, chunks=range(4)):
                stream = NORMS[q][2]
                a.wait_ge(coef_done, q + 1)
                for c in chunks:
                    a.wait_ge(x_upd, 4 * NTH[q - 1] + c + 1)
                    for m in (2 * c, 2 * c + 1):
                        ins = nc.scalar.activation(z[:, m, :], X[stream][:, m, :], ACT.Copy, scale=coef[:, q, m:m + 1])
                    ins.then_inc(weighed, 1)

            def h_his(q, chunks=range(4)):
                p = NTH[q]
                _, layer, stream, _, shift, _ = NORMS[q]
                for c in chunks:
                    if q >= LATE:
                        a.wait_ge(z_done, 4 * q + c + 1)
                        for m in (2 * c, 2 * c + 1):
                            col = mod_column(layer, shift, stream, m)
                            ins = nc.scalar.activation(h_hi[stream][:, m, :], z[:, m, :], ACT.Identity,
                                                       bias=mod[:, col:col + 1])
                        ins.then_inc(hh_done, 1)
                        continue
                    a.wait_ge(hf_done, 8 * p + 2 * c + 2)
                    nc.scalar.activation(h_hi[stream][:, 2 * c:2 * c + 2, :], scaled(q)[:, 2 * c:2 * c + 2, :],
                                         ACT.Copy).then_inc(hh_done, 1)

            def norm_parts(qs, at):
                for q in qs:
                    plan = BESIDE[q]
                    if plan["root"] == at:
                        roots(q)
                    for c in range(4):
                        if q in (2, 4) and plan["squares"][c] == at:
                            squares(q + 1, (c,))
                            weigh(q + 1, (c,))
                        if q in (3, 5) and plan["hi"][c] == at:
                            h_his(q, (c,))

            def gate_silu(n, s):
                nc.scalar.activation(gated[:, s, :], gu[:, s, 0:T], ACT.Silu).then_inc(silu_done, 1)

            def act_his(n, s):
                a.wait_ge(act_mul, n + 1)
                nc.scalar.activation(act_hi[:, s, :], act[:, s, :], ACT.Copy).then_inc(act_hi_done, 1)

            def ffn_turn(u, n, both=False, ft=None, between={}, last=False):
                for k in range(6):
                    s = (k // 2) % 2
                    if k in (1, 3):
                        if both:
                            a.wait_ge(lat_pair, ft + (s + 1))
                            gate_silu(n + 2 * s, 0)
                            act_his(n + 2 * s, s)
                            a.wait_ge(pe_done, at_unit(u, k + 1))
                            gate_silu(n + (2 * s + 1), 1)
                        else:
                            a.wait_ge(pe_done, at_unit(u, k + 1))
                            gate_silu(n + s, s)
                            act_his(n + s, s)
                    if not (last and k == 5):
                        split(u.plus(k + RING))
                    if k in between:
                        between[k]()

            def ffn(f, peeled={}):
                for i, end in turns_of(f):
                    if end is None:
                        ffn_turn(Unit(U_FFN[f] + 6 * i), PAIR0[f] + 2 * i, between=peeled.get(i, {}), last=i == FH - 1)
                    else:
                        with a.Fori(i, end) as j:
                            ffn_turn(Unit(U_FFN[f], j), j * 2 + PAIR0[f])

            def row(l):
                a.wait_ge(wm_used, 2 * l + 2)
                if l:
                    a.wait_ge(cols_done, l)
                nc.scalar.activation(row_sb[0:2, :], [job_p, gu[:, 0, :]][l % 2][0:2, :], ACT.Copy).then_inc(row_out, 1)

            def batch_rows(b):
                a.wait_ge(colsum, JOB_T[b + 1] - T_AHEAD)
                a.wait_ge(cols_done, AHEAD + b)
                nc.scalar.activation(row_sb[:, :], job_p[0:WIDE, :], ACT.Copy).then_inc(row_out, 1)

            a.wait_ge(c_landed, 16)
            nc.scalar.activation(cvec[:, :, :], cvec[:, :, :], ACT.Silu).then_inc(cs_ready, 1)
            squares(0)
            a.wait_ge(const_in, 16 * 6)
            nc.scalar.activation(cs[:, :], cs[:, :], ACT.Silu).then_inc(cs_ready, 1)
            a.wait_ge(made, 4)
            row(0)
            roots(0)
            squares(1)
            row(1)
            roots(1)
            row(2)
            row(3)
            split_hi(0, 0, first=True)
            h_his(0)
            split_hi(1, 1, first=True)
            h_his(1)
            for u in range(2, RING):
                split_hi(u, u, first=True)
            for i, end in turns_of(0):
                if end is None:
                    ffn_turn(Unit(6 * i), 4 * i, True, 2 * i)
                else:
                    with a.Fori(i, end) as j:
                        ffn_turn(Unit(0, j), j * 4, True, j * 2)

            def context_his(ft, s, u):
                a.wait_ge(pe_done, at_unit(u, -1))
                src = act_ctx[:, ft, :] if isinstance(ft, int) else act_ctx[:, bass.ds(ft, 1), :].rearrange("p a b -> p (a b)")
                nc.scalar.activation(act_hi[:, s, :], src, ACT.Copy).then_inc(act_hi_done, 1)

            a.wait_ge(act_mul, 2 * FT)
            load_table(ACT.Sqrt)
            context_his(0, 0, Unit(U_CD))
            context_his(1, 1, Unit(U_CD + 1))
            squares(2)
            batch_rows(0)
            for ft in range(FT):
                if ft + 2 < FT:
                    context_his(ft + 2, ft % 2, Unit(U_CD + ft + 2))
                split(Unit(U_CD + ft + RING))
                norm_parts((2, 3), ft)
            squares(4)

            def take_out(idx):
                a.wait_ge(pe_done, U_AB + idx + 1)
                if idx < 4:
                    ins = nc.scalar.activation(q_t[:, idx, :], region(idx), ACT.Copy, scale=DH ** -0.5)
                elif idx < 16:
                    if idx >= 7:
                        a.wait_ge(conv_step, 5 * ((idx - 4) // 3))
                    ins = nc.scalar.activation(gates[:, (idx - 4) % 3, :], region(idx), ACT.Copy)
                else:
                    ins = nc.scalar.activation(k_t[:, idx - 16, :], gu[:, idx % 2, :], ACT.Copy)
                ins.then_inc(proj_out, 1)

            for idx in range(20):
                take_out(idx)
                split(Unit(U_AB + idx + RING))
                norm_parts((4, 5), idx)
            for idx in range(20, 24):
                split(Unit(U_AB + idx + RING))
            a.wait_ge(pe_done, U_AB + 24)
            for t in range(4):
                nc.scalar.activation(v_n[:, t, :], acc[:, t, :], ACT.Copy).then_inc(proj_out, 1)

            for c in range(4):
                a.wait_ge(conv_step, 5 * (c + 1))
                nc.scalar.activation(m_hi[:, 4 + c, :], conv_b[:, c, :], ACT.Copy).then_inc(m_half, 1)

            def exps(h):
                for t in range(2):
                    i = 2 * h + t
                    a.wait_ge(s_max, i + 1)
                    if h >= 2:
                        a.wait_ge(pt_done, i - 3)
                    nc.scalar.activation(prob[:, i % 4, :], scores(i), ACT.Exp, bias=stats[:, i % 4, 1:2],
                                         accum_out=stats[:, i % 4, 2:3]).then_inc(p_exp, 1)

            exps(0)
            for h in range(HEADS):
                if h + 1 < HEADS:
                    exps(h + 1)
                for t in range(2):
                    i = 2 * h + t
                    a.wait_ge(pt_done, i + 1)
                    if h:
                        a.wait_ge(pv_done, h)
                    nc.scalar.activation(prob_t[:, :, t * P:(t + 1) * P],
                                         acc[:, t, :].rearrange("p (k q) -> p k q", k=4),
                                         ACT.Copy).then_inc(pt_out, 1)
            for c in range(7):
                a.wait_ge(pe_done, U_ABO + c + 1)
                split(Unit(U_ABO + c + RING))
            load_table(ACT.Sqrt)
            squares(6)
            split(Unit(U_ABO + 7 + RING))
            roots(6)
            squares(7)
            weigh(7)
            roots(7)
            h_his(7)
            load_table(ACT.Silu)
            ffn(1)
            load_table(ACT.Sqrt)
            squares(8)
            batch_rows(1)
            split(Unit(U_FFN[2] + 5))
            roots(8)
            squares(9)
            weigh(9)
            roots(9)
            h_his(9)
            load_table(ACT.Silu)
            def sine(l):
                a.wait_ge(fd, FD_SIN[l])
                nc.scalar.activation(hid[0:HY_FFN, :], sin_r[0:HY_FFN, :], ACT.Sin).then_inc(fa, 1)

            def spectrum_out(i):
                half, what, w = SPECTRUM[i]
                cols = slice(half * 512, half * 512 + 512)
                a.wait_ge(fp, FP_DFT + i + 1)
                if what == "nyquist":
                    ins = nc.scalar.activation(k_nyq[half][0:1, :], spectrum_bank(i)[0:1, :], ACT.Copy)
                else:
                    ins = nc.scalar.activation((k_re if what == "re" else k_s)[:, w, cols], spectrum_bank(i), ACT.Copy)
                ins.then_inc(fa, 1)

            ffn(2, peeled=at_steps([BATCH_AT] + FILTER_AT, [lambda: batch_rows(2)] + [lambda l=l: sine(l) for l in range(3)]))
            load_table(ACT.Sqrt)
            squares(10)
            split(Unit(U_HY + 5))
            roots(10)
            for i in range(5):
                spectrum_out(i)
            squares(11)
            weigh(11)
            roots(11)
            spectrum_out(5)
            spectrum_out(6)
            h_his(11, (0, 1))
            spectrum_out(7)
            h_his(11, (2, 3))
            spectrum_out(8)
            spectrum_out(9)


            for idx in range(24):
                j = hy_tile(idx)
                a.wait_ge(pe_done, U_HY + idx + 1)
                if idx >= 4:
                    a.wait_ge(hy_step, HY_STEPS(idx - 3 if idx < 20 and idx % 2 == 0 else idx - 4))
                nc.scalar.activation(conv[:, idx % 4, :], region(idx), ACT.Copy,
                                     scale=sm[:, S_SHORT + 24 + j:S_SHORT + 25 + j]).then_inc(hy_act, 1)
                split(Unit(U_HY + idx + RING))
                if idx in (TR_AT[0] + 1, TR_AT[1] + 1):
                    g = (TR_AT[0] + 1, TR_AT[1] + 1).index(idx)
                    a.wait_ge(tr_done, g + 1)
                    nc.scalar.activation(u_n[:, 0, g * 512:g * 512 + 512], job_p[:, :], ACT.Copy).then_inc(un_out, 1)
                    nc.scalar.activation(u_n[:, 1, g * 512:g * 512 + 512], mean_p[:, :], ACT.Copy).then_inc(un_out, 1)
            for c in range(KT):
                a.wait_ge(inv_step, 2 * c + 2)
                nc.scalar.activation(m_hi[:, c, :], conv[:, c % 4, :], ACT.Copy).then_inc(m_half, 1)
            for c in range(7):
                a.wait_ge(pe_done, U_HYO + c + 1)
                split(Unit(U_HYO + c + RING))
            load_table(ACT.Sqrt)
            squares(12)
            split(Unit(U_HYO + 7 + RING))
            roots(12)
            squares(13)
            weigh(13)
            roots(13)
            h_his(13)
            load_table(ACT.Silu)
            ffn(3)
            load_table(ACT.Sqrt)
            squares(14)
            roots(14)

        @block.vector
        def _(v):
            def split(u):
                if u.i is None and u.base >= UNITS:
                    return
                v.wait_ge(hi_done, at_unit(u, 1))
                nc.vector.tensor_tensor(wlo[:, u.base % RING, :], raw[:, u.base % RAW, :],
                                        whi[:, u.base % RING, :].bitcast(F32), ALU.subtract).then_inc(lo_done, 1)

            def job_ops(t, row_, landed_, kts):
                for kt in kts:
                    if kt in (0, 4) and landed_ is not None:
                        v.wait_ge(wm_landed[kt // 4], landed_)
                    fixed = isinstance(t, int)
                    if not (fixed and t == T_AHEAD and kt == 0):
                        v.wait_ge(gemv, t * 8 + (kt - 8 * T_AHEAD))
                    c = cs[:, t * 8 + kt:t * 8 + kt + 1] if fixed else cs[:, bass.ds(t * 8 + kt, 1)]
                    if kt == 7:
                        if not (fixed and t == T_AHEAD):
                            v.wait_ge(colsum, t - T_AHEAD)
                        nc.vector.tensor_copy(hot[:, :], one_in[:, row_:row_ + WIDE] if isinstance(row_, int)
                                              else one_in[:, bass.ds(row_, WIDE)])
                    dst = total if kt == 7 else part
                    if kt == 0:
                        ins = nc.vector.tensor_scalar(dst[:, :], wm[:, kt, :], c, None, ALU.mult)
                    else:
                        ins = nc.vector.scalar_tensor_tensor(out=dst[:, :], in0=wm[:, kt, :], scalar=c,
                                                             in1=part[:, :], op0=ALU.mult, op1=ALU.add)
                    ins.then_inc(gemv, 1)

            def ahead_out(l):
                v.wait_ge(cols_done, l + 1)
                v.wait_ge(const_in, 16 * 6)
                nc.vector.tensor_tensor(mod[:, 8 * l:8 * l + 8].rearrange("p (s i) -> p s i", s=2),
                                        gu[:, 1, 0:8].rearrange("p (i s) -> p s i", s=2),
                                        bm[:, 8 * l:8 * l + 8].rearrange("p (s i) -> p s i", s=2),
                                        ALU.add).then_inc(mod_ready, 1)

            def batch_out(b):
                t, n = JOB_T[b], JOB_T[b + 1] - JOB_T[b]
                v.wait_ge(cols_done, AHEAD + b + 1)
                nc.vector.tensor_tensor(mod[:, 4 * t:4 * (t + n)].rearrange("p (t i) -> p t i", i=4),
                                        job_p[:, 0:4 * n].rearrange("p (i t) -> p t i", i=4),
                                        bm[:, 4 * t:4 * (t + n)].rearrange("p (t i) -> p t i", i=4),
                                        ALU.add).then_inc(mod_ready, 1)

            def norm_coef(q):
                kind, layer, stream, g, b0, b1 = NORMS[q]
                gain = sm[:, S_NORM + (layer * 6 + g) * 8:S_NORM + (layer * 6 + g) * 8 + 8]
                block_ = b0 if kind == POST else b1
                v.wait_ge(mod_ready, mod_count(layer, block_, stream))
                scalar, op = (b1, ALU.mult) if kind == POST else (1.0, ALU.add)
                t, n = first_pass(layer, block_, stream), pass_step(layer, block_)
                cols = mod[:, 4 * t:4 * t + 4 * n + 4].rearrange("p (a b) -> p a b", b=4)[:, ::n, :]
                nc.vector.scalar_tensor_tensor(out=coef[:, q, :].rearrange("p (a b) -> p a b", a=2), in0=cols,
                                               scalar=scalar, in1=gain.rearrange("p (a b) -> p a b", a=2),
                                               op0=op, op1=ALU.mult).then_inc(coef_done, 1)

            def reciprocal(q):
                v.wait_ge(root_done, q + 1)
                if q:
                    v.wait_ge(z_done, 4 * q)
                nc.vector.reciprocal(rstd[:, :], root[:, :]).then_inc(rstd_done, 1)

            def scale(q, c):
                v.wait_ge(rstd_done, q + 1)
                dst = src = scaled(q)[:, 2 * c:2 * c + 2, :]
                if q < 2:
                    src = X[NORMS[q][2]][:, 2 * c:2 * c + 2, :]
                elif q == 2:
                    v.wait_ge(y_copied, c + 1)
                else:
                    v.wait_ge(weighed, 4 * (q - LATE) + c + 1)
                nc.vector.tensor_tensor(dst, src, rstd[:, :].unsqueeze(1).to_broadcast([P, 2, T]),
                                        ALU.mult).then_inc(z_done, 1)

            def weigh(q, c):
                v.wait_ge(coef_done, q + 1)
                if q == 4:
                    v.wait_ge(h_ready, 4 * 3)
                v.wait_ge(sq_done, 4 * q + c + 1)
                for m in (2 * c, 2 * c + 1):
                    ins = nc.vector.tensor_scalar(z[:, m, :], acc_tile(m), coef[:, q, m:m + 1], None, ALU.mult)
                ins.then_inc(weighed, 1)

            def add(q, c):
                v.wait_ge(z_done, 4 * q + c + 1)
                x_ = X[NORMS[q][2]]
                if q >= LATE:
                    x2 = x_[:, 2 * c:2 * c + 2, :]
                    nc.vector.tensor_tensor(x2, x2, z[:, 2 * c:2 * c + 2, :], ALU.add).then_inc(x_upd, 1)
                    return
                v.wait_ge(coef_done, q + 1)
                for m in (2 * c, 2 * c + 1):
                    ins = nc.vector.scalar_tensor_tensor(out=x_[:, m, :], in0=z[:, m, :], scalar=coef[:, q, m:m + 1],
                                                         in1=x_[:, m, :], op0=ALU.mult, op1=ALU.add)
                ins.then_inc(x_upd, 1)

            def lo(q, c):
                _, layer, stream, _, shift, _ = NORMS[q]
                v.wait_ge(hh_done, 4 * NTH[q] + c + 1)
                v.wait_ge(z_done, 4 * q + c + 1)
                for m in (2 * c, 2 * c + 1):
                    col = mod_column(layer, shift, stream, m)
                    ins = nc.vector.scalar_tensor_tensor(out=h_lo[stream][:, m, :], in0=z[:, m, :],
                                                         scalar=mod[:, col:col + 1], in1=h_hi[stream][:, m, :].bitcast(F32),
                                                         op0=ALU.add, op1=ALU.subtract)
                ins.then_inc(h_ready, 1)

            def norm_parts(qs, at):
                for q in qs:
                    plan = BESIDE[q]
                    for c in range(4):
                        if plan.get("weigh", (None,) * 4)[c] == at:
                            weigh(q, c)
                    if plan["recip"] == at:
                        reciprocal(q)
                    if q in (2, 4) and at == plan["scale"][3]:
                        norm_coef(q + 1)
                    for c in range(4):
                        if q in (3, 5) and plan["lo"][c] == at:
                            lo(q, c)
                    for c in range(4):
                        if plan["scale"][c] == at:
                            scale(q, c)
                    for c in range(4):
                        if q in (2, 4) and plan["add"][c] == at:
                            add(q, c)
                    if q in (3, 5) and plan["lo"][3] == at:
                        norm_coef(q + 1)

            def post(q, between=None, held=None):
                for c in range(4):
                    weigh(q, c)
                if held is not None:
                    split(Unit(held))
                reciprocal(q)
                for c in range(4):
                    scale(q, c)
                if between:
                    between()
                if q + 1 < len(NORMS):
                    norm_coef(q + 1)
                for c in range(4):
                    add(q, c)

            def pre(q):
                reciprocal(q)
                scale(q, 0)
                scale(q, 1)
                lo(q, 0)
                scale(q, 2)
                lo(q, 1)
                scale(q, 3)
                lo(q, 2)
                lo(q, 3)

            def pre_rest(q):
                _, layer, stream, _, shift, _ = NORMS[q]
                p, z = NTH[q], scaled(q)
                v.wait_ge(coef_done, q + 1)
                v.wait_ge(mod_ready, mod_count(layer, shift, stream))

                def affine(c):
                    v.wait_ge(z_done, 4 * q + c + 1)
                    for m in (2 * c, 2 * c + 1):
                        col = mod_column(layer, shift, stream, m)
                        nc.vector.tensor_scalar(z[:, m, :], z[:, m, :], coef[:, q, m:m + 1], mod[:, col:col + 1],
                                                ALU.mult, ALU.add).then_inc(hf_done, 1)

                def rest(c):
                    v.wait_ge(hf_done, 8 * p + 2 * c + 2)
                    v.wait_ge(hh_done, 4 * p + c + 1)
                    nc.vector.tensor_tensor(h_lo[stream][:, 2 * c:2 * c + 2, :], z[:, 2 * c:2 * c + 2, :],
                                            h_hi[stream][:, 2 * c:2 * c + 2, :].bitcast(F32), ALU.subtract).then_inc(h_ready, 1)

                affine(0)
                affine(1)
                rest(0)
                affine(2)
                rest(1)
                affine(3)
                rest(2)
                rest(3)

            def gate_up(n, s, dst):
                v.wait_ge(silu_done, n + 1)
                nc.vector.tensor_tensor(dst, gated[:, s, :], gu[:, s, T:2 * T], ALU.mult).then_inc(act_mul, 1)

            def act_los(n, na, s):
                v.wait_ge(act_hi_done, na + 1)
                v.wait_ge(act_mul, n + 1)
                nc.vector.tensor_tensor(act_lo[:, s, :], act[:, s, :], act_hi[:, s, :].bitcast(F32),
                                        ALU.subtract).then_inc(act_lo_done, 1)

            def ffn_turn(u, n, na, job, between={}, last=False):
                def ops(*kts):
                    if job is not None:
                        job_ops(*job, kts)

                for k in range(6):
                    s = (k // 2) % 2
                    if k == 0:
                        ops(0, 1)
                    if k in (1, 3):
                        kt = {1: 2, 3: 5}[k]
                        gate_up(n + s, s, act[:, s, :])
                        ops(kt)
                        act_los(n + s, na + s, s)
                        ops(kt + 1, kt + 2)
                    if not (last and k == 5):
                        split(u.plus(k + RING))
                    if k in between:
                        between[k]()

            def ffn(f, peeled={}):
                n0, a0, t0, l0, jobs = PAIR0[f], ACT0[f], JOB_T[f], JOB_L[f], JOB_TURNS[f]

                def job(i):
                    return (i + t0, i, i * 32 + 32 * (l0 - 1))

                for i, end in turns_of(f):
                    if end is None:
                        ffn_turn(Unit(U_FFN[f] + 6 * i), n0 + 2 * i, a0 + 2 * i, job(i) if i < jobs else None,
                                 peeled.get(i, {}), i == FH - 1)
                    else:
                        with v.Fori(i, end) as j:
                            ffn_turn(Unit(U_FFN[f], j), j * 2 + n0, j * 2 + a0, job(j) if i < jobs else None)

            def both_turn(u, n, ft, i, dual):
                t, r = i * 2 + T_AHEAD, i * 2
                if dual:
                    at_a, at_b = i * 32 + 32 * (AHEAD - 1), None
                else:
                    at_a = i * 64 + 32 * (AHEAD + DUAL_TURNS - 2 * DUAL_TURNS - 1)
                    at_b = at_a + 32
                plan = {0: (0, 1, 2, 3), 1: (4, 5, 6, 7), 2: (8, 9, 10, 11), 3: (12, 13, 14), 4: (15,)}

                def op(x):
                    if x < 8:
                        job_ops(t, r, at_a, (x,))
                    else:
                        job_ops(t + 1, r + 1, at_b, (x - 8,))

                for k in range(6):
                    s = (k // 2) % 2
                    ops = plan.get(k, ())
                    if k in (1, 3):
                        gate_up(n + 2 * s, 0, act[:, s, :])
                        for x in ops[:2]:
                            op(x)
                        act_los(n + 2 * s, ft + s, s)
                        for x in ops[2:]:
                            op(x)
                        dst = act_ctx[:, ft + s, :] if isinstance(ft, int) \
                            else act_ctx[:, bass.ds(ft + s, 1), :].rearrange("p a b -> p (a b)")
                        gate_up(n + (2 * s + 1), 1, dst)
                    else:
                        for x in ops:
                            op(x)
                    split(u.plus(k + RING))

            nc.vector.memset(mean_mat[:, :], 1.0 / D).then_inc(made, 1)
            nc.vector.memset(one_in[:, :], 0.0).then_inc(made, 1)
            nc.vector.memset(eps[:, :], EPS).then_inc(made, 1)
            v.wait_ge(made, 2)
            nc.vector.memset(one_in[:, WIDE - 1:WIDE], 1.0).then_inc(made, 1)
            v.wait_ge(x_landed, 16)
            reciprocal(0)
            for c in range(4):
                scale(0, c)
            v.wait_ge(ctx_landed, 16)
            reciprocal(1)
            v.wait_ge(sum_done, 2)
            for c in range(4):
                scale(1, c)
            for l in range(AHEAD):
                ahead_out(l)
            norm_coef(0)
            norm_coef(1)
            split(Unit(0))
            pre_rest(0)
            split(Unit(1))
            pre_rest(1)
            for u in range(2, RING):
                split(Unit(u))
            v.wait_ge(made, 4)
            v.wait_ge(cs_ready, 2)
            for i, end in turns_of(0):
                if end is None:
                    both_turn(Unit(6 * i), 4 * i, 2 * i, i, i < DUAL_TURNS)
                else:
                    with v.Fori(i, end) as j:
                        both_turn(Unit(0, j), j * 4, j * 2, j, i < DUAL_TURNS)

            def context_los(ft, s):
                v.wait_ge(act_hi_done, ft + (FT + 1))
                src = act_ctx[:, ft, :] if isinstance(ft, int) else act_ctx[:, bass.ds(ft, 1), :].rearrange("p a b -> p (a b)")
                nc.vector.tensor_tensor(act_lo[:, s, :], src, act_hi[:, s, :].bitcast(F32),
                                        ALU.subtract).then_inc(act_lo_done, 1)

            v.wait_ge(act_mul, 2 * FT)
            context_los(0, 0)
            context_los(1, 1)
            for c in range(4):
                v.wait_ge(sq_done, 4 * 2 + c + 1)
                nc.vector.tensor_copy(z[:, 2 * c:2 * c + 2, :].rearrange("p a b -> p (a b)"),
                                      acc[:, c, :]).then_inc(y_copied, 1)
            for ft in range(FT):
                if ft + 2 < FT:
                    context_los(ft + 2, ft % 2)
                split(Unit(U_CD + ft + RING))
                if ft == 1:
                    batch_out(0)
                    norm_coef(2)
                norm_parts((2, 3), ft)

            def short_conv(c):
                n = 5 * c
                v.wait_ge(proj_out, 4 + 3 * c + 3)
                nc.vector.tensor_tensor(prod[:, 0, :], gates[:, 0, :], gates[:, 1, :], ALU.mult).then_inc(conv_step, 1)
                v.wait_ge(conv_step, n + 1)
                w = [sm[:, S_CONV + 4 * i + c:S_CONV + 4 * i + c + 1] for i in range(3)]
                nc.vector.tensor_scalar(conv_b[:, c, :], prod[:, 0, :], w[1], None, ALU.mult).then_inc(conv_step, 1)
                v.wait_ge(conv_step, n + 2)
                nc.vector.scalar_tensor_tensor(out=conv_b[:, c, 1:T], in0=prod[:, 0, 0:T - 1], scalar=w[0],
                                               in1=conv_b[:, c, 1:T], op0=ALU.mult, op1=ALU.add).then_inc(conv_step, 1)
                v.wait_ge(conv_step, n + 3)
                nc.vector.scalar_tensor_tensor(out=conv_b[:, c, 0:T - 1], in0=prod[:, 0, 1:T], scalar=w[2],
                                               in1=conv_b[:, c, 0:T - 1], op0=ALU.mult, op1=ALU.add).then_inc(conv_step, 1)
                v.wait_ge(conv_step, n + 4)
                nc.vector.tensor_tensor(conv_b[:, c, :], conv_b[:, c, :], gates[:, 2, :], ALU.mult).then_inc(conv_step, 1)

            for idx in range(24):
                split(Unit(U_AB + idx + RING))
                norm_parts((4, 5), idx)
                if idx >= 6 and idx % 3 == 0 and idx <= 15:
                    short_conv(idx // 3 - 2)
            for c in range(4):
                v.wait_ge(m_half, c + 1)
                nc.vector.tensor_tensor(m_lo[:, 4 + c, :], conv_b[:, c, :], m_hi[:, 4 + c, :].bitcast(F32),
                                        ALU.subtract).then_inc(m_ready, 1)

            def maxima(h):
                for t in range(2):
                    i, n = 2 * h + t, soft_of(2 * h + t)
                    v.wait_ge(s_done, i + 1)
                    if i >= 4:
                        v.wait_ge(p_norm, i - 3)
                    nc.vector.tensor_reduce(stats[:, i % 4, 0:1], scores(i), AX.X, ALU.max).then_inc(soft_step, 1)
                    v.wait_ge(soft_step, n + 1)
                    nc.vector.tensor_scalar(stats[:, i % 4, 1:2], stats[:, i % 4, 0:1], -1.0, None, ALU.mult).then_inc(s_max, 1)

            def soft_of(i):
                return soft_base[i]

            soft_base, recip_base, n = {}, {}, 0
            for i in (0, 1):
                soft_base[i] = n
                n += 1
            for h in range(HEADS):
                if h + 1 < HEADS:
                    for t in range(2):
                        soft_base[2 * h + 2 + t] = n
                        n += 1
                for t in range(2):
                    recip_base[2 * h + t] = n
                    n += 1
            def pair_out(pair):
                v.wait_ge(pv_done, 2 * pair + 2)
                o = acc[:, 2 + pair % 2, 0:T]
                nc.vector.tensor_copy(m_hi[:, pair, :], o).then_inc(m_half, 1)
                v.wait_ge(m_half, 4 + pair + 1)
                nc.vector.tensor_tensor(m_lo[:, pair, :], o, m_hi[:, pair, :].bitcast(F32),
                                        ALU.subtract).then_inc(m_ready, 1)

            maxima(0)
            for h in range(HEADS):
                if h + 1 < HEADS:
                    maxima(h + 1)
                for t in range(2):
                    i = 2 * h + t
                    v.wait_ge(p_exp, i + 1)
                    nc.vector.reciprocal(stats[:, i % 4, 3:4], stats[:, i % 4, 2:3]).then_inc(soft_step, 1)
                    v.wait_ge(soft_step, recip_base[i] + 1)
                    nc.vector.tensor_scalar(prob[:, i % 4, :], prob[:, i % 4, :], stats[:, i % 4, 3:4], None,
                                            ALU.mult).then_inc(p_norm, 1)
                if h % 2 == 0 and h:
                    pair_out(h // 2 - 1)
            pair_out(HEADS // 2 - 1)
            for c in range(7):
                split(Unit(U_ABO + c + RING))
            post(6, held=U_ABO + 7 + RING)
            pre(7)
            norm_coef(8)
            ffn(1)
            post(8, lambda: batch_out(1), U_FFN[2] + 5)
            pre(9)

            count = [0]

            def step(ins):
                ins.then_inc(fd, 1)
                count[0] += 1

            def settle():
                v.wait_ge(fd, count[0])

            TWO_PI = 2 * math.pi
            c1 = 6.28125
            c2 = float(np.float32(math.floor((TWO_PI - c1) * 2 ** 21) / 2 ** 21))
            c3 = TWO_PI - c1 - c2
            big = 1.5 * 2 ** 23
            H = slice(0, HY_FFN)

            def sine_argument(l):
                if l == 0:
                    v.wait_ge(filt_in, 16 * 7)
                v.wait_ge(fp, l + 1)
                step(nc.vector.tensor_scalar(sin_a[H, :], mean_p[H, 0:T], fc[H, l:l + 1], fc[H, 3:4], ALU.add, ALU.mult))
                settle()
                step(nc.vector.tensor_scalar(sin_k[H, :], sin_a[H, :], 1 / TWO_PI, big, ALU.mult, ALU.add))
                settle()
                step(nc.vector.tensor_scalar(sin_k[H, :], sin_k[H, :], -big, None, ALU.add))
                settle()
                for c in (c1, c2, c3):
                    step(nc.vector.scalar_tensor_tensor(out=sin_a[H, :], in0=sin_k[H, :], scalar=-c, in1=sin_a[H, :],
                                                        op0=ALU.mult, op1=ALU.add))
                    settle()
                step(nc.vector.tensor_scalar(sin_r[H, :], sin_a[H, :], PI_F, -PI_F, ALU.min, ALU.max))
                assert count[0] == FD_SIN[l]

            def filter_sums(i):
                th, half = i % 2, i // 2
                cols = slice(half * 512, half * 512 + 512)
                v.wait_ge(fp, 3 + i + 1)
                step(nc.vector.tensor_tensor(p_f[:, th, cols], job_p[:, :], window[:, th, cols], ALU.mult))
                step(nc.vector.tensor_tensor(m_f[:, th, cols], mean_p[:, :], window[:, th, cols], ALU.mult))
                settle()
                if th == 0:
                    step(nc.vector.memset(m_f[0:1, th, cols], 0.0))
                    settle()
                step(nc.vector.tensor_tensor(p_f[:, th, cols], p_f[:, th, cols], m_f[:, th, cols], ALU.add))
                settle()
                step(nc.vector.scalar_tensor_tensor(out=m_f[:, th, cols], in0=m_f[:, th, cols], scalar=-2.0,
                                                    in1=p_f[:, th, cols], op0=ALU.mult, op1=ALU.add))
                assert count[0] == FD_SUM[i]

            norm_coef(10)
            ffn(2, peeled=at_steps([BATCH_AT] + FILTER_AT, [lambda: batch_out(2)]
                                   + [lambda l=l: sine_argument(l) for l in range(3)]
                                   + [lambda i=i: filter_sums(i) for i in range(4)]))
            post(10, held=U_HY + 5)
            pre(11)
            norm_coef(12)
            v.wait_ge(fa, 3 + 10)
            step(nc.vector.memset(k_s[0:1, 0, :], 0.0))

            def taps(idx):
                j, n = hy_tile(idx), HY_STEPS(idx - 1) if idx else 0
                w0 = sm[:, S_SHORT + j:S_SHORT + j + 1]
                w2 = sm[:, S_SHORT + 48 + j:S_SHORT + 49 + j]
                c = conv[:, idx % 4, :]
                r = region(idx)
                v.wait_ge(hy_act, idx + 1)
                nc.vector.scalar_tensor_tensor(out=c[:, 1:T], in0=r[:, 0:T - 1], scalar=w0, in1=c[:, 1:T],
                                               op0=ALU.mult, op1=ALU.add).then_inc(hy_step, 1)
                v.wait_ge(hy_step, n + 1)
                nc.vector.scalar_tensor_tensor(out=c[:, 0:T - 1], in0=r[:, 1:T], scalar=w2, in1=c[:, 0:T - 1],
                                               op0=ALU.mult, op1=ALU.add).then_inc(hy_step, 1)
                v.wait_ge(hy_step, n + 2)
                if idx < 16 and idx % 2:
                    nc.vector.tensor_tensor(u_t[:, idx // 2, :], conv[:, (idx - 1) % 4, :], c, ALU.mult).then_inc(hy_step, 1)
                elif idx >= 16:
                    nc.vector.tensor_copy(x0[:, idx - 16, :], c).then_inc(hy_step, 1)

            def spectrum_product(g):
                cols = slice(g * 512, g * 512 + 512)
                n = 7 * g
                v.wait_ge(uf_done, g + 1)
                re, s_ = y_f[:, 0:2, cols], y_f[:, 2:4, cols]
                tmp = prod_tmp(0)
                tmp2 = prod_tmp(1)
                nc.vector.tensor_tensor(re, acc[:, 0:2, :], k_re[:, :, cols], ALU.mult).then_inc(yf_step, 1)
                nc.vector.tensor_tensor(tmp, acc[:, 2:4, :], k_s[:, :, cols], ALU.mult).then_inc(yf_step, 1)
                nc.vector.tensor_tensor(s_, acc[:, 0:2, :], k_s[:, :, cols], ALU.mult).then_inc(yf_step, 1)
                nc.vector.tensor_tensor(tmp2, acc[:, 2:4, :], k_re[:, :, cols], ALU.mult).then_inc(yf_step, 1)
                v.wait_ge(yf_step, n + 4)
                nc.vector.tensor_tensor(re, re, tmp, ALU.subtract).then_inc(yf_step, 1)
                nc.vector.tensor_tensor(s_, s_, tmp2, ALU.add).then_inc(yf_step, 1)
                v.wait_ge(yf_step, n + 6)
                nc.vector.tensor_tensor(y_f[0:1, 2, cols], acc[0:1, 2, :], k_nyq[g][0:1, :], ALU.mult).then_inc(yf_step, 1)

            def prod_tmp(i):
                return wm[:, 2 * i:2 * i + 2, :]

            for idx in range(24):
                taps(idx)
                split(Unit(U_HY + idx + RING))
                if idx == 0:
                    v.wait_ge(fd, count[0])
                if idx in (13, 21):
                    spectrum_product((13, 21).index(idx))
            for c in range(KT):
                v.wait_ge(inv_done, c + 1)
                b = sm[:, S_BIAS + c:S_BIAS + c + 1]
                if c >= 4:
                    v.wait_ge(m_ready, 8 + c - 3)
                nc.vector.scalar_tensor_tensor(out=conv[:, c % 4, :], in0=u_t[:, c, :], scalar=b, in1=region(c),
                                               op0=ALU.mult, op1=ALU.add).then_inc(inv_step, 1)
                v.wait_ge(inv_step, 2 * c + 1)
                nc.vector.tensor_tensor(conv[:, c % 4, :], conv[:, c % 4, :], x0[:, c, :], ALU.mult).then_inc(inv_step, 1)
                v.wait_ge(m_half, 8 + c + 1)
                nc.vector.tensor_tensor(m_lo[:, c, :], conv[:, c % 4, :], m_hi[:, c, :].bitcast(F32),
                                        ALU.subtract).then_inc(m_ready, 1)
            for c in range(7):
                split(Unit(U_HYO + c + RING))
            post(12, held=U_HYO + 7 + RING)
            pre(13)
            norm_coef(14)
            ffn(3)
            post(14)

        @block.tensor
        def _(pe):
            def product(out_, w_hi, w_lo, x_hi, x_lo, start, stop):
                nc.tensor.matmul(out_, w_hi, x_hi, start=start, stop=False, skip_group_check=True)
                nc.tensor.matmul(out_, w_hi, x_lo, start=False, stop=False, skip_group_check=True)
                return nc.tensor.matmul(out_, w_lo, x_hi, start=False, stop=stop, skip_group_check=True)

            def wblock(u, kt):
                s = u.base % RING
                return whi[:, s, kt * P:(kt + 1) * P], wlo[:, s, kt * P:(kt + 1) * P]

            def column_unit(u, out_, xs, wait_h=None, last=True):
                pe.wait_ge(lo_done, at_unit(u, 1))
                for kt in range(KT):
                    if wait_h is not None and kt % 2 == 0:
                        pe.wait_ge(h_ready, wait_h + kt // 2 + 1)
                    ins = product(out_, *wblock(u, kt), xs[0][:, kt, :], xs[1][:, kt, :], kt == 0, kt == KT - 1)
                if last:
                    ins.then_inc(pe_done, 1)
                return ins

            def job_sum(t, first=False):
                pe.wait_ge(gemv, t * 8 + (8 - 8 * T_AHEAD))
                nc.tensor.matmul(job_p[0:WIDE, :], hot[:, :], total[:, :], start=first, stop=True,
                                 skip_group_check=True).then_inc(colsum, 1)

            def batch_columns(b):
                n = JOB_T[b + 1] - JOB_T[b]
                pe.wait_ge(row_out, AHEAD + b + 1)
                for i in range(4):
                    ins = nc.tensor.matmul(job_p[:, i * n:(i + 1) * n], row_sb[:, i * P:(i + 1) * P],
                                           turn[0:WIDE, GRID_W - WIDE:GRID_W - WIDE + n], start=True, stop=True)
                ins.then_inc(cols_done, 1)

            def mean_of(q):
                if q:
                    pe.wait_ge(root_done, q)
                for m in range(KT):
                    if m % 2 == 0:
                        pe.wait_ge(sq_done, 4 * q + m // 2 + 1)
                    ins = nc.tensor.matmul(mean_p[:, 0:T], mean_mat[:, :], sq[:, m, :], start=(m == 0), stop=(m == KT - 1))
                ins.then_inc(sum_done, 1)

            def down(uk, s, first, stop, copied=False):
                pe.wait_ge(lo_done, at_unit(uk, 1))
                for m in range(KT):
                    if copied and m % 2 == 0:
                        pe.wait_ge(y_copied, m // 2 + 1)
                    ins = product(acc_tile(m), *wblock(uk, m), act_hi[:, s, :], act_lo[:, s, :],
                                  first and m % 2 == 0, stop)
                ins.then_inc(pe_done, 1)

            def column_units(us, outs, xs, wait_h):
                for u in us:
                    pe.wait_ge(lo_done, at_unit(u, 1))
                for c in range(KT // 2):
                    pe.wait_ge(h_ready, wait_h + c + 1)
                    for u, (out_, bank_first) in zip(us, outs):
                        for kt in (2 * c, 2 * c + 1):
                            ins = product(out_, *wblock(u, kt), xs[0][:, kt, :], xs[1][:, kt, :],
                                          kt == 0 and bank_first, kt == KT - 1)
                        if c == KT // 2 - 1:
                            ins.then_inc(pe_done, 1)

            def ffn_turn(u, n, na, t, xs, first=False, acc_free=0, wait_h=None, stop=False, between={}):
                if first:
                    pe.wait_ge(act_mul, n - 1)
                    column_units([u, u.plus(1)], [(gu[:, 0, 0:T], True), (gu[:, 0, T:2 * T], False)], xs, wait_h)
                for k in range(2 if first else 0, 6):
                    s = (k // 2) % 2
                    uk = u.plus(k)
                    if k < 4:
                        if k % 2 == 0:
                            pe.wait_ge(act_mul, n + (s - 1))
                        column_unit(uk, gu[:, s, (k % 2) * T:(k % 2) * T + T], xs)
                    else:
                        s = k - 4
                        if first and s == 0:
                            pe.wait_ge(weighed, acc_free)
                        pe.wait_ge(act_lo_done, na + (s + 1))
                        down(uk, s, first and s == 0, stop and s == 1)
                    if k == 5 and t is not None:
                        job_sum(t, first)
                    if k in between:
                        between[k]()

            def ffn(f, p, acc_free, peeled={}):
                xs = (h_hi[LAT], h_lo[LAT])
                n0, a0, t0, u0, jobs = PAIR0[f], ACT0[f], JOB_T[f], U_FFN[f], JOB_TURNS[f]
                for i, end in turns_of(f):
                    if end is None:
                        ffn_turn(Unit(u0 + 6 * i), n0 + 2 * i, a0 + 2 * i, t0 + i if i < jobs else None, xs, i == 0,
                                 acc_free, 4 * p if i == 0 else None, i == FH - 1, peeled.get(i, {}))
                    else:
                        with pe.Fori(i, end) as j:
                            ffn_turn(Unit(u0, j), j * 2 + n0, j * 2 + a0, j + t0 if i < jobs else None, xs)

            def ahead(l):
                src, sems = ((wm, wm_landed), (wm_alt, alt_landed))[l % 2]
                if l >= 2:
                    pe.wait_ge(row_out, l - 1)
                for kt in range(KT):
                    if kt % 4 == 0:
                        pe.wait_ge(sems[kt // 4], 32 * (l // 2 + 1))
                    ins = nc.tensor.matmul([job_p, gu[:, 0, :]][l % 2][0:2, :], cvec[:, kt, :], src[:, kt, :],
                                           start=(kt == 0), stop=(kt == KT - 1))
                    if kt == 3:
                        ins.then_inc(wm_used, 1)
                ins.then_inc(wm_used, 1)

            def ahead_columns(l):
                pe.wait_ge(row_out, l + 1)
                if l == 0:
                    pe.wait_ge(const_in, 16 * 6)
                else:
                    pe.wait_ge(mod_ready, l)
                for i in range(4):
                    ins = nc.tensor.matmul(gu[:, 1, 2 * i:2 * i + 2], row_sb[0:2, i * P:(i + 1) * P], ident[0:2, 0:2],
                                           start=True, stop=True)
                ins.then_inc(cols_done, 1)

            pe.wait_ge(cs_ready, 1)
            ahead(0)
            pe.wait_ge(made, 4)
            mean_of(0)
            ahead(1)
            ahead_columns(0)
            mean_of(1)
            ahead(2)
            ahead_columns(1)
            ahead(3)
            ahead_columns(2)
            ahead_columns(3)

            def both_turn(u, n, ft, i, first=False, stop=False):
                t = i * 2 + T_AHEAD
                for k in range(6):
                    s = (k // 2) % 2
                    uk = u.plus(k)
                    if k < 4:
                        pe.wait_ge(lo_done, at_unit(uk, 1))
                        for stream in (LAT, CTX):
                            if k % 2 == 0 and not (first and k == 0):
                                pe.wait_ge(act_mul, n + (2 * s + stream - 1))
                            for kt in range(KT):
                                if first and k == 0 and kt % 2 == 0:
                                    pe.wait_ge(h_ready, 4 * stream + kt // 2 + 1)
                                ins = product(gu[:, stream, (k % 2) * T:(k % 2) * T + T], *wblock(uk, kt),
                                              h_hi[stream][:, kt, :], h_lo[stream][:, kt, :], kt == 0, kt == KT - 1)
                            if stream == CTX:
                                ins.then_inc(pe_done, 1)
                            elif k % 2:
                                ins.then_inc(lat_pair, 1)
                    else:
                        s = k - 4
                        pe.wait_ge(act_lo_done, ft + (s + 1))
                        down(uk, s, first and s == 0, stop and s == 1)
                    if k == 2:
                        job_sum(t, first)
                    if k == 5:
                        job_sum(t + 1)

            pe.wait_ge(mod_ready, AHEAD)
            for i, end in turns_of(0):
                if end is None:
                    both_turn(Unit(6 * i), 4 * i, 2 * i, i, i == 0, i == FH - 1)
                else:
                    with pe.Fori(i, end) as j:
                        both_turn(Unit(0, j), j * 4, j * 2, j)

            def context_down(u, ft, s, first=False, stop=False):
                pe.wait_ge(act_lo_done, ft + (FT + 1))
                down(u, s, first, stop, first)

            for ft in range(FT):
                context_down(Unit(U_CD + ft), ft, ft % 2, ft == 0, ft == FT - 1)
                if ft == 0:
                    mean_of(2)
                    batch_columns(0)
                if ft == BESIDE[3]["mean"]:
                    mean_of(3)

            lat = (h_hi[LAT], h_lo[LAT])
            pe.wait_ge(h_ready, 4 * 3)
            pe.wait_ge(act_mul, 2 * FT)
            for idx in range(16):
                if idx >= 2:
                    pe.wait_ge(proj_out, idx - 1)
                column_unit(Unit(U_AB + idx), region(idx), lat)
                if idx == 0:
                    mean_of(4)
                if idx == BESIDE[5]["mean"]:
                    mean_of(5)
            con = (h_hi[CTX], h_lo[CTX])
            pe.wait_ge(h_ready, 4 * 4)
            for idx in range(16, 20):
                pe.wait_ge(proj_out, idx - 1)
                column_unit(Unit(U_AB + idx), gu[:, idx % 2, 0:T], lat, last=False)
                column_unit(Unit(U_AB + idx), gu[:, idx % 2, T:2 * T], con)
            pe.wait_ge(z_done, 4 * 5)
            for c in range(4):
                u = Unit(U_AB + 20 + c)
                s = u.base % RING
                pe.wait_ge(lo_done, u.base + 1)
                for half in range(2):
                    kt = 2 * c + half
                    w_hi, w_lo = (w[:, s, half * 512:half * 512 + 512] for w in (whi, wlo))
                    for t in range(4):
                        st = t // 2
                        tok = slice((t % 2) * P, (t % 2) * P + P)
                        x_hi, x_lo = h_hi[st][:, kt, tok], h_lo[st][:, kt, tok]
                        nc.tensor.matmul(acc[:, t, :], x_hi, w_hi, start=(kt == 0), stop=False, skip_group_check=True)
                        nc.tensor.matmul(acc[:, t, :], x_lo, w_hi, start=False, stop=False, skip_group_check=True)
                        ins = nc.tensor.matmul(acc[:, t, :], x_hi, w_lo, start=False, stop=(kt == KT - 1),
                                               skip_group_check=True)
                ins.then_inc(pe_done, 1)

            def score(h):
                rows = slice(DH * (h % 2), DH * (h % 2) + DH)
                pe.wait_ge(masked, h + 1)
                for t in range(2):
                    i = 2 * h + t
                    if h >= 2:
                        pe.wait_ge(p_exp, i - 3)
                    nc.tensor.matmul(scores(i), q_t[rows, h // 2, t * P:(t + 1) * P], k_t[rows, h // 2, :],
                                     start=True, stop=False, skip_group_check=True)
                    nc.tensor.matmul(scores(i)[:, 0:T], turn[:, :], bias[:, h % 4, t, :], start=False, stop=True,
                                     skip_group_check=True).then_inc(s_done, 1)

            pe.wait_ge(proj_out, 24)
            pe.wait_ge(mod_ready, AHEAD + 1)
            score(0)
            score(1)
            for h in range(HEADS):
                for t in range(2):
                    i = 2 * h + t
                    pe.wait_ge(p_norm, i + 1)
                    if h:
                        pe.wait_ge(pt_out, i - 1)
                    for k in range(4):
                        ins = nc.tensor.transpose(acc[:, t, k * P:(k + 1) * P], prob[:, i % 4, k * P:(k + 1) * P], ident[:, :])
                    ins.then_inc(pt_done, 1)
                if h + 2 < HEADS:
                    score(h + 2)
                pe.wait_ge(pt_out, 2 * h + 2)
                pair = h // 2
                if h % 2 == 0 and pair >= 2:
                    pe.wait_ge(m_ready, 4 + pair - 1)
                rows = slice(DH * (h % 2), DH * (h % 2) + DH)
                for k in range(4):
                    ins = nc.tensor.matmul(acc[rows, 2 + pair % 2, 0:T], v_n[:, k, h * DH:(h + 1) * DH], prob_t[:, k, :],
                                           start=(k == 0), stop=(k == 3))
                ins.then_inc(pv_done, 1)

            def out_projection(u0, ready):
                pe.wait_ge(m_ready, ready)
                for m in range(KT):
                    u = Unit(u0 + m)
                    pe.wait_ge(lo_done, u.base + 1)
                    for kt in range(KT):
                        ins = product(acc_tile(m), *wblock(u, kt), m_hi[:, kt, :], m_lo[:, kt, :], kt == 0, kt == KT - 1)
                    ins.then_inc(pe_done, 1)

            out_projection(U_ABO, 8)
            mean_of(6)
            mean_of(7)
            ffn(1, 4, 4 * (6 - LATE + 1))
            mean_of(8)
            batch_columns(1)
            mean_of(9)

            E = slice(0, HY_EMB)
            H = slice(0, HY_FFN)

            def filter_layer(l):
                if l == 0:
                    pe.wait_ge(filt_in, 16 * 7)
                    w, x_ = fw[E, 0:64], zf[E, :]
                else:
                    pe.wait_ge(fa, l)
                    w, x_ = fw[H, 64 * l:64 * l + 64], hid[H, :]
                nc.tensor.matmul(mean_p[H, 0:T], w, x_, start=True, stop=True).then_inc(fp, 1)

            def filter_out(i):
                th, half = i % 2, i // 2
                if i == 0:
                    pe.wait_ge(fa, 3)
                    pe.wait_ge(mod_ready, AHEAD + 3)
                else:
                    pe.wait_ge(fd, FD_SUM[i - 1])
                for b, bank in enumerate((job_p, mean_p)):
                    ins = nc.tensor.matmul(bank[:, :], hid[H, th * P:(th + 1) * P],
                                           w4[H, b * D + half * 512:b * D + half * 512 + 512], start=True, stop=True)
                ins.then_inc(fp, 1)

            def spectrum(i):
                half, what, w = SPECTRUM[i]
                cols = slice(half * 512, half * 512 + 512)
                if i >= 3:
                    pe.wait_ge(fa, 3 + i - 2)
                for th in range(2):
                    if what == "nyquist":
                        out_, w_, x_ = spectrum_bank(i)[0:1, :], dft[:, 2 + th, 0:1], p_f
                    else:
                        base = 0 if what == "re" else 2
                        out_, w_, x_ = spectrum_bank(i), dft[:, base + th, w * P:(w + 1) * P], p_f if what == "re" else m_f
                    ins = nc.tensor.matmul(out_, w_, x_[:, th, cols], start=(th == 0), stop=(th == 1))
                ins.then_inc(fp, 1)

            ffn(2, 5, 4 * (8 - LATE + 1), peeled=at_steps([BATCH_AT] + FILTER_AT, [lambda: batch_columns(2)]
                                             + [lambda l=l: filter_layer(l) for l in range(3)]
                                             + [lambda i=i: filter_out(i) for i in range(4)]))
            pe.wait_ge(dft_landed, 16)
            pe.wait_ge(act_mul, 4 * FT)
            pe.wait_ge(fd, FD_SUM[3])
            mean_of(10)
            for i in range(5):
                spectrum(i)
            mean_of(11)
            for i in range(5, 10):
                spectrum(i)

            pe.wait_ge(h_ready, 4 * 7)
            pe.wait_ge(fa, 3 + 10)

            def transposes(g):
                pe.wait_ge(hy_step, HY_STEPS(8 * g + 7))
                if g:
                    pe.wait_ge(un_out, 2)
                for th, bank in ((0, job_p), (1, mean_p)):
                    for c in range(4):
                        ins = nc.tensor.transpose(bank[:, c * P:(c + 1) * P], u_t[:, 4 * g + c, th * P:(th + 1) * P], ident[:, :])
                ins.then_inc(tr_done, 1)

            def u_spectrum(g):
                pe.wait_ge(un_out, 2 * g + 2)
                if g:
                    pe.wait_ge(yf_step, 7)
                for b in range(4):
                    base = 0 if b < 2 else 2
                    for th in range(2):
                        ins = nc.tensor.matmul(acc[:, b, :], dft[:, base + th, (b % 2) * P:(b % 2 + 1) * P],
                                               u_n[:, th, g * 512:g * 512 + 512], start=(th == 0), stop=(th == 1))
                ins.then_inc(uf_done, 1)

            for idx in range(24):
                if idx >= 2:
                    pe.wait_ge(hy_step, HY_STEPS(idx - 2))
                column_unit(Unit(U_HY + idx), region(idx), lat)
                if idx in TR_AT:
                    transposes(TR_AT.index(idx))
                if idx in (12, 20):
                    u_spectrum((12, 20).index(idx))
            pe.wait_ge(hy_step, HY_STEPS(23))
            pe.wait_ge(yf_step, 14)
            for c in range(KT):
                if c >= 2:
                    pe.wait_ge(inv_step, 2 * (c - 2) + 1)
                for k in range(4):
                    ins = nc.tensor.matmul(region(c), y_f[:, k, c * P:(c + 1) * P], dft[:, 4 + k, :], start=(k == 0), stop=(k == 3))
                ins.then_inc(inv_done, 1)
            out_projection(U_HYO, 16)
            mean_of(12)
            mean_of(13)
            ffn(3, 7, 4 * (12 - LATE + 1))
            mean_of(14)


class Unit:

    def __init__(self, base, i=None):
        self.base, self.i = base, i

    def plus(self, k):
        return Unit(self.base + k, self.i)


def at_unit(u, k):
    if isinstance(u, int):
        return u + k
    return u.base + k if u.i is None else u.i * 6 + (u.base + k)


PI_F = float(np.float32(3.1415925))
FD_SIN = [7, 14, 21]
FD_SUM = [21 + 5, 21 + 9, 21 + 14, 21 + 18]
FP_DFT = 7
SPECTRUM = [(half, what, w) for half in range(2) for what in ("re", "sine") for w in range(2)] \
    + [(half, "nyquist", 0) for half in range(2)]
BATCH_AT = (5, 0)
FILTER_AT = [(8, 5), (9, 1), (9, 3), (9, 5), (10, 1), (10, 2), (10, 4)]


def at_steps(places, calls):
    table = {}
    for (turn_, k), call in zip(places, calls):
        table.setdefault(turn_, {})[k] = call
    return table


TR_AT = (9, 17)


def hy_tile(idx):
    if idx < 16:
        return 8 + idx // 2 if idx % 2 == 0 else 16 + idx // 2
    return idx - 16


def HY_STEPS(idx):
    return 2 * (idx + 1) + (min(idx + 1, 16) // 2) + max(idx + 1 - 16, 0)



def columns(w):
    k, n = w.shape
    return w.reshape(k // P, P, n // P, P).transpose(2, 1, 0, 3).reshape(n // P, P, k)


def rows(w):
    return w.reshape(w.shape[0] // P, P, D)


def pack_ffn(g, u, d):
    g, u, d = columns(g), columns(u), rows(d)
    return np.stack([g[0::2], u[0::2], g[1::2], u[1::2], d[0::2], d[1::2]], 1).reshape(-1, P, UNIT)


def pack(x, c, ctx, c_ctx, w_mod, b_mod, norm_g, ffn_w_gate, ffn_w_up, ffn_w_down, ab_w_in, na_rpb, sc_conv_w,
         ab_w_out, hy_w_in, hy_short_w, hy_f_w1, hy_f_b1, hy_f_w2, hy_f_b2, hy_f_w3, hy_f_b3, hy_f_w4,
         hy_sin_freq, hy_bias, hy_w_out):
    ffns = [pack_ffn(ffn_w_gate[l, j], ffn_w_up[l, j], ffn_w_down[l, j]) for l, j in FFN_OF]
    ab = columns(ab_w_in[0])
    ab_lat = ab[0:4], np.stack([ab[16:20], ab[20:24], ab[12:16]], 1).reshape(-1, P, UNIT)
    v = ab_w_in[0][:, 1024:1536].reshape(4, 2, P, 512).transpose(0, 2, 1, 3).reshape(4, P, UNIT)
    hy = columns(hy_w_in[0])
    order = [hy_tile(i) for i in range(24)]
    wstream = np.concatenate([ffns[0], rows(ffn_w_down[0, 0]), *ab_lat, ab[4:8], v, columns(ab_w_out[0]), ffns[1],
                              ffns[2], hy[order], columns(hy_w_out[0]), ffns[3]])
    assert wstream.shape[0] == UNITS
    wmod = np.stack([w_mod[l][:, b * D + h * 512:b * D + h * 512 + 512].reshape(KT, P, 512).transpose(1, 0, 2)
                     for l, b, h in LOADS])
    cols = {LAT: c.reshape(KT, P).T, CTX: c_ctx.reshape(KT, P).T}
    cjob = np.concatenate([cols[s] for *_, s in PASSES], 1)
    cvec = np.stack([cols[LAT], cols[CTX]], 2)
    bmod = np.concatenate([b_mod[l, b * D + h * 512:b * D + h * 512 + 512].reshape(4, P).T for l, b, h, _ in PASSES], 1)
    small = np.concatenate([norm_g.reshape(12 * KT, P).T, sc_conv_w[0].reshape(12, P).T,
                            hy_short_w[0].reshape(72, P).T, hy_bias[0].reshape(8, P).T], 1)
    rpb = np.zeros((HEADS, 15, 127), np.float32)
    rpb[:, :, 48:79] = na_rpb[0]
    fcols = np.stack([hy_f_b1[0], hy_f_b2[0], hy_f_b3[0], hy_sin_freq[0]], 1)

    def stream(s):
        return s[0].T.reshape(KT, P, T).transpose(1, 0, 2)

    return {"wstream": wstream, "wmod": wmod, "cjob": cjob, "cvec_in": cvec, "bmod": bmod, "small": small, "x_in": stream(x),
            "ctx_in": stream(ctx), "rpb": rpb, "fw1": hy_f_w1[0], "fw2": hy_f_w2[0], "fw3": hy_f_w3[0],
            "fw4": hy_f_w4[0], "fcols": fcols, **constants()}


def constants():
    f = np.float32
    c = np.arange(GRID_W)
    first = np.clip(c - KW // 2, 0, GRID_W - KW)
    inside = (c[None, :] >= first[:, None]) & (c[None, :] < first[:, None] + KW)
    mask = np.tile(np.where(inside, 0.0, NEG).astype(f)[::-1], (2, 1))
    t = np.linspace(0.0, 1.0, T, dtype=f)[:, None]
    w = (f(2.0 * math.pi) * np.arange(T, dtype=f)[:, None] / f(T)).astype(f)
    bands = np.linspace(1e-4, 15, 16, dtype=f)[None, :]
    bw = (bands * w).astype(f)
    z = np.concatenate([t, np.cos(bw), -np.sin(bw)], 1).astype(f)
    deltas = np.linspace(math.log(1e-2) / 1.5, math.log(1e-2) / 0.3, D, dtype=f)
    window = np.exp(-t * np.abs(deltas)[None, :]).astype(f).reshape(2, P, D).transpose(1, 0, 2)
    n = np.arange(T)
    angle = 2 * np.pi * np.outer(n, n) / (2 * T)
    cos, sin = np.cos(angle), np.sin(angle)
    nyquist = np.where(n % 2, -1.0, 1.0)
    fwd_sin = sin.copy()
    fwd_sin[:, 0] = nyquist
    inv_cos, inv_sin = 2 * cos / (2 * T), 2 * sin / (2 * T)
    inv_cos[0] = 1 / (2 * T)
    inv_sin[0] = nyquist / (2 * T)
    dft = np.stack([cos, fwd_sin, inv_cos, inv_sin]).astype(f).reshape(8, P, T).transpose(1, 0, 2)
    turn = np.kron(np.eye(2, dtype=f), np.eye(GRID_W, dtype=f)[::-1])
    return {"mask_in": mask, "ident_in": np.eye(P, dtype=f), "turn_in": turn, "zfeat": z.T, "window_in": window, "dft_in": dft}


_ORDER = ["wstream", "wmod", "cjob", "cvec_in", "bmod", "small", "x_in", "ctx_in", "rpb", "mask_in", "ident_in", "turn_in", "zfeat",
          "fw1", "fw2", "fw3", "fw4", "fcols", "window_in", "dft_in"]


def kernel(**inputs):
    import numpy as _np
    import concourse.bacc as _bacc
    from concourse import mybir as _mybir
    from concourse.bass_utils import run_bass_kernel_spmd as _run

    packed = pack(**{k: _np.asarray(a) for k, a in inputs.items()})
    nc = _bacc.Bacc("TRN2", target_bir_lowering=False, num_devices=1)
    arrays, args = {}, []
    for name in _ORDER:
        a = _np.ascontiguousarray(packed[name])
        arrays[f"in_{name}_dram"] = a
        args.append(nc.dram_tensor(f"in_{name}_dram", a.shape, _mybir.dt.from_np(a.dtype), kind="ExternalInput").ap())
    args.append(nc.dram_tensor("out_0_dram", (P, KT, T), _mybir.dt.float32, kind="ExternalOutput").ap())
    program(nc, *args)
    r = _run(nc, [arrays], core_ids=[0])
    got = r.results[0]["out_0_dram"]
    return got.transpose(1, 0, 2).reshape(D, T).T.reshape(1, T, D)
```

```python
import math
from contextlib import ExitStack

import numpy as np

import concourse.bass as bass
from concourse import mybir

F32 = mybir.dt.float32
F32R = mybir.dt.float32r
ACT = mybir.ActivationFunctionType
ALU = mybir.AluOpType
AX = mybir.AxisListType

P = 128
D = 1024
T = 256
KT = D // P
DFF = 2816
FT = DFF // P
FH = FT // 2
HEADS = 8
DH = 64
GRID_W = 64
ROWS = T // GRID_W
KH, KW = 8, 16
EPS = 1e-6
HY_EMB = 33
HY_FFN = 64
NEG = -1e30

RING = 6
RAW = 3
UNIT = 1024

PER_FFN = 3 * FT
U_CD = PER_FFN
U_AB = U_CD + FT
U_ABO = U_AB + 24
U_F2 = U_ABO + 8
U_HY = U_F2 + 2 * PER_FFN
U_HYO = U_HY + 24
U_F4 = U_HYO + 8
UNITS = U_F4 + PER_FFN
FFN_OF = [(0, 0), (0, 1), (1, 0), (1, 1)]
U_FFN = [0, U_F2, U_F2 + PER_FFN, U_F4]
PAIR0 = [0, 2 * FT, 3 * FT, 4 * FT]
ACT0 = [0, 2 * FT, 3 * FT, 4 * FT]
LOOPS = [{1: 6, 6: 10}, {1: 10}, {1: 5, 6: 8}, {1: 10}]

LAT, CTX = 0, 1
DUAL = 5
PASSES = [(0, b, h, s) for b in range(DUAL) for h in range(2) for s in (LAT, CTX)] \
    + [(l, b, h, LAT) for l, b0 in ((0, DUAL), (1, 0)) for b in range(b0, 9) for h in range(2)]
LOADS = [(l, b, h) for l in range(2) for b in range(9) for h in range(2)]
AHEAD = 4
T_AHEAD = 2 * AHEAD
DUAL_TURNS = 2 * DUAL - AHEAD
WIDE = 2 * FH
JOB_T = [T_AHEAD, T_AHEAD + WIDE, T_AHEAD + WIDE + FH, len(PASSES)]
JOB_L = [AHEAD, JOB_T[1] - 2 * DUAL, JOB_T[2] - 2 * DUAL, len(LOADS)]
JOB_TURNS = [FH, FH, JOB_T[3] - JOB_T[2], 0]

POST, PRE = "post", "pre"
NORMS = [(PRE, 0, LAT, 0, 0, 1), (PRE, 0, CTX, 0, 0, 1),
         (POST, 0, LAT, 1, 2, 0.5), (PRE, 0, LAT, 2, 3, 4),
         (POST, 0, CTX, 1, 2, 0.5), (PRE, 0, CTX, 2, 3, 4),
         (POST, 0, LAT, 3, 5, 1.0), (PRE, 0, LAT, 4, 6, 7),
         (POST, 0, LAT, 5, 8, 0.5), (PRE, 1, LAT, 0, 0, 1),
         (POST, 1, LAT, 1, 2, 0.5), (PRE, 1, LAT, 2, 3, 4),
         (POST, 1, LAT, 3, 5, 1.0), (PRE, 1, LAT, 4, 6, 7),
         (POST, 1, LAT, 5, 8, 0.5)]
BESIDE = {
    2: dict(root=1, recip=1, scale=(2, 2, 3, 3), add=(4, 5, 6, 7), squares=(5, 6, 7, 8)),
    3: dict(mean=9, root=10, recip=11, scale=(12, 12, 13, 14), hi=(12, 13, 14, 15), lo=(13, 14, 15, 16)),
    4: dict(weigh=(0, 1, 1, 2), root=1, recip=2, scale=(2, 3, 3, 4), add=(4, 5, 5, 6), squares=(5, 6, 6, 7)),
    5: dict(mean=8, root=9, recip=9, scale=(10, 10, 11, 12), hi=(10, 11, 12, 13), lo=(11, 12, 13, 14)),
}
LATE = 3
NTH = [sum(n[0] == NORMS[q][0] for n in NORMS[:q]) for q in range(len(NORMS))]
NORM_UNIT = {2: PER_FFN, 4: U_AB, 6: U_F2, 8: U_FFN[2], 10: U_HY, 12: U_F4, 14: UNITS}

S_NORM = 0
S_CONV = S_NORM + 96
S_SHORT = S_CONV + 12
S_BIAS = S_SHORT + 72
S_COLS = S_BIAS + 8


def first_pass(layer, block, stream):
    return PASSES.index((layer, block, 0, stream))


def pass_step(layer, block):
    return 2 if layer == 0 and block < DUAL else 1


def turns_of(f):
    i = 0
    while i < FH:
        end = LOOPS[f].get(i)
        yield i, end
        i = end or i + 1


def mod_column(layer, block, stream, m):
    return 4 * PASSES.index((layer, block, m // 4, stream)) + m % 4


def mod_count(layer, block, stream):
    t = PASSES.index((layer, block, 1, stream))
    return t // 2 + 1 if t < T_AHEAD else AHEAD + sum(t >= t0 for t0 in JOB_T[:3])


def program(nc, wstream, wmod, cvec_in, bmod, small, x_in, ctx_in, rpb, mask_in, ident_in, turn_in, zfeat, fw1, fw2,
            fw3, fw4, fcols, window_in, dft_in, out):
    with ExitStack() as ctx:
        def sb(name, shape, dt=F32):
            return ctx.enter_context(nc.sbuf_tensor(name, shape, dt))

        def ps(name, shape):
            return ctx.enter_context(nc.psum_tensor(name, shape, F32))

        def sem(name):
            return ctx.enter_context(nc.semaphore(name))

        raw = sb("raw", [P, RAW, UNIT])
        whi = sb("whi", [P, RING, UNIT], F32R)
        wlo = sb("wlo", [P, RING, UNIT], F32R)
        wm = sb("wm", [P, 8, 512])
        part = sb("part", [P, 512])
        total_hi = sb("total_hi", [P, 512], F32R)
        total_lo = sb("total_lo", [P, 512], F32R)
        cvec = sb("cvec", [P, KT, 2])
        bm = sb("bm", [P, len(PASSES) * 4])
        mod = sb("mod", [P, len(PASSES) * 4])
        row_sb = sb("row_sb", [WIDE, 512])
        one_in = sb("one_in", [P, 2 * WIDE - 1])
        hot = sb("hot", [P, WIDE], F32R)
        sm = sb("sm", [P, S_COLS])
        coef = sb("coef", [P, len(NORMS), KT])
        x_lat = sb("x_lat", [P, KT, T])
        h_hi = [sb("h_lat_hi", [P, KT, T], F32R), sb("h_ctx_hi", [P, KT, T], F32R)]
        h_lo = [sb("h_lat_lo", [P, KT, T], F32R), sb("h_ctx_lo", [P, KT, T], F32R)]
        m_hi, m_lo = h_hi[CTX], h_lo[CTX]
        sq = sb("sq", [P, KT, T])
        z = sb("z", [P, KT, T])
        root = sb("root", [P, T])
        rstd = sb("rstd", [P, T])
        gated = sb("gated", [P, 2, T])
        act = sb("act", [P, 2, T])
        act_hi = sb("act_hi", [P, 2, T], F32R)
        act_lo = sb("act_lo", [P, 2, T], F32R)
        mean_mat = sb("mean_mat", [P, P])
        eps = sb("eps", [P, 1])
        ident = sb("ident", [P, P])
        turn = sb("turn", [P, P])
        mask = sb("mask", [P, GRID_W])
        area = sb("area", [P, 13312])
        at = [0]

        def take(*shape):
            n = int(np.prod(shape))
            v = area[:, at[0]:at[0] + n]
            at[0] += n
            assert at[0] <= 13312
            letters = "abc"[:len(shape)]
            if len(shape) == 1:
                return v
            return v.rearrange(f"p ({' '.join(letters)}) -> p {' '.join(letters)}",
                               **{c: s for c, s in zip(letters, shape)})

        x_ctx = take(KT, T)
        act_ctx = take(FT, T)
        wm_alt = act_ctx[:, 0:16, :].rearrange("p a b -> p (a b)").rearrange("p (k n) -> p k n", n=512)
        at[0] = KT * T
        bias = take(4, 2, T)
        q_t = take(4, T)
        k_t = take(4, 2 * T)
        v_n = take(4, 512)
        conv_b = take(4, T)
        prob = take(4, 2 * T)
        gates = take(3, T)
        prod = take(1, T)
        at[0] -= 4 * T
        prob_t = [take(4, T), x_ctx[:, 0:4, :]]
        at[0] = 0
        k_re = take(2, D)
        k_s = take(2, D)
        y_f = take(4, D)
        dft = take(8, T)
        x0 = take(KT, T)
        conv = take(4, T)
        k_nyq = [part, row_sb]
        sin_a = x0[:, 0, :]
        sin_k = x0[:, 1, :]
        sin_r = x0[:, 2, :]
        hid = x0[:, 3, :]
        zf = x0[:, 4, :]
        fw = x0[:, 5, :]
        fc = x0[:, 6, 0:4]
        p_f = y_f[:, 0:2, :]
        m_f = y_f[:, 2:4, :]
        w4 = k_re[:, :, :].rearrange("p a b -> p (a b)")
        window = k_s
        u_t = z
        u_n = sq[:, :, :].rearrange("p a b -> p (a b)").rearrange("p (a b) -> p a b", a=2)

        scrap = sb("scrap", [P, 12])
        stats = sb("stats", [P, 4, 4])

        acc = ps("acc", [P, 4, 512])
        gu = ps("gu", [P, 2, 512])
        job_p = ps("job_p", [P, 512])
        mean_p = ps("mean_p", [P, 512])

        def region(i):
            return gu[:, i % 2, 0:T]

        def acc_tile(m):
            return acc[:, m // 2, (m % 2) * T:(m % 2) * T + T]

        def scaled(q):
            return sq if q == 1 else z

        def product_b(i):
            return wm[:, 2 * i:2 * i + 2, :]

        def tap_buffer(idx):
            return conv[:, idx % 4, :] if idx < 16 else x0[:, idx - 16, :]

        def spectrum_bank(i):
            return [gu[:, 0, :], gu[:, 1, :], job_p[:, :]][i % 3]

        def scores(i):
            return [gu[:, 0, :], gu[:, 1, :], job_p[:, :], mean_p[:, :]][i % 4]

        landed = [sem(f"unit_landed{i}") for i in range(RAW)]
        hi_done, lo_done, pe_done = sem("hi_done"), sem("lo_done"), sem("pe_done")
        wm_landed = [sem("wm_landed0"), sem("wm_landed1")]
        gemv, colsum, mod_ready = sem("gemv_step"), sem("colsum_done"), sem("mod_ready")
        const_in, x_landed, ctx_landed, bias_in = sem("const_in"), sem("x_landed"), sem("ctx_landed"), [sem(f"bias_in{i}") for i in range(4)]
        filt_in, dft_landed = sem("filt_in"), sem("dft_landed")
        made = sem("constants_made")
        c_landed = sem("c_landed")
        alt_landed = [sem("wm_alt_landed0"), sem("wm_alt_landed1")]
        wm_used, row_out, cols_done = sem("wm_used"), sem("row_out"), sem("cols_done")
        weighed = sem("weighed")
        total_split, total_done = sem("total_hi_done"), sem("total_lo_done")
        lat_pair, y_copied = sem("latent_pair_done"), sem("y_copied")
        cs_ready = sem("cs_ready")
        sq_done, sum_done, root_done = sem("sq_done"), sem("sum_done"), sem("root_done")
        coef_done, rstd_done, z_done, x_upd = sem("coef_done"), sem("rstd_done"), sem("z_done"), sem("x_updated")
        hf_done, hh_done, h_ready = sem("hf_done"), sem("hh_done"), sem("h_ready")
        silu_done, act_mul, act_hi_done, act_lo_done = sem("silu_done"), sem("act_mul"), sem("act_hi_done"), sem("act_lo_done")
        proj_out, conv_step = sem("proj_out"), sem("conv_step")
        s_done, s_max, p_exp, p_norm = sem("s_done"), sem("s_max"), sem("p_exp"), sem("p_norm")
        soft_step = sem("soft_step")
        pt_done, pt_out, pv_done = sem("pt_done"), sem("pt_out"), sem("pv_done")
        masked = sem("masked")
        m_half, m_ready = sem("m_hi_done"), sem("m_ready")
        hy_act, hy_step, u_ready = sem("hy_act"), sem("hy_step"), sem("u_ready")
        fp, fa, fd = sem("filter_pe"), sem("filter_act"), sem("filter_dve")
        tr_done, un_out, uf_done, yf_step = sem("tr_done"), sem("un_out"), sem("uf_done"), sem("yf_step")
        yf_sum = sem("yf_sum")
        inv_done, inv_step = sem("inv_done"), sem("inv_step")
        stored = sem("stored")

        X = [x_lat, x_ctx]

        block = ctx.enter_context(nc.Block())

        @block.sync
        def _(sp):
            def load(u, phase):
                sp.dma_start(raw[:, phase % RAW, :],
                             wstream[u] if isinstance(u, int) else
                             wstream[bass.ds(u, 1)].rearrange("a p n -> p (a n)")).then_inc(landed[phase % RAW], 16)

            sp.dma_start(cvec[:, :, :], cvec_in).then_inc(c_landed, 16)
            sp.dma_start(sm[:, :], small).then_inc(const_in, 16)
            sp.dma_start(bm[:, :], bmod).then_inc(const_in, 16)
            sp.dma_start(ident[:, :], ident_in).then_inc(const_in, 16)
            sp.dma_start(turn[:, :], turn_in).then_inc(const_in, 16)
            sp.dma_start(mask[:, :], mask_in).then_inc(const_in, 16)
            sp.wait_ge(wm_landed[0], 32)
            sp.dma_start(x_lat[:, :, :], x_in).then_inc(x_landed, 16)
            sp.dma_start(x_ctx, ctx_in).then_inc(ctx_landed, 16)
            sp.wait_ge(wm_landed[0], 64)
            for u in range(RAW):
                load(u, u)
            for u in range(RAW, RING):
                sp.wait_ge(lo_done, u - RAW + 1)
                load(u, u)
            turns = UNITS // RING
            with sp.Fori(1, turns) as i:
                for k in range(RING):
                    sp.wait_ge(lo_done, i * RING + (k - RAW + 1))
                    load(i * RING + k, k)
            for u in range(turns * RING, UNITS):
                sp.wait_ge(lo_done, u - RAW + 1)
                load(u, u)
            for c in range(4):
                sp.wait_ge(x_upd, 4 * 6 + c + 1)
                sp.dma_start(out[:, 2 * c:2 * c + 2, :], x_lat[:, 2 * c:2 * c + 2, :]).then_inc(stored, 16)
            sp.wait_ge(stored, 64)

        @block.gpsimd
        def _(pool):
            def load_job(l, used=None, count=None, dst=wm, sems=wm_landed):
                for part_ in range(4):
                    if used is not None:
                        pool.wait_ge(used, count(part_))
                    src = wmod[l] if isinstance(l, int) else wmod[bass.ds(l, 1)].rearrange("a p k n -> p (a k) n")
                    pool.dma_start(dst[:, 2 * part_:2 * part_ + 2, :],
                                   src[:, 2 * part_:2 * part_ + 2, :]).then_inc(sems[part_ // 2], 16)

            def steps_before(l):
                return lambda part_: l * 8 + (10 + 2 * part_)

            def load_bias(h):
                if h >= 4:
                    pool.wait_ge(p_exp, 2 * (h - 4) + 2)
                for r in range(ROWS):
                    src = bass.AP(rpb.tensor, rpb.offset + (h * 15 + 7 - r) * 127,
                                  [[1, GRID_W], [127, ROWS], [1, GRID_W]])
                    q0 = (r % 2) * GRID_W
                    dst = bias[q0:q0 + GRID_W, h % 4, r // 2, :].rearrange("p (y k) -> p y k", y=ROWS)
                    pool.dma_start(dst, src).then_inc(bias_in[h % 4], 16)

            def mask_bias(h):
                pool.wait_ge(bias_in[h % 4], 64 * (h // 4 + 1))
                v = bias[:, h % 4, :, :].rearrange("p t (y k) -> p (t y) k", y=ROWS)
                nc.gpsimd.tensor_tensor(v, v, mask[:, :].unsqueeze(1).to_broadcast([P, 2 * ROWS, GRID_W]),
                                        ALU.add).then_inc(masked, 1)

            load_job(0)
            load_job(1, dst=wm_alt, sems=alt_landed)
            load_job(2, wm_used, lambda part_: 1 + part_ // 2)
            load_job(3, wm_used, lambda part_: 3 + part_ // 2, wm_alt, alt_landed)
            load_job(AHEAD, wm_used, lambda part_: 5 + part_ // 2)
            with pool.Fori(1, DUAL_TURNS) as i:
                load_job(i + AHEAD, gemv, lambda part_: i * 16 + (2 * part_ - 6))
            with pool.Fori(AHEAD + DUAL_TURNS, JOB_L[1] + 1) as l:
                load_job(l, gemv, steps_before(l))
            pool.wait_ge(const_in, 16 * 5)
            pool.wait_ge(pe_done, U_AB)
            for h in range(4):
                load_bias(h)
            for h in range(4):
                mask_bias(h)
            for h in range(4, HEADS):
                load_bias(h)
                mask_bias(h)
            pool.wait_ge(x_upd, 4 * 3)
            pool.dma_start(zf[0:HY_EMB, :], zfeat).then_inc(filt_in, 16)
            pool.dma_start(fw[0:HY_EMB, 0:64], fw1).then_inc(filt_in, 16)
            pool.dma_start(fw[0:HY_FFN, 64:128], fw2).then_inc(filt_in, 16)
            pool.dma_start(fw[0:HY_FFN, 128:192], fw3).then_inc(filt_in, 16)
            pool.dma_start(fc[0:HY_FFN, :], fcols).then_inc(filt_in, 16)
            pool.dma_start(dft, dft_in).then_inc(dft_landed, 16)
            pool.dma_start(w4[0:HY_FFN, :], fw4).then_inc(filt_in, 16)
            pool.dma_start(window, window_in).then_inc(filt_in, 16)
            with pool.Fori(JOB_L[1] + 1, len(LOADS)) as l:
                load_job(l, gemv, steps_before(l))

            for g in range(2):
                cols = slice(g * 512, g * 512 + 512)
                for i, op in enumerate((ALU.subtract, ALU.add)):
                    pool.wait_ge(yf_step, 5 * g + i + 3)
                    dst = y_f[:, 2 * i:2 * i + 2, cols]
                    nc.gpsimd.tensor_tensor(dst, dst, product_b(i), op).then_inc(yf_sum, 1)

        @block.scalar
        def _(a):
            def split_hi(u, phase, first=False):
                turn = u * 16 if isinstance(u, int) else None
                if isinstance(u, int):
                    a.wait_ge(landed[u % RAW], 16 * (u // RAW + 1))
                else:
                    base, i = u.base, u.i
                    a.wait_ge(landed[base % RAW], i * 32 + 16 * (base // RAW + 1))
                if not first:
                    a.wait_ge(pe_done, at_unit(u, -RING + 1))
                nc.scalar.activation(whi[:, phase % RING, :], raw[:, phase % RAW, :], ACT.Copy).then_inc(hi_done, 1)

            def split(u):
                if u.base < UNITS or u.i is not None:
                    if u.i is None and u.base >= UNITS:
                        return
                    split_hi(u if u.i is not None else u.base, u.base)

            def load_table(func):
                i = tables[0]
                tables[0] += 1
                nc.scalar.activation(scrap[:, i:i + 1], eps[:, 0:1], func)

            tables = [0]

            def squares(q, chunks=range(4)):
                kind, _, stream, *_ = NORMS[q]
                if 0 in chunks:
                    if q:
                        a.wait_ge(sum_done, q)
                    if kind == POST and q != 2:
                        a.wait_ge(pe_done, NORM_UNIT[q])
                    elif q == 0:
                        a.wait_ge(x_landed, 16)
                    elif q == 1:
                        a.wait_ge(ctx_landed, 16)
                for c in chunks:
                    if kind == PRE and q > 1:
                        a.wait_ge(x_upd, 4 * NTH[q - 1] + c + 1)
                    src = acc[:, c, :] if kind == POST else X[stream][:, 2 * c:2 * c + 2, :]
                    dst = sq[:, 2 * c:2 * c + 2, :]
                    if q == 2:
                        a.wait_ge(y_copied, c + 1)
                        src = z[:, 2 * c:2 * c + 2, :]
                    elif kind == POST:
                        dst = dst.rearrange("p a b -> p (a b)")
                    nc.scalar.activation(dst, src, ACT.Square).then_inc(sq_done, 1)

            def roots(q):
                a.wait_ge(sum_done, q + 1)
                if q:
                    a.wait_ge(rstd_done, q)
                nc.scalar.activation(root[:, :], mean_p[:, 0:T], ACT.Sqrt, bias=eps[:, 0:1]).then_inc(root_done, 1)

            def weigh(q, chunks=range(4)):
                kind, _, stream, *_ = NORMS[q]
                a.wait_ge(coef_done, q + 1)
                for c in chunks:
                    if kind == POST:
                        a.wait_ge(h_ready, 4 * (NTH[q - 1] + 1))
                    else:
                        a.wait_ge(x_upd, 4 * NTH[q - 1] + c + 1)
                    for m in (2 * c, 2 * c + 1):
                        ins = nc.scalar.activation(z[:, m, :], acc_tile(m) if kind == POST else X[stream][:, m, :],
                                                   ACT.Copy, scale=coef[:, q, m:m + 1])
                    ins.then_inc(weighed, 1)

            def h_his(q, chunks=range(4)):
                p = NTH[q]
                _, layer, stream, _, shift, _ = NORMS[q]
                for c in chunks:
                    if q >= LATE:
                        a.wait_ge(z_done, 4 * q + c + 1)
                        for m in (2 * c, 2 * c + 1):
                            col = mod_column(layer, shift, stream, m)
                            ins = nc.scalar.activation(h_hi[stream][:, m, :], z[:, m, :], ACT.Identity,
                                                       bias=mod[:, col:col + 1])
                        ins.then_inc(hh_done, 1)
                        continue
                    a.wait_ge(hf_done, 8 * p + 2 * c + 2)
                    nc.scalar.activation(h_hi[stream][:, 2 * c:2 * c + 2, :], scaled(q)[:, 2 * c:2 * c + 2, :],
                                         ACT.Copy).then_inc(hh_done, 1)

            def squares_weighed(q):
                for c in range(4):
                    squares(q, (c,))
                    weigh(q, (c,))

            def norm_parts(qs, at):
                for q in qs:
                    plan = BESIDE[q]
                    if plan["root"] == at:
                        roots(q)
                    for c in range(4):
                        if q == 4 and plan["weigh"][c] == at:
                            weigh(q, (c,))
                    for c in range(4):
                        if q in (2, 4) and plan["squares"][c] == at:
                            squares(q + 1, (c,))
                            weigh(q + 1, (c,))
                        if q in (3, 5) and plan["hi"][c] == at:
                            h_his(q, (c,))

            def job_hi(t):
                a.wait_ge(gemv, t * 8 + (8 - 8 * T_AHEAD))
                if not (isinstance(t, int) and t == T_AHEAD):
                    a.wait_ge(colsum, t - T_AHEAD)
                nc.scalar.activation(total_hi[:, :], part[:, :], ACT.Copy).then_inc(total_split, 1)

            def gate_silu(n, s):
                nc.scalar.activation(gated[:, s, :], gu[:, s, 0:T], ACT.Silu).then_inc(silu_done, 1)

            def act_his(n, s):
                a.wait_ge(act_mul, n + 1)
                nc.scalar.activation(act_hi[:, s, :], act[:, s, :], ACT.Copy).then_inc(act_hi_done, 1)

            def ffn_turn(u, n, both=False, ft=None, between={}, last=False, t=None):
                def latent(s):
                    a.wait_ge(lat_pair, ft + (s + 1))
                    gate_silu(n + 2 * s, 0)
                    act_his(n + 2 * s, s)

                first = both and isinstance(n, int) and n == 0
                for k in range(6):
                    s = (k // 2) % 2
                    if k == 0 and first:
                        latent(0)
                    if k in (1, 3):
                        if both:
                            if not (k == 1 and first):
                                latent(s)
                            a.wait_ge(pe_done, at_unit(u, k + 1))
                            gate_silu(n + (2 * s + 1), 1)
                        else:
                            a.wait_ge(pe_done, at_unit(u, k + 1))
                            gate_silu(n + s, s)
                            act_his(n + s, s)
                    if not (last and k == 5):
                        split(u.plus(k + RING))
                    if t is not None and both and k in (1, 4):
                        job_hi(t if k == 1 else t + 1)
                    if t is not None and not both and k == 3:
                        job_hi(t)
                    if k in between:
                        between[k]()

            def ffn(f, peeled={}):
                t0, jobs = JOB_T[f], JOB_TURNS[f]
                for i, end in turns_of(f):
                    if end is None:
                        ffn_turn(Unit(U_FFN[f] + 6 * i), PAIR0[f] + 2 * i, between=peeled.get(i, {}), last=i == FH - 1,
                                 t=t0 + i if i < jobs else None)
                    else:
                        with a.Fori(i, end) as j:
                            ffn_turn(Unit(U_FFN[f], j), j * 2 + PAIR0[f], t=j + t0 if i < jobs else None)

            def row(l):
                a.wait_ge(wm_used, 2 * l + 2)
                if l:
                    a.wait_ge(cols_done, l)
                nc.scalar.activation(row_sb[0:2, :], [job_p, gu[:, 0, :]][l % 2][0:2, :], ACT.Copy).then_inc(row_out, 1)

            def batch_rows(b):
                a.wait_ge(colsum, JOB_T[b + 1] - T_AHEAD)
                a.wait_ge(cols_done, AHEAD + b)
                nc.scalar.activation(row_sb[:, :], job_p[0:WIDE, :], ACT.Copy).then_inc(row_out, 1)

            a.wait_ge(c_landed, 16)
            nc.scalar.activation(cvec[:, :, :], cvec[:, :, :], ACT.Silu).then_inc(cs_ready, 1)
            squares(0)
            a.wait_ge(const_in, 16 * 5)
            a.wait_ge(made, 4)
            row(0)
            roots(0)
            squares(1)
            row(1)
            roots(1)
            row(2)
            for u in range(RAW):
                split_hi(u, u, first=True)
            row(3)
            h_his(0)
            split_hi(RAW, RAW, first=True)
            h_his(1)
            load_table(ACT.Silu)
            for u in range(RAW + 1, RING):
                split_hi(u, u, first=True)
            for i, end in turns_of(0):
                if end is None:
                    ffn_turn(Unit(6 * i), 4 * i, True, 2 * i, t=T_AHEAD + 2 * i)
                else:
                    with a.Fori(i, end) as j:
                        ffn_turn(Unit(0, j), j * 4, True, j * 2, t=j * 2 + T_AHEAD)

            def context_his(ft, s, u):
                a.wait_ge(pe_done, at_unit(u, -1))
                src = act_ctx[:, ft, :] if isinstance(ft, int) else act_ctx[:, bass.ds(ft, 1), :].rearrange("p a b -> p (a b)")
                nc.scalar.activation(act_hi[:, s, :], src, ACT.Copy).then_inc(act_hi_done, 1)

            a.wait_ge(act_mul, 2 * FT)
            context_his(0, 0, Unit(U_CD))
            context_his(1, 1, Unit(U_CD + 1))
            load_table(ACT.Sqrt)
            squares(2)
            batch_rows(0)
            for ft in range(FT):
                if ft + 2 < FT:
                    context_his(ft + 2, ft % 2, Unit(U_CD + ft + 2))
                split(Unit(U_CD + ft + RING))
                norm_parts((2, 3), ft)
            squares(4)

            def take_out(idx):
                a.wait_ge(pe_done, U_AB + idx + 1)
                if idx < 4:
                    ins = nc.scalar.activation(q_t[:, idx, :], region(idx), ACT.Copy, scale=DH ** -0.5)
                elif idx < 16:
                    if idx >= 7:
                        a.wait_ge(conv_step, 5 * ((idx - 4) // 3))
                    ins = nc.scalar.activation(gates[:, (idx - 4) % 3, :], region(idx), ACT.Copy)
                else:
                    ins = nc.scalar.activation(k_t[:, idx - 16, :], gu[:, idx % 2, :], ACT.Copy)
                ins.then_inc(proj_out, 1)

            for idx in range(20):
                take_out(idx)
                split(Unit(U_AB + idx + RING))
                norm_parts((4, 5), idx)

            def exps(h):
                for t in range(2):
                    i = 2 * h + t
                    a.wait_ge(s_max, i + 1)
                    if h >= 2:
                        a.wait_ge(pt_done, i - 3)
                    nc.scalar.activation(prob[:, i % 4, :], scores(i), ACT.Exp, bias=stats[:, i % 4, 1:2],
                                         accum_out=stats[:, i % 4, 2:3]).then_inc(p_exp, 1)

            load_table(ACT.Exp)
            split(Unit(U_AB + 20 + RING))
            exps(0)
            split(Unit(U_AB + 21 + RING))
            exps(1)
            split(Unit(U_AB + 22 + RING))
            split(Unit(U_AB + 23 + RING))
            a.wait_ge(pe_done, U_AB + 24)
            for t in range(4):
                nc.scalar.activation(v_n[:, t, :], acc[:, t, :], ACT.Copy).then_inc(proj_out, 1)

            for h in range(HEADS):
                for t in range(2):
                    i = 2 * h + t
                    a.wait_ge(pt_done, i + 1)
                    if h >= 2:
                        a.wait_ge(pv_done, h - 1)
                    nc.scalar.activation(prob_t[h % 2][:, :, t * P:(t + 1) * P],
                                         acc[:, t, :].rearrange("p (k q) -> p k q", k=4),
                                         ACT.Copy).then_inc(pt_out, 1)
                if h + 2 < HEADS:
                    exps(h + 2)
                if h == 0:
                    for c in range(4):
                        a.wait_ge(conv_step, 5 * (c + 1))
                        nc.scalar.activation(m_hi[:, 4 + c, :], conv_b[:, c, :], ACT.Copy).then_inc(m_half, 1)
            for c in range(7):
                a.wait_ge(pe_done, U_ABO + c + 1)
                split(Unit(U_ABO + c + RING))
            load_table(ACT.Sqrt)
            squares(6)
            split(Unit(U_ABO + 7 + RING))
            roots(6)
            squares_weighed(7)
            roots(7)
            h_his(7)
            load_table(ACT.Silu)
            ffn(1)
            load_table(ACT.Sqrt)
            squares(8)
            batch_rows(1)
            split(Unit(U_FFN[2] + 5))
            roots(8)
            squares_weighed(9)
            roots(9)
            h_his(9)
            load_table(ACT.Silu)
            def sine(l):
                a.wait_ge(fd, FD_SIN[l])
                nc.scalar.activation(hid[0:HY_FFN, :], sin_r[0:HY_FFN, :], ACT.Sin).then_inc(fa, 1)

            def spectrum_out(i):
                half, what, w = SPECTRUM[i]
                cols = slice(half * 512, half * 512 + 512)
                a.wait_ge(fp, FP_DFT + i + 1)
                if what == "nyquist":
                    ins = nc.scalar.activation(k_nyq[half][0:1, :], spectrum_bank(i)[0:1, :], ACT.Copy)
                else:
                    ins = nc.scalar.activation((k_re if what == "re" else k_s)[:, w, cols], spectrum_bank(i), ACT.Copy)
                ins.then_inc(fa, 1)

            ffn(2, peeled=at_steps([BATCH_AT] + FILTER_AT, [lambda: batch_rows(2)] + [lambda l=l: sine(l) for l in range(3)]))
            load_table(ACT.Sqrt)
            squares(10)
            split(Unit(U_HY + 5))
            roots(10)
            for i in range(5):
                spectrum_out(i)
            squares_weighed(11)
            roots(11)
            spectrum_out(5)
            spectrum_out(6)
            h_his(11, (0, 1))
            spectrum_out(7)
            h_his(11, (2, 3))
            spectrum_out(8)
            spectrum_out(9)


            for idx in range(24):
                j = hy_tile(idx)
                a.wait_ge(pe_done, U_HY + idx + 1)
                if 4 <= idx < 16:
                    a.wait_ge(hy_step, HY_STEPS(idx - 3 if idx % 2 == 0 else idx - 4))
                nc.scalar.activation(tap_buffer(idx), region(idx), ACT.Copy,
                                     scale=sm[:, S_SHORT + 24 + j:S_SHORT + 25 + j]).then_inc(hy_act, 1)
                split(Unit(U_HY + idx + RING))
                if idx in (TR_AT[0] + 1, TR_AT[1] + 1):
                    g = (TR_AT[0] + 1, TR_AT[1] + 1).index(idx)
                    a.wait_ge(tr_done, g + 1)
                    nc.scalar.activation(u_n[:, 0, g * 512:g * 512 + 512], job_p[:, :], ACT.Copy).then_inc(un_out, 1)
                    nc.scalar.activation(u_n[:, 1, g * 512:g * 512 + 512], mean_p[:, :], ACT.Copy).then_inc(un_out, 1)
            for c in range(KT):
                a.wait_ge(inv_step, 2 * c + 2)
                nc.scalar.activation(m_hi[:, c, :], conv[:, c % 4, :], ACT.Copy).then_inc(m_half, 1)
            for c in range(7):
                a.wait_ge(pe_done, U_HYO + c + 1)
                split(Unit(U_HYO + c + RING))
            load_table(ACT.Sqrt)
            squares(12)
            split(Unit(U_HYO + 7 + RING))
            roots(12)
            squares_weighed(13)
            roots(13)
            h_his(13)
            load_table(ACT.Silu)
            ffn(3)
            load_table(ACT.Sqrt)
            squares(14)
            roots(14)

        @block.vector
        def _(v):
            def split(u):
                if u.i is None and u.base >= UNITS:
                    return
                v.wait_ge(hi_done, at_unit(u, 1))
                nc.vector.tensor_tensor(wlo[:, u.base % RING, :], raw[:, u.base % RAW, :],
                                        whi[:, u.base % RING, :].bitcast(F32), ALU.subtract).then_inc(lo_done, 1)

            def job_ops(t, landed_, kts, stream=LAT):
                for kt in kts:
                    if kt in (0, 4) and landed_ is not None:
                        v.wait_ge(wm_landed[kt // 4], landed_)
                    fixed = isinstance(t, int)
                    if not (fixed and t == T_AHEAD and kt == 0):
                        v.wait_ge(gemv, t * 8 + (kt - 8 * T_AHEAD))
                    c = cvec[:, kt, stream:stream + 1]
                    if kt == 0:
                        if not (fixed and t == T_AHEAD):
                            v.wait_ge(total_done, t - T_AHEAD)
                        ins = nc.vector.tensor_scalar(part[:, :], wm[:, kt, :], c, None, ALU.mult)
                    else:
                        ins = nc.vector.scalar_tensor_tensor(out=part[:, :], in0=wm[:, kt, :], scalar=c,
                                                             in1=part[:, :], op0=ALU.mult, op1=ALU.add)
                    ins.then_inc(gemv, 1)

            def job_lo(t, row_):
                v.wait_ge(total_split, t + (1 - T_AHEAD))
                nc.vector.tensor_copy(hot[:, :], one_in[:, row_:row_ + WIDE] if isinstance(row_, int)
                                      else one_in[:, bass.ds(row_, WIDE)])
                nc.vector.tensor_tensor(total_lo[:, :], part[:, :], total_hi[:, :].bitcast(F32),
                                        ALU.subtract).then_inc(total_done, 1)

            def ahead_out(l):
                v.wait_ge(cols_done, l + 1)
                v.wait_ge(const_in, 16 * 5)
                nc.vector.tensor_tensor(mod[:, 8 * l:8 * l + 8].rearrange("p (s i) -> p s i", s=2),
                                        gu[:, 1, 0:8].rearrange("p (i s) -> p s i", s=2),
                                        bm[:, 8 * l:8 * l + 8].rearrange("p (s i) -> p s i", s=2),
                                        ALU.add).then_inc(mod_ready, 1)

            def batch_out(b):
                t, n = JOB_T[b], JOB_T[b + 1] - JOB_T[b]
                v.wait_ge(cols_done, AHEAD + b + 1)
                nc.vector.tensor_tensor(mod[:, 4 * t:4 * (t + n)].rearrange("p (t i) -> p t i", i=4),
                                        job_p[:, 0:4 * n].rearrange("p (i t) -> p t i", i=4),
                                        bm[:, 4 * t:4 * (t + n)].rearrange("p (t i) -> p t i", i=4),
                                        ALU.add).then_inc(mod_ready, 1)

            def norm_coef(q):
                kind, layer, stream, g, b0, b1 = NORMS[q]
                gain = sm[:, S_NORM + (layer * 6 + g) * 8:S_NORM + (layer * 6 + g) * 8 + 8]
                block_ = b0 if kind == POST else b1
                v.wait_ge(mod_ready, mod_count(layer, block_, stream))
                scalar, op = (b1, ALU.mult) if kind == POST else (1.0, ALU.add)
                t, n = first_pass(layer, block_, stream), pass_step(layer, block_)
                cols = mod[:, 4 * t:4 * t + 4 * n + 4].rearrange("p (a b) -> p a b", b=4)[:, ::n, :]
                nc.vector.scalar_tensor_tensor(out=coef[:, q, :].rearrange("p (a b) -> p a b", a=2), in0=cols,
                                               scalar=scalar, in1=gain.rearrange("p (a b) -> p a b", a=2),
                                               op0=op, op1=ALU.mult).then_inc(coef_done, 1)

            def reciprocal(q):
                v.wait_ge(root_done, q + 1)
                if q:
                    v.wait_ge(z_done, 4 * q)
                nc.vector.reciprocal(rstd[:, :], root[:, :]).then_inc(rstd_done, 1)

            def scale(q, c):
                v.wait_ge(rstd_done, q + 1)
                dst = src = scaled(q)[:, 2 * c:2 * c + 2, :]
                if q < 2:
                    src = X[NORMS[q][2]][:, 2 * c:2 * c + 2, :]
                elif q == 2:
                    v.wait_ge(y_copied, c + 1)
                else:
                    v.wait_ge(weighed, 4 * (q - LATE) + c + 1)
                nc.vector.tensor_tensor(dst, src, rstd[:, :].unsqueeze(1).to_broadcast([P, 2, T]),
                                        ALU.mult).then_inc(z_done, 1)

            def weigh(q, c):
                v.wait_ge(coef_done, q + 1)
                v.wait_ge(sq_done, 4 * q + c + 1)
                for m in (2 * c, 2 * c + 1):
                    ins = nc.vector.tensor_scalar(z[:, m, :], acc_tile(m), coef[:, q, m:m + 1], None, ALU.mult)
                ins.then_inc(weighed, 1)

            def add(q, c):
                v.wait_ge(z_done, 4 * q + c + 1)
                x_ = X[NORMS[q][2]]
                if q >= LATE:
                    x2 = x_[:, 2 * c:2 * c + 2, :]
                    nc.vector.tensor_tensor(x2, x2, z[:, 2 * c:2 * c + 2, :], ALU.add).then_inc(x_upd, 1)
                    return
                v.wait_ge(coef_done, q + 1)
                for m in (2 * c, 2 * c + 1):
                    ins = nc.vector.scalar_tensor_tensor(out=x_[:, m, :], in0=z[:, m, :], scalar=coef[:, q, m:m + 1],
                                                         in1=x_[:, m, :], op0=ALU.mult, op1=ALU.add)
                ins.then_inc(x_upd, 1)

            def lo(q, c):
                _, layer, stream, _, shift, _ = NORMS[q]
                v.wait_ge(hh_done, 4 * NTH[q] + c + 1)
                v.wait_ge(z_done, 4 * q + c + 1)
                for m in (2 * c, 2 * c + 1):
                    col = mod_column(layer, shift, stream, m)
                    ins = nc.vector.scalar_tensor_tensor(out=h_lo[stream][:, m, :], in0=z[:, m, :],
                                                         scalar=mod[:, col:col + 1], in1=h_hi[stream][:, m, :].bitcast(F32),
                                                         op0=ALU.add, op1=ALU.subtract)
                ins.then_inc(h_ready, 1)

            def norm_parts(qs, at):
                for q in qs:
                    plan = BESIDE[q]
                    if plan["recip"] == at:
                        reciprocal(q)
                    if q in (2, 4) and at == plan["scale"][3]:
                        norm_coef(q + 1)
                    for c in range(4):
                        if q in (3, 5) and plan["lo"][c] == at:
                            lo(q, c)
                    for c in range(4):
                        if plan["scale"][c] == at:
                            scale(q, c)
                    for c in range(4):
                        if q in (2, 4) and plan["add"][c] == at:
                            add(q, c)
                    if q in (3, 5) and plan["lo"][3] == at:
                        norm_coef(q + 1)

            def post(q, between=None, held=None):
                for c in range(4):
                    weigh(q, c)
                if held is not None:
                    split(Unit(held))
                reciprocal(q)
                scale(q, 0)
                scale(q, 1)
                if between:
                    between()
                if q + 1 < len(NORMS):
                    norm_coef(q + 1)
                add(q, 0)
                scale(q, 2)
                add(q, 1)
                scale(q, 3)
                add(q, 2)
                add(q, 3)

            def pre(q):
                reciprocal(q)
                scale(q, 0)
                scale(q, 1)
                lo(q, 0)
                scale(q, 2)
                lo(q, 1)
                scale(q, 3)
                lo(q, 2)
                lo(q, 3)

            def pre_rest(q):
                _, layer, stream, _, shift, _ = NORMS[q]
                p, z = NTH[q], scaled(q)
                v.wait_ge(coef_done, q + 1)
                v.wait_ge(mod_ready, mod_count(layer, shift, stream))

                def affine(c):
                    v.wait_ge(z_done, 4 * q + c + 1)
                    for m in (2 * c, 2 * c + 1):
                        col = mod_column(layer, shift, stream, m)
                        nc.vector.tensor_scalar(z[:, m, :], z[:, m, :], coef[:, q, m:m + 1], mod[:, col:col + 1],
                                                ALU.mult, ALU.add).then_inc(hf_done, 1)

                def rest(c):
                    v.wait_ge(hf_done, 8 * p + 2 * c + 2)
                    v.wait_ge(hh_done, 4 * p + c + 1)
                    nc.vector.tensor_tensor(h_lo[stream][:, 2 * c:2 * c + 2, :], z[:, 2 * c:2 * c + 2, :],
                                            h_hi[stream][:, 2 * c:2 * c + 2, :].bitcast(F32), ALU.subtract).then_inc(h_ready, 1)

                affine(0)
                affine(1)
                rest(0)
                affine(2)
                rest(1)
                affine(3)
                rest(2)
                rest(3)

            def gate_up(n, s, dst):
                v.wait_ge(silu_done, n + 1)
                nc.vector.tensor_tensor(dst, gated[:, s, :], gu[:, s, T:2 * T], ALU.mult).then_inc(act_mul, 1)

            def act_los(n, na, s):
                v.wait_ge(act_hi_done, na + 1)
                v.wait_ge(act_mul, n + 1)
                nc.vector.tensor_tensor(act_lo[:, s, :], act[:, s, :], act_hi[:, s, :].bitcast(F32),
                                        ALU.subtract).then_inc(act_lo_done, 1)

            def ffn_turn(u, n, na, job, between={}, last=False):
                def ops(*kts):
                    if job is not None:
                        job_ops(job[0], job[2], kts)

                for k in range(6):
                    s = (k // 2) % 2
                    if k == 0:
                        ops(0, 1)
                    if k in (1, 3):
                        kt = {1: 2, 3: 5}[k]
                        gate_up(n + s, s, act[:, s, :])
                        ops(kt)
                        act_los(n + s, na + s, s)
                        ops(kt + 1, kt + 2)
                    if k == 4 and job is not None:
                        job_lo(*job[:2])
                    if not (last and k == 5):
                        split(u.plus(k + RING))
                    if k in between:
                        between[k]()

            def ffn(f, peeled={}):
                n0, a0, t0, l0, jobs = PAIR0[f], ACT0[f], JOB_T[f], JOB_L[f], JOB_TURNS[f]

                def job(i):
                    return (i + t0, i, i * 32 + 32 * (l0 - 1))

                for i, end in turns_of(f):
                    if end is None:
                        ffn_turn(Unit(U_FFN[f] + 6 * i), n0 + 2 * i, a0 + 2 * i, job(i) if i < jobs else None,
                                 peeled.get(i, {}), i == FH - 1)
                    else:
                        with v.Fori(i, end) as j:
                            ffn_turn(Unit(U_FFN[f], j), j * 2 + n0, j * 2 + a0, job(j) if i < jobs else None)

            def both_turn(u, n, ft, i, dual):
                t, r = i * 2 + T_AHEAD, i * 2
                if dual:
                    at_a, at_b = i * 32 + 32 * (AHEAD - 1), None
                else:
                    at_a = i * 64 + 32 * (AHEAD + DUAL_TURNS - 2 * DUAL_TURNS - 1)
                    at_b = at_a + 32
                plan = {0: (0, 1, 2, 3), 1: (4, 5, 6, 7), 2: (8, 9, 10, 11), 3: (12, 13, 14), 4: (15,)}

                def op(x):
                    if x < 8:
                        job_ops(t, at_a, (x,))
                    else:
                        job_ops(t + 1, at_b, (x - 8,), CTX if dual else LAT)

                def latent(s, ops):
                    gate_up(n + 2 * s, 0, act[:, s, :])
                    for x in ops[:2]:
                        op(x)
                    act_los(n + 2 * s, ft + s, s)
                    for x in ops[2:]:
                        op(x)

                first = isinstance(i, int) and i == 0
                for k in range(6):
                    s = (k // 2) % 2
                    ops = plan.get(k, ())
                    if k == 0 and first:
                        latent(0, ops)
                    elif k in (1, 3):
                        if not (k == 1 and first):
                            latent(s, ops)
                        dst = act_ctx[:, ft + s, :] if isinstance(ft, int) \
                            else act_ctx[:, bass.ds(ft + s, 1), :].rearrange("p a b -> p (a b)")
                        gate_up(n + (2 * s + 1), 1, dst)
                        if k == 1 and first:
                            for x in ops:
                                op(x)
                    else:
                        if k == 2:
                            job_lo(t, r)
                        for x in ops:
                            op(x)
                    split(u.plus(k + RING))
                    if k == 4:
                        job_lo(t + 1, r + 1)

            nc.vector.memset(mean_mat[:, :], 1.0 / D).then_inc(made, 1)
            nc.vector.memset(one_in[:, :], 0.0).then_inc(made, 1)
            nc.vector.memset(eps[:, :], EPS).then_inc(made, 1)
            v.wait_ge(made, 2)
            nc.vector.memset(one_in[:, WIDE - 1:WIDE], 1.0).then_inc(made, 1)
            v.wait_ge(x_landed, 16)
            reciprocal(0)
            for c in range(4):
                scale(0, c)
            v.wait_ge(ctx_landed, 16)
            reciprocal(1)
            v.wait_ge(sum_done, 2)
            for c in range(4):
                scale(1, c)
            ahead_out(0)
            ahead_out(1)
            for u in range(RAW):
                split(Unit(u))
            ahead_out(2)
            ahead_out(3)
            norm_coef(0)
            norm_coef(1)
            pre_rest(0)
            split(Unit(RAW))
            pre_rest(1)
            for u in range(RAW + 1, RING):
                split(Unit(u))
            v.wait_ge(made, 4)
            v.wait_ge(cs_ready, 1)
            for i, end in turns_of(0):
                if end is None:
                    both_turn(Unit(6 * i), 4 * i, 2 * i, i, i < DUAL_TURNS)
                else:
                    with v.Fori(i, end) as j:
                        both_turn(Unit(0, j), j * 4, j * 2, j, i < DUAL_TURNS)

            def context_los(ft, s):
                v.wait_ge(act_hi_done, ft + (FT + 1))
                src = act_ctx[:, ft, :] if isinstance(ft, int) else act_ctx[:, bass.ds(ft, 1), :].rearrange("p a b -> p (a b)")
                nc.vector.tensor_tensor(act_lo[:, s, :], src, act_hi[:, s, :].bitcast(F32),
                                        ALU.subtract).then_inc(act_lo_done, 1)

            v.wait_ge(act_mul, 2 * FT)
            context_los(0, 0)
            v.wait_ge(pe_done, PER_FFN)
            for c in range(4):
                if c == 2:
                    context_los(1, 1)
                nc.vector.tensor_copy(z[:, 2 * c:2 * c + 2, :].rearrange("p a b -> p (a b)"),
                                      acc[:, c, :]).then_inc(y_copied, 1)
            for ft in range(FT):
                if ft + 2 < FT:
                    context_los(ft + 2, ft % 2)
                split(Unit(U_CD + ft + RING))
                if ft == 1:
                    batch_out(0)
                    norm_coef(2)
                norm_parts((2, 3), ft)

            def short_conv(c):
                n = 5 * c
                v.wait_ge(proj_out, 4 + 3 * c + 3)
                nc.vector.tensor_tensor(prod[:, 0, :], gates[:, 0, :], gates[:, 1, :], ALU.mult).then_inc(conv_step, 1)
                v.wait_ge(conv_step, n + 1)
                w = [sm[:, S_CONV + 4 * i + c:S_CONV + 4 * i + c + 1] for i in range(3)]
                nc.vector.tensor_scalar(conv_b[:, c, :], prod[:, 0, :], w[1], None, ALU.mult).then_inc(conv_step, 1)
                v.wait_ge(conv_step, n + 2)
                nc.vector.scalar_tensor_tensor(out=conv_b[:, c, 1:T], in0=prod[:, 0, 0:T - 1], scalar=w[0],
                                               in1=conv_b[:, c, 1:T], op0=ALU.mult, op1=ALU.add).then_inc(conv_step, 1)
                v.wait_ge(conv_step, n + 3)
                nc.vector.scalar_tensor_tensor(out=conv_b[:, c, 0:T - 1], in0=prod[:, 0, 1:T], scalar=w[2],
                                               in1=conv_b[:, c, 0:T - 1], op0=ALU.mult, op1=ALU.add).then_inc(conv_step, 1)
                v.wait_ge(conv_step, n + 4)
                nc.vector.tensor_tensor(conv_b[:, c, :], conv_b[:, c, :], gates[:, 2, :], ALU.mult).then_inc(conv_step, 1)

            def maxima(h):
                for t in range(2):
                    i, n = 2 * h + t, soft_of(2 * h + t)
                    v.wait_ge(s_done, i + 1)
                    if i >= 4:
                        v.wait_ge(p_norm, i - 3)
                    nc.vector.tensor_reduce(stats[:, i % 4, 0:1], scores(i), AX.X, ALU.max).then_inc(soft_step, 1)
                    v.wait_ge(soft_step, n + 1)
                    nc.vector.tensor_scalar(stats[:, i % 4, 1:2], stats[:, i % 4, 0:1], -1.0, None, ALU.mult).then_inc(s_max, 1)

            def soft_of(i):
                return soft_base[i]

            soft_base, recip_base, n = {}, {}, 0
            for base, h in [(soft_base, 0), (soft_base, 1), (recip_base, 0), (recip_base, 1)] \
                    + [(base, h) for h in range(2, HEADS) for base in (soft_base, recip_base)]:
                for t in range(2):
                    base[2 * h + t] = n
                    n += 1

            def pair_out(pair):
                v.wait_ge(pv_done, 2 * pair + 2)
                o = acc[:, 2 + pair % 2, 0:T]
                nc.vector.tensor_copy(m_hi[:, pair, :], o).then_inc(m_half, 1)
                v.wait_ge(m_half, 4 + pair + 1)
                nc.vector.tensor_tensor(m_lo[:, pair, :], o, m_hi[:, pair, :].bitcast(F32),
                                        ALU.subtract).then_inc(m_ready, 1)

            def normalise(h):
                for t in range(2):
                    i = 2 * h + t
                    v.wait_ge(p_exp, i + 1)
                    nc.vector.reciprocal(stats[:, i % 4, 3:4], stats[:, i % 4, 2:3]).then_inc(soft_step, 1)
                    v.wait_ge(soft_step, recip_base[i] + 1)
                    nc.vector.tensor_scalar(prob[:, i % 4, :], prob[:, i % 4, :], stats[:, i % 4, 3:4], None,
                                            ALU.mult).then_inc(p_norm, 1)

            for idx in range(24):
                if idx >= 6 and idx % 3 == 0 and idx <= 15:
                    short_conv(idx // 3 - 2)
                split(Unit(U_AB + idx + RING))
                norm_parts((4, 5), idx)
                if idx == 20:
                    maxima(0)
                    maxima(1)
                if idx == 21:
                    normalise(0)
                    normalise(1)

            for h in range(2, HEADS):
                maxima(h)
                normalise(h)
                if h == 2:
                    for c in range(4):
                        v.wait_ge(m_half, c + 1)
                        nc.vector.tensor_tensor(m_lo[:, 4 + c, :], conv_b[:, c, :], m_hi[:, 4 + c, :].bitcast(F32),
                                                ALU.subtract).then_inc(m_ready, 1)
                if h % 2 == 0 and h >= 4:
                    pair_out(h // 2 - 2)
            pair_out(HEADS // 2 - 2)
            pair_out(HEADS // 2 - 1)
            for c in range(7):
                split(Unit(U_ABO + c + RING))
            post(6, held=U_ABO + 7 + RING)
            pre(7)
            norm_coef(8)
            ffn(1)
            post(8, lambda: batch_out(1), U_FFN[2] + 5)
            pre(9)

            count = [0]

            def step(ins):
                ins.then_inc(fd, 1)
                count[0] += 1

            def settle():
                v.wait_ge(fd, count[0])

            TWO_PI = 2 * math.pi
            c1 = 6.28125
            c2 = float(np.float32(math.floor((TWO_PI - c1) * 2 ** 21) / 2 ** 21))
            c3 = TWO_PI - c1 - c2
            big = 1.5 * 2 ** 23
            H = slice(0, HY_FFN)

            def sine_argument(l):
                if l == 0:
                    v.wait_ge(filt_in, 16 * 7)
                v.wait_ge(fp, l + 1)
                step(nc.vector.tensor_scalar(sin_a[H, :], mean_p[H, 0:T], fc[H, l:l + 1], fc[H, 3:4], ALU.add, ALU.mult))
                settle()
                step(nc.vector.tensor_scalar(sin_k[H, :], sin_a[H, :], 1 / TWO_PI, big, ALU.mult, ALU.add))
                settle()
                step(nc.vector.tensor_scalar(sin_k[H, :], sin_k[H, :], -big, None, ALU.add))
                settle()
                for c in (c1, c2, c3):
                    step(nc.vector.scalar_tensor_tensor(out=sin_a[H, :], in0=sin_k[H, :], scalar=-c, in1=sin_a[H, :],
                                                        op0=ALU.mult, op1=ALU.add))
                    settle()
                step(nc.vector.tensor_scalar(sin_r[H, :], sin_a[H, :], PI_F, -PI_F, ALU.min, ALU.max))
                assert count[0] == FD_SIN[l]

            def filter_sums(i):
                th, half = i % 2, i // 2
                cols = slice(half * 512, half * 512 + 512)
                v.wait_ge(fp, 3 + i + 1)
                step(nc.vector.tensor_tensor(p_f[:, th, cols], job_p[:, :], window[:, th, cols], ALU.mult))
                step(nc.vector.tensor_tensor(m_f[:, th, cols], mean_p[:, :], window[:, th, cols], ALU.mult))
                settle()
                if th == 0:
                    step(nc.vector.memset(m_f[0:1, th, cols], 0.0))
                    settle()
                step(nc.vector.tensor_tensor(p_f[:, th, cols], p_f[:, th, cols], m_f[:, th, cols], ALU.add))
                settle()
                step(nc.vector.scalar_tensor_tensor(out=m_f[:, th, cols], in0=m_f[:, th, cols], scalar=-2.0,
                                                    in1=p_f[:, th, cols], op0=ALU.mult, op1=ALU.add))
                assert count[0] == FD_SUM[i]

            norm_coef(10)
            ffn(2, peeled=at_steps([BATCH_AT] + FILTER_AT, [lambda: batch_out(2)]
                                   + [lambda l=l: sine_argument(l) for l in range(3)]
                                   + [lambda i=i: filter_sums(i) for i in range(4)]))
            post(10, held=U_HY + 5)
            pre(11)
            norm_coef(12)
            v.wait_ge(fa, 3 + 10)
            step(nc.vector.memset(k_s[0:1, 0, :], 0.0))

            def taps(idx):
                j, n = hy_tile(idx), HY_STEPS(idx - 1) if idx else 0
                w0 = sm[:, S_SHORT + j:S_SHORT + j + 1]
                w2 = sm[:, S_SHORT + 48 + j:S_SHORT + 49 + j]
                c = tap_buffer(idx)
                r = region(idx)
                v.wait_ge(hy_act, idx + 1)
                nc.vector.scalar_tensor_tensor(out=c[:, 1:T], in0=r[:, 0:T - 1], scalar=w0, in1=c[:, 1:T],
                                               op0=ALU.mult, op1=ALU.add).then_inc(hy_step, 1)
                v.wait_ge(hy_step, n + 1)
                nc.vector.scalar_tensor_tensor(out=c[:, 0:T - 1], in0=r[:, 1:T], scalar=w2, in1=c[:, 0:T - 1],
                                               op0=ALU.mult, op1=ALU.add).then_inc(hy_step, 1)
                v.wait_ge(hy_step, n + 2)
                if idx < 16 and idx % 2:
                    nc.vector.tensor_tensor(u_t[:, idx // 2, :], conv[:, (idx - 1) % 4, :], c, ALU.mult).then_inc(hy_step, 1)

            def spectrum_product(g, step_):
                cols = slice(g * 512, g * 512 + 512)
                re, s_ = y_f[:, 0:2, cols], y_f[:, 2:4, cols]
                if step_ in (0, 2):
                    v.wait_ge(uf_done, 2 * g + step_ // 2 + 1)
                if step_ == 4:
                    v.wait_ge(yf_sum, 2 * g + 2)
                    nc.vector.tensor_tensor(y_f[0:1, 2, cols], acc[0:1, 2, :], k_nyq[g][0:1, :], ALU.mult).then_inc(yf_step, 1)
                    return
                dst, banks, k_ = [(re, slice(0, 2), k_re), (s_, slice(0, 2), k_s),
                                  (product_b(0), slice(2, 4), k_s), (product_b(1), slice(2, 4), k_re)][step_]
                nc.vector.tensor_tensor(dst, acc[:, banks, :], k_[:, :, cols], ALU.mult).then_inc(yf_step, 1)

            for idx in range(24):
                taps(idx)
                split(Unit(U_HY + idx + RING))
                if idx == 0:
                    v.wait_ge(fd, count[0])
                for g, step_ in YF_AT.get(idx, ()):
                    spectrum_product(g, step_)
            for c in range(KT):
                for g, step_ in YF_AT.get(24 + c, ()):
                    spectrum_product(g, step_)
                v.wait_ge(inv_done, c + 1)
                b = sm[:, S_BIAS + c:S_BIAS + c + 1]
                if c >= 4:
                    v.wait_ge(m_ready, 8 + c - 3)
                nc.vector.scalar_tensor_tensor(out=conv[:, c % 4, :], in0=u_t[:, c, :], scalar=b, in1=region(c),
                                               op0=ALU.mult, op1=ALU.add).then_inc(inv_step, 1)
                v.wait_ge(inv_step, 2 * c + 1)
                nc.vector.tensor_tensor(conv[:, c % 4, :], conv[:, c % 4, :], x0[:, c, :], ALU.mult).then_inc(inv_step, 1)
                v.wait_ge(m_half, 8 + c + 1)
                nc.vector.tensor_tensor(m_lo[:, c, :], conv[:, c % 4, :], m_hi[:, c, :].bitcast(F32),
                                        ALU.subtract).then_inc(m_ready, 1)
            for c in range(7):
                split(Unit(U_HYO + c + RING))
            post(12, held=U_HYO + 7 + RING)
            pre(13)
            norm_coef(14)
            ffn(3)
            post(14)

        @block.tensor
        def _(pe):
            def product(out_, w_hi, w_lo, x_hi, x_lo, start, stop):
                nc.tensor.matmul(out_, w_hi, x_hi, start=start, stop=False, skip_group_check=True)
                nc.tensor.matmul(out_, w_hi, x_lo, start=False, stop=False, skip_group_check=True)
                return nc.tensor.matmul(out_, w_lo, x_hi, start=False, stop=stop, skip_group_check=True)

            def wblock(u, kt):
                s = u.base % RING
                return whi[:, s, kt * P:(kt + 1) * P], wlo[:, s, kt * P:(kt + 1) * P]

            def column_unit(u, out_, xs, wait_h=None, last=True):
                pe.wait_ge(lo_done, at_unit(u, 1))
                for kt in range(KT):
                    if wait_h is not None and kt % 2 == 0:
                        pe.wait_ge(h_ready, wait_h + kt // 2 + 1)
                    ins = product(out_, *wblock(u, kt), xs[0][:, kt, :], xs[1][:, kt, :], kt == 0, kt == KT - 1)
                if last:
                    ins.then_inc(pe_done, 1)
                return ins

            def job_sum(t, first=False):
                pe.wait_ge(total_done, t + (1 - T_AHEAD))
                nc.tensor.matmul(job_p[0:WIDE, :], hot[:, :], total_hi[:, :], start=first, stop=False,
                                 skip_group_check=True)
                nc.tensor.matmul(job_p[0:WIDE, :], hot[:, :], total_lo[:, :], start=False, stop=True,
                                 skip_group_check=True).then_inc(colsum, 1)

            def batch_columns(b):
                n = JOB_T[b + 1] - JOB_T[b]
                pe.wait_ge(row_out, AHEAD + b + 1)
                for i in range(4):
                    ins = nc.tensor.matmul(job_p[:, i * n:(i + 1) * n], row_sb[:, i * P:(i + 1) * P],
                                           turn[0:WIDE, GRID_W - WIDE:GRID_W - WIDE + n], start=True, stop=True)
                ins.then_inc(cols_done, 1)

            def mean_of(q):
                if q:
                    pe.wait_ge(root_done, q)
                for m in range(KT):
                    if m % 2 == 0:
                        pe.wait_ge(sq_done, 4 * q + m // 2 + 1)
                    ins = nc.tensor.matmul(mean_p[:, 0:T], mean_mat[:, :], sq[:, m, :], start=(m == 0), stop=(m == KT - 1))
                ins.then_inc(sum_done, 1)

            def down(uk, s, first, stop, copied=False):
                pe.wait_ge(lo_done, at_unit(uk, 1))
                for m in range(KT):
                    if copied and m % 2 == 0:
                        pe.wait_ge(y_copied, m // 2 + 1)
                    ins = product(acc_tile(m), *wblock(uk, m), act_hi[:, s, :], act_lo[:, s, :],
                                  first and m % 2 == 0, stop)
                ins.then_inc(pe_done, 1)

            def column_units(us, outs, xs, wait_h):
                for u in us:
                    pe.wait_ge(lo_done, at_unit(u, 1))
                for c in range(KT // 2):
                    pe.wait_ge(h_ready, wait_h + c + 1)
                    for u, (out_, bank_first) in zip(us, outs):
                        for kt in (2 * c, 2 * c + 1):
                            ins = product(out_, *wblock(u, kt), xs[0][:, kt, :], xs[1][:, kt, :],
                                          kt == 0 and bank_first, kt == KT - 1)
                        if c == KT // 2 - 1:
                            ins.then_inc(pe_done, 1)

            def ffn_turn(u, n, na, t, xs, first=False, acc_free=0, wait_h=None, stop=False, between={}):
                if first:
                    pe.wait_ge(act_mul, n - 1)
                    column_units([u, u.plus(1)], [(gu[:, 0, 0:T], True), (gu[:, 0, T:2 * T], False)], xs, wait_h)
                for k in range(2 if first else 0, 6):
                    s = (k // 2) % 2
                    uk = u.plus(k)
                    if k < 4:
                        if k % 2 == 0:
                            pe.wait_ge(act_mul, n + (s - 1))
                        column_unit(uk, gu[:, s, (k % 2) * T:(k % 2) * T + T], xs)
                    else:
                        s = k - 4
                        if first and s == 0:
                            pe.wait_ge(weighed, acc_free)
                        pe.wait_ge(act_lo_done, na + (s + 1))
                        down(uk, s, first and s == 0, stop and s == 1)
                    if k == 5 and t is not None:
                        job_sum(t, first)
                    if k in between:
                        between[k]()

            def ffn(f, p, acc_free, peeled={}):
                xs = (h_hi[LAT], h_lo[LAT])
                n0, a0, t0, u0, jobs = PAIR0[f], ACT0[f], JOB_T[f], U_FFN[f], JOB_TURNS[f]
                for i, end in turns_of(f):
                    if end is None:
                        ffn_turn(Unit(u0 + 6 * i), n0 + 2 * i, a0 + 2 * i, t0 + i if i < jobs else None, xs, i == 0,
                                 acc_free, 4 * p if i == 0 else None, i == FH - 1, peeled.get(i, {}))
                    else:
                        with pe.Fori(i, end) as j:
                            ffn_turn(Unit(u0, j), j * 2 + n0, j * 2 + a0, j + t0 if i < jobs else None, xs)

            def ahead(l):
                src, sems = ((wm, wm_landed), (wm_alt, alt_landed))[l % 2]
                if l >= 2:
                    pe.wait_ge(row_out, l - 1)
                for kt in range(KT):
                    if kt % 4 == 0:
                        pe.wait_ge(sems[kt // 4], 32 * (l // 2 + 1))
                    ins = nc.tensor.matmul([job_p, gu[:, 0, :]][l % 2][0:2, :], cvec[:, kt, :], src[:, kt, :],
                                           start=(kt == 0), stop=(kt == KT - 1))
                    if kt == 3:
                        ins.then_inc(wm_used, 1)
                ins.then_inc(wm_used, 1)

            def ahead_columns(l):
                pe.wait_ge(row_out, l + 1)
                if l == 0:
                    pe.wait_ge(const_in, 16 * 5)
                else:
                    pe.wait_ge(mod_ready, l)
                for i in range(4):
                    ins = nc.tensor.matmul(gu[:, 1, 2 * i:2 * i + 2], row_sb[0:2, i * P:(i + 1) * P], ident[0:2, 0:2],
                                           start=True, stop=True)
                ins.then_inc(cols_done, 1)

            pe.wait_ge(cs_ready, 1)
            ahead(0)
            pe.wait_ge(made, 4)
            mean_of(0)
            ahead(1)
            ahead_columns(0)
            mean_of(1)
            ahead(2)
            ahead_columns(1)
            ahead(3)
            ahead_columns(2)
            ahead_columns(3)

            def both_turn(u, n, ft, i, first=False, stop=False):
                t = i * 2 + T_AHEAD

                def tile(k, stream):
                    s = (k // 2) % 2
                    uk = u.plus(k)
                    if stream == LAT or first:
                        pe.wait_ge(lo_done, at_unit(uk, 1))
                    if k % 2 == 0 and not (first and k == 0):
                        pe.wait_ge(act_mul, n + (2 * s + stream - 1))
                    for kt in range(KT):
                        if first and k == 0 and kt % 2 == 0:
                            pe.wait_ge(h_ready, 4 * stream + kt // 2 + 1)
                        ins = product(gu[:, stream, (k % 2) * T:(k % 2) * T + T], *wblock(uk, kt),
                                      h_hi[stream][:, kt, :], h_lo[stream][:, kt, :], kt == 0, kt == KT - 1)
                    if stream == CTX:
                        ins.then_inc(pe_done, 1)
                    elif k % 2:
                        ins.then_inc(lat_pair, 1)

                start = [(0, LAT), (1, LAT), (0, CTX), (1, CTX)] if first else \
                    [(0, LAT), (0, CTX), (1, LAT), (1, CTX)]
                for k, stream in start + [(2, LAT), (2, CTX)]:
                    tile(k, stream)
                job_sum(t, first)
                tile(3, LAT)
                tile(3, CTX)
                for s in range(2):
                    pe.wait_ge(act_lo_done, ft + (s + 1))
                    down(u.plus(4 + s), s, first and s == 0, stop and s == 1)
                job_sum(t + 1)

            pe.wait_ge(mod_ready, AHEAD)
            for i, end in turns_of(0):
                if end is None:
                    both_turn(Unit(6 * i), 4 * i, 2 * i, i, i == 0, i == FH - 1)
                else:
                    with pe.Fori(i, end) as j:
                        both_turn(Unit(0, j), j * 4, j * 2, j)

            def context_down(u, ft, s, first=False, stop=False):
                pe.wait_ge(act_lo_done, ft + (FT + 1))
                down(u, s, first, stop, first)

            for ft in range(FT):
                context_down(Unit(U_CD + ft), ft, ft % 2, ft == 0, ft == FT - 1)
                if ft == 0:
                    mean_of(2)
                    batch_columns(0)
                if ft == BESIDE[3]["mean"]:
                    mean_of(3)

            def keep_warm(n):
                for _ in range(n):
                    nc.tensor.matmul(gu[:, 1, 0:P], mean_mat[:, :], mean_mat[:, :], start=True, stop=True)

            lat = (h_hi[LAT], h_lo[LAT])
            pe.wait_ge(h_ready, 4 * 3)
            pe.wait_ge(act_mul, 2 * FT)
            for idx in range(16):
                if idx >= 2:
                    pe.wait_ge(proj_out, idx - 1)
                column_unit(Unit(U_AB + idx), region(idx), lat)
                if idx == 0:
                    mean_of(4)
                if idx == BESIDE[5]["mean"]:
                    mean_of(5)
            con = (h_hi[CTX], h_lo[CTX])
            pe.wait_ge(h_ready, 4 * 4)
            for idx in range(16, 20):
                pe.wait_ge(proj_out, idx - 1)
                column_unit(Unit(U_AB + idx), gu[:, idx % 2, 0:T], lat, last=False)
                column_unit(Unit(U_AB + idx), gu[:, idx % 2, T:2 * T], con)
            def score(h):
                rows = slice(DH * (h % 2), DH * (h % 2) + DH)
                pe.wait_ge(masked, h + 1)
                for t in range(2):
                    i = 2 * h + t
                    if h >= 2:
                        pe.wait_ge(p_exp, i - 3)
                    nc.tensor.matmul(scores(i), q_t[rows, h // 2, t * P:(t + 1) * P], k_t[rows, h // 2, :],
                                     start=True, stop=False, skip_group_check=True)
                    nc.tensor.matmul(scores(i)[:, 0:T], turn[:, :], bias[:, h % 4, t, :], start=False, stop=True,
                                     skip_group_check=True).then_inc(s_done, 1)

            pe.wait_ge(proj_out, 20)
            pe.wait_ge(mod_ready, AHEAD + 1)
            score(0)
            score(1)

            pe.wait_ge(z_done, 4 * 5)
            for c in range(4):
                u = Unit(U_AB + 20 + c)
                s = u.base % RING
                pe.wait_ge(lo_done, u.base + 1)
                for half in range(2):
                    kt = 2 * c + half
                    w_hi, w_lo = (w[:, s, half * 512:half * 512 + 512] for w in (whi, wlo))
                    for t in range(4):
                        st = t // 2
                        tok = slice((t % 2) * P, (t % 2) * P + P)
                        x_hi, x_lo = h_hi[st][:, kt, tok], h_lo[st][:, kt, tok]
                        nc.tensor.matmul(acc[:, t, :], x_hi, w_hi, start=(kt == 0), stop=False, skip_group_check=True)
                        nc.tensor.matmul(acc[:, t, :], x_lo, w_hi, start=False, stop=False, skip_group_check=True)
                        ins = nc.tensor.matmul(acc[:, t, :], x_hi, w_lo, start=False, stop=(kt == KT - 1),
                                               skip_group_check=True)
                ins.then_inc(pe_done, 1)

            pe.wait_ge(proj_out, 22)

            def values(h):
                if h == 0:
                    pe.wait_ge(proj_out, 24)
                pe.wait_ge(pt_out, 2 * h + 2)
                pair = h // 2
                if h % 2 == 0 and pair >= 2:
                    pe.wait_ge(m_ready, 4 + pair - 1)
                rows = slice(DH * (h % 2), DH * (h % 2) + DH)
                for k in range(4):
                    ins = nc.tensor.matmul(acc[rows, 2 + pair % 2, 0:T], v_n[:, k, h * DH:(h + 1) * DH],
                                           prob_t[h % 2][:, k, :], start=(k == 0), stop=(k == 3))
                ins.then_inc(pv_done, 1)

            for h in range(HEADS):
                for t in range(2):
                    i = 2 * h + t
                    pe.wait_ge(p_norm, i + 1)
                    if h:
                        pe.wait_ge(pt_out, i - 1)
                    for k in range(4):
                        ins = nc.tensor.transpose(acc[:, t, k * P:(k + 1) * P], prob[:, i % 4, k * P:(k + 1) * P], ident[:, :])
                    ins.then_inc(pt_done, 1)
                if h + 2 < HEADS:
                    score(h + 2)
                if h:
                    values(h - 1)
            values(HEADS - 1)

            def out_projection(u0, ready, kts):
                for m in range(KT):
                    u = Unit(u0 + m)
                    pe.wait_ge(lo_done, u.base + 1)
                    for i, kt in enumerate(kts):
                        if m == 0:
                            pe.wait_ge(m_ready, ready + i + 1)
                        ins = product(acc_tile(m), *wblock(u, kt), m_hi[:, kt, :], m_lo[:, kt, :], i == 0, i == KT - 1)
                    ins.then_inc(pe_done, 1)

            out_projection(U_ABO, 0, (4, 5, 6, 7, 0, 1, 2, 3))
            mean_of(6)
            keep_warm(WARM[0])
            mean_of(7)
            keep_warm(WARM[1])
            ffn(1, 4, 4 * (6 - LATE + 1))
            mean_of(8)
            batch_columns(1)
            pe.wait_ge(act_mul, 3 * FT)
            keep_warm(WARM[0])
            mean_of(9)
            keep_warm(WARM[1])

            E = slice(0, HY_EMB)
            H = slice(0, HY_FFN)

            def filter_layer(l):
                if l == 0:
                    pe.wait_ge(filt_in, 16 * 7)
                    w, x_ = fw[E, 0:64], zf[E, :]
                else:
                    pe.wait_ge(fa, l)
                    w, x_ = fw[H, 64 * l:64 * l + 64], hid[H, :]
                nc.tensor.matmul(mean_p[H, 0:T], w, x_, start=True, stop=True).then_inc(fp, 1)

            def filter_out(i):
                th, half = i % 2, i // 2
                if i == 0:
                    pe.wait_ge(fa, 3)
                    pe.wait_ge(mod_ready, AHEAD + 3)
                else:
                    pe.wait_ge(fd, FD_SUM[i - 1])
                for b, bank in enumerate((job_p, mean_p)):
                    ins = nc.tensor.matmul(bank[:, :], hid[H, th * P:(th + 1) * P],
                                           w4[H, b * D + half * 512:b * D + half * 512 + 512], start=True, stop=True)
                ins.then_inc(fp, 1)

            def spectrum(i):
                half, what, w = SPECTRUM[i]
                cols = slice(half * 512, half * 512 + 512)
                if i >= 3:
                    pe.wait_ge(fa, 3 + i - 2)
                for th in range(2):
                    if what == "nyquist":
                        out_, w_, x_ = spectrum_bank(i)[0:1, :], dft[:, 2 + th, 0:1], p_f
                    else:
                        base = 0 if what == "re" else 2
                        out_, w_, x_ = spectrum_bank(i), dft[:, base + th, w * P:(w + 1) * P], p_f if what == "re" else m_f
                    ins = nc.tensor.matmul(out_, w_, x_[:, th, cols], start=(th == 0), stop=(th == 1))
                ins.then_inc(fp, 1)

            ffn(2, 5, 4 * (8 - LATE + 1), peeled=at_steps([BATCH_AT] + FILTER_AT, [lambda: batch_columns(2)]
                                             + [lambda l=l: filter_layer(l) for l in range(3)]
                                             + [lambda i=i: filter_out(i) for i in range(4)]))
            pe.wait_ge(dft_landed, 16)
            pe.wait_ge(act_mul, 4 * FT)
            pe.wait_ge(fd, FD_SUM[3])
            mean_of(10)
            for i in range(5):
                spectrum(i)
            mean_of(11)
            for i in range(5, 10):
                spectrum(i)

            pe.wait_ge(h_ready, 4 * 7)
            pe.wait_ge(fa, 3 + 10)

            def transposes(g):
                pe.wait_ge(hy_step, HY_STEPS(8 * g + 7))
                if g:
                    pe.wait_ge(un_out, 2)
                for th, bank in ((0, job_p), (1, mean_p)):
                    for c in range(4):
                        ins = nc.tensor.transpose(bank[:, c * P:(c + 1) * P], u_t[:, 4 * g + c, th * P:(th + 1) * P], ident[:, :])
                ins.then_inc(tr_done, 1)

            def u_spectrum(g, b):
                if b == 0:
                    pe.wait_ge(un_out, 2 * g + 2)
                    if g:
                        pe.wait_ge(yf_step, 5)
                base = 0 if b < 2 else 2
                for th in range(2):
                    ins = nc.tensor.matmul(acc[:, b, :], dft[:, base + th, (b % 2) * P:(b % 2 + 1) * P],
                                           u_n[:, th, g * 512:g * 512 + 512], start=(th == 0), stop=(th == 1))
                if b % 2:
                    ins.then_inc(uf_done, 1)

            for idx in range(24):
                if idx >= 2:
                    pe.wait_ge(hy_step, HY_STEPS(idx - 2))
                column_unit(Unit(U_HY + idx), region(idx), lat)
                if idx in TR_AT:
                    transposes(TR_AT.index(idx))
                if idx in UF_AT:
                    u_spectrum(*UF_AT[idx])
            for c in range(KT):
                if c < 2:
                    pe.wait_ge(hy_step, HY_STEPS(22 + c))
                if c % 4 == 0:
                    pe.wait_ge(yf_step, 5 * (c // 4) + 5)
                if c >= 2:
                    pe.wait_ge(inv_step, 2 * (c - 2) + 1)
                for k in range(4):
                    ins = nc.tensor.matmul(region(c), y_f[:, k, c * P:(c + 1) * P], dft[:, 4 + k, :], start=(k == 0), stop=(k == 3))
                ins.then_inc(inv_done, 1)
            out_projection(U_HYO, 8, range(KT))
            mean_of(12)
            keep_warm(WARM[0])
            mean_of(13)
            keep_warm(WARM[1])
            ffn(3, 7, 4 * (12 - LATE + 1))
            mean_of(14)


class Unit:

    def __init__(self, base, i=None):
        self.base, self.i = base, i

    def plus(self, k):
        return Unit(self.base + k, self.i)


def at_unit(u, k):
    if isinstance(u, int):
        return u + k
    return u.base + k if u.i is None else u.i * 6 + (u.base + k)


WARM = [18, 18]
PI_F = float(np.float32(3.1415925))
FD_SIN = [7, 14, 21]
FD_SUM = [21 + 5, 21 + 9, 21 + 14, 21 + 18]
FP_DFT = 7
SPECTRUM = [(half, what, w) for half in range(2) for what in ("re", "sine") for w in range(2)] \
    + [(half, "nyquist", 0) for half in range(2)]
BATCH_AT = (5, 0)
FILTER_AT = [(8, 5), (9, 1), (9, 3), (9, 5), (10, 1), (10, 2), (10, 4)]


def at_steps(places, calls):
    table = {}
    for (turn_, k), call in zip(places, calls):
        table.setdefault(turn_, {})[k] = call
    return table


TR_AT = (9, 18)
UF_AT = {11: (0, 0), 12: (0, 1), 13: (0, 2), 14: (0, 3), 20: (1, 0), 21: (1, 1), 22: (1, 2), 23: (1, 3)}
YF_AT = {13: [(0, 0)], 14: [(0, 1)], 15: [(0, 2)], 16: [(0, 3)], 18: [(0, 4)],
         22: [(1, 0)], 23: [(1, 1)], 24: [(1, 2)], 25: [(1, 3)], 27: [(1, 4)]}


def hy_tile(idx):
    if idx < 16:
        return 8 + idx // 2 if idx % 2 == 0 else 16 + idx // 2
    return idx - 16


def HY_STEPS(idx):
    return 2 * (idx + 1) + (min(idx + 1, 16) // 2)



def columns(w):
    k, n = w.shape
    return w.reshape(k // P, P, n // P, P).transpose(2, 1, 0, 3).reshape(n // P, P, k)


def rows(w):
    return w.reshape(w.shape[0] // P, P, D)


def pack_ffn(g, u, d):
    g, u, d = columns(g), columns(u), rows(d)
    return np.stack([g[0::2], u[0::2], g[1::2], u[1::2], d[0::2], d[1::2]], 1).reshape(-1, P, UNIT)


def pack(x, c, ctx, c_ctx, w_mod, b_mod, norm_g, ffn_w_gate, ffn_w_up, ffn_w_down, ab_w_in, na_rpb, sc_conv_w,
         ab_w_out, hy_w_in, hy_short_w, hy_f_w1, hy_f_b1, hy_f_w2, hy_f_b2, hy_f_w3, hy_f_b3, hy_f_w4,
         hy_sin_freq, hy_bias, hy_w_out):
    ffns = [pack_ffn(ffn_w_gate[l, j], ffn_w_up[l, j], ffn_w_down[l, j]) for l, j in FFN_OF]
    ab = columns(ab_w_in[0])
    ab_lat = ab[0:4], np.stack([ab[16:20], ab[20:24], ab[12:16]], 1).reshape(-1, P, UNIT)
    v = ab_w_in[0][:, 1024:1536].reshape(4, 2, P, 512).transpose(0, 2, 1, 3).reshape(4, P, UNIT)
    hy = columns(hy_w_in[0])
    order = [hy_tile(i) for i in range(24)]
    wstream = np.concatenate([ffns[0], rows(ffn_w_down[0, 0]), *ab_lat, ab[4:8], v, columns(ab_w_out[0]), ffns[1],
                              ffns[2], hy[order], columns(hy_w_out[0]), ffns[3]])
    assert wstream.shape[0] == UNITS
    wmod = np.stack([w_mod[l][:, b * D + h * 512:b * D + h * 512 + 512].reshape(KT, P, 512).transpose(1, 0, 2)
                     for l, b, h in LOADS])
    cols = {LAT: c.reshape(KT, P).T, CTX: c_ctx.reshape(KT, P).T}
    cvec = np.stack([cols[LAT], cols[CTX]], 2)
    bmod = np.concatenate([b_mod[l, b * D + h * 512:b * D + h * 512 + 512].reshape(4, P).T for l, b, h, _ in PASSES], 1)
    small = np.concatenate([norm_g.reshape(12 * KT, P).T, sc_conv_w[0].reshape(12, P).T,
                            hy_short_w[0].reshape(72, P).T, hy_bias[0].reshape(8, P).T], 1)
    rpb = np.zeros((HEADS, 15, 127), np.float32)
    rpb[:, :, 48:79] = na_rpb[0]
    fcols = np.stack([hy_f_b1[0], hy_f_b2[0], hy_f_b3[0], hy_sin_freq[0]], 1)

    def stream(s):
        return s[0].T.reshape(KT, P, T).transpose(1, 0, 2)

    return {"wstream": wstream, "wmod": wmod, "cvec_in": cvec, "bmod": bmod, "small": small, "x_in": stream(x),
            "ctx_in": stream(ctx), "rpb": rpb, "fw1": hy_f_w1[0], "fw2": hy_f_w2[0], "fw3": hy_f_w3[0],
            "fw4": hy_f_w4[0], "fcols": fcols, **constants()}


def constants():
    f = np.float32
    c = np.arange(GRID_W)
    first = np.clip(c - KW // 2, 0, GRID_W - KW)
    inside = (c[None, :] >= first[:, None]) & (c[None, :] < first[:, None] + KW)
    mask = np.tile(np.where(inside, 0.0, NEG).astype(f)[::-1], (2, 1))
    t = np.linspace(0.0, 1.0, T, dtype=f)[:, None]
    w = (f(2.0 * math.pi) * np.arange(T, dtype=f)[:, None] / f(T)).astype(f)
    bands = np.linspace(1e-4, 15, 16, dtype=f)[None, :]
    bw = (bands * w).astype(f)
    z = np.concatenate([t, np.cos(bw), -np.sin(bw)], 1).astype(f)
    deltas = np.linspace(math.log(1e-2) / 1.5, math.log(1e-2) / 0.3, D, dtype=f)
    window = np.exp(-t * np.abs(deltas)[None, :]).astype(f).reshape(2, P, D).transpose(1, 0, 2)
    n = np.arange(T)
    angle = 2 * np.pi * np.outer(n, n) / (2 * T)
    cos, sin = np.cos(angle), np.sin(angle)
    nyquist = np.where(n % 2, -1.0, 1.0)
    fwd_sin = sin.copy()
    fwd_sin[:, 0] = nyquist
    inv_cos, inv_sin = 2 * cos / (2 * T), 2 * sin / (2 * T)
    inv_cos[0] = 1 / (2 * T)
    inv_sin[0] = nyquist / (2 * T)
    dft = np.stack([cos, fwd_sin, inv_cos, inv_sin]).astype(f).reshape(8, P, T).transpose(1, 0, 2)
    turn = np.kron(np.eye(2, dtype=f), np.eye(GRID_W, dtype=f)[::-1])
    return {"mask_in": mask, "ident_in": np.eye(P, dtype=f), "turn_in": turn, "zfeat": z.T, "window_in": window, "dft_in": dft}


_ORDER = ["wstream", "wmod", "cvec_in", "bmod", "small", "x_in", "ctx_in", "rpb", "mask_in", "ident_in", "turn_in", "zfeat",
          "fw1", "fw2", "fw3", "fw4", "fcols", "window_in", "dft_in"]


def kernel(**inputs):
    import numpy as _np
    import concourse.bacc as _bacc
    from concourse import mybir as _mybir
    from concourse.bass_utils import run_bass_kernel_spmd as _run

    packed = pack(**{k: _np.asarray(a) for k, a in inputs.items()})
    nc = _bacc.Bacc("TRN2", target_bir_lowering=False, num_devices=1)
    arrays, args = {}, []
    for name in _ORDER:
        a = _np.ascontiguousarray(packed[name])
        arrays[f"in_{name}_dram"] = a
        args.append(nc.dram_tensor(f"in_{name}_dram", a.shape, _mybir.dt.from_np(a.dtype), kind="ExternalInput").ap())
    args.append(nc.dram_tensor("out_0_dram", (P, KT, T), _mybir.dt.float32, kind="ExternalOutput").ap())
    program(nc, *args)
    r = _run(nc, [arrays], core_ids=[0])
    got = r.results[0]["out_0_dram"]
    return got.transpose(1, 0, 2).reshape(D, T).T.reshape(1, T, D)
```
